# Optimizing a Trainium2 kernel written in Bass

```python
import math
import jax
import jax.numpy as jnp
from jax import lax
import numpy as np

D_MODEL = 1024
BATCH = 1
SEQ = 512
DEPTH = 2

N_META = 16
BLOCK = 128
N_FRONT = BLOCK - N_META
ROPE_THETA = 500000.0
ROT_FRAC_DIV = 4
EPS = 1e-6
NEG_INF = -1e30
D_FF = 2816

DIFF_HEADS = 4
DIFF_HEAD_DIM = 64
DIFF_V_DIM = 2 * DIFF_HEAD_DIM
DIFF_EPS = 1e-5
MLA_HEADS = 4
MLA_NOPE = 128
MLA_ROPE = 64
MLA_V = 128
MLA_Q_RANK = 256
MLA_KV_RANK = 256
SWA_HEADS = 16
SWA_KV_HEADS = 2
SWA_GROUP = SWA_HEADS // SWA_KV_HEADS
SWA_HEAD_DIM = 64
WINDOW = 128

N_EVEN = (DEPTH + 1) // 2
N_ODD = DEPTH // 2

DIFF_QK_COLS = DIFF_HEADS * 2 * DIFF_HEAD_DIM
DIFF_V_COLS = DIFF_HEADS * DIFF_V_DIM
AB_SPLITS = (DIFF_QK_COLS,
             2 * DIFF_QK_COLS,
             2 * DIFF_QK_COLS + DIFF_V_COLS,
             2 * DIFF_QK_COLS + DIFF_V_COLS + MLA_Q_RANK,
             2 * DIFF_QK_COLS + DIFF_V_COLS + MLA_Q_RANK + MLA_KV_RANK)
AB_IN_COLS = AB_SPLITS[-1] + MLA_ROPE
AB_OUT_COLS = DIFF_V_COLS + MLA_HEADS * MLA_V
SWA_Q_COLS = SWA_HEADS * SWA_HEAD_DIM
SWA_KV_COLS = SWA_KV_HEADS * SWA_HEAD_DIM
SWA_IN_COLS = SWA_Q_COLS + 2 * SWA_KV_COLS

kernel_name = "hybrid_diffattn_mla_swa_macaron"

def rms_norm(x, g, eps=EPS):
    xf = x.astype(jnp.float32)
    y = xf * lax.rsqrt(jnp.mean(xf * xf, axis=-1, keepdims=True) + eps)
    return (y * g.astype(jnp.float32)).astype(x.dtype)

def rope_tables(pos, rot_dim):
    inv = ROPE_THETA ** (-jnp.arange(0, rot_dim, 2, dtype=jnp.float32) / rot_dim)
    ang = pos.astype(jnp.float32)[:, None] * inv[None, :]
    return jnp.cos(ang), jnp.sin(ang)

def apply_rope(x, cos, sin):
    half = x.shape[-1] // 2
    x1 = x[..., :half].astype(jnp.float32)
    x2 = x[..., half:].astype(jnp.float32)
    return jnp.concatenate([x1 * cos - x2 * sin, x2 * cos + x1 * sin], axis=-1).astype(x.dtype)

def partial_rope(x, cos, sin):
    r = x.shape[-1] // ROT_FRAC_DIV
    return jnp.concatenate([apply_rope(x[..., :r], cos, sin), x[..., r:]], axis=-1)

def swiglu(x, w_gate, w_up, w_down):
    return (jax.nn.silu(x @ w_gate) * (x @ w_up)) @ w_down

def to_blocks(a):
    b, l = a.shape[:2]
    return jnp.moveaxis(a.reshape((b, l // BLOCK, BLOCK) + a.shape[2:]), 1, 0)

def from_blocks(a):
    a = jnp.moveaxis(a, 0, 1)
    return a.reshape((a.shape[0], a.shape[1] * a.shape[2]) + a.shape[3:])

def causal_mask(q_idx, k_idx, k_valid):
    return (k_idx[None, :] <= q_idx[:, None]) & k_valid[None, :]

def diff_attention(q, k, v, lam, k_valid):
    L = q.shape[1]
    idx = jnp.arange(L)
    scale = DIFF_HEAD_DIM ** -0.5

    def block(args):
        qb, qi = args
        s = jnp.einsum('bqhcd,bkhcd->bhcqk', qb, k).astype(jnp.float32) * scale
        m = causal_mask(qi, idx, k_valid)
        p = jax.nn.softmax(jnp.where(m, s, NEG_INF), axis=-1)
        w = p[:, :, 0] - lam * p[:, :, 1]
        return jnp.einsum('bhqk,bkhe->bqhe', w.astype(v.dtype), v)

    return from_blocks(lax.map(block, (to_blocks(q), idx.reshape(-1, BLOCK))))

def mla_attention(qn, qr, kn, kr, v, k_valid):
    L = qn.shape[1]
    idx = jnp.arange(L)
    scale = (MLA_NOPE + MLA_ROPE) ** -0.5

    def block(args):
        qnb, qrb, qi = args
        s = (jnp.einsum('bqhd,bkhd->bhqk', qnb, kn)
             + jnp.einsum('bqhr,bkr->bhqk', qrb, kr)).astype(jnp.float32) * scale
        m = causal_mask(qi, idx, k_valid)
        p = jax.nn.softmax(jnp.where(m, s, NEG_INF), axis=-1)
        return jnp.einsum('bhqk,bkhe->bqhe', p.astype(v.dtype), v)

    return from_blocks(lax.map(block, (to_blocks(qn), to_blocks(qr), idx.reshape(-1, BLOCK))))

def swa_sink_attention(q, k, v, sinks, k_valid):
    L = q.shape[1]
    scale = SWA_HEAD_DIM ** -0.5
    kp = jnp.pad(k, ((0, 0), (BLOCK, 0), (0, 0), (0, 0)))
    vp = jnp.pad(v, ((0, 0), (BLOCK, 0), (0, 0), (0, 0)))
    validp = jnp.pad(k_valid, (BLOCK, 0))
    meta_k = k[:, N_FRONT:BLOCK]
    meta_v = v[:, N_FRONT:BLOCK]
    sink = sinks.reshape(SWA_KV_HEADS, SWA_GROUP)[None, :, :, None, None].astype(jnp.float32)
    band_off = jnp.arange(2 * BLOCK)
    q_off = jnp.arange(BLOCK)

    def block(args):
        qb, n = args
        start = n * BLOCK
        kb = lax.dynamic_slice_in_dim(kp, start, 2 * BLOCK, axis=1)
        vb = lax.dynamic_slice_in_dim(vp, start, 2 * BLOCK, axis=1)
        kvalid = lax.dynamic_slice_in_dim(validp, start, 2 * BLOCK, axis=0)
        q_idx = start + q_off
        k_idx = start - BLOCK + band_off
        keys = jnp.concatenate([meta_k, kb], axis=1)
        vals = jnp.concatenate([meta_v, vb], axis=1)
        s = jnp.einsum('bqhgd,bkhd->bhgqk', qb, keys).astype(jnp.float32) * scale
        dist = q_idx[:, None] - k_idx[None, :]
        is_meta = (k_idx >= N_FRONT) & (k_idx < BLOCK)
        band = kvalid[None, :] & (dist >= 0) & ((dist < WINDOW) | is_meta[None, :])
        extra = jnp.broadcast_to(n >= 2, (BLOCK, N_META))
        mask = jnp.concatenate([extra, band], axis=-1)
        s = jnp.where(mask, s, NEG_INF)
        m = jnp.maximum(jnp.max(s, axis=-1, keepdims=True), sink)
        e = jnp.exp(s - m)
        p = e / (jnp.sum(e, axis=-1, keepdims=True) + jnp.exp(sink - m))
        return jnp.einsum('bhgqk,bkhe->bqhge', p.astype(vals.dtype), vals)

    return from_blocks(lax.map(block, (to_blocks(q), jnp.arange(L // BLOCK))))

def ab_mixer(h, w_in, lq1, lk1, lq2, lk2, subln, q_norm, w_uq, kv_norm, w_ukv, w_out,
             lambda_init, cos_p, sin_p, cos_m, sin_m, k_valid):
    B, L, _ = h.shape
    proj = h @ w_in
    q_a, k_a, v_a, c_q, c_kv, k_r = jnp.split(proj, list(AB_SPLITS), axis=-1)
    q_a = partial_rope(q_a.reshape(B, L, DIFF_HEADS, 2, DIFF_HEAD_DIM), cos_p[:, None, None, :], sin_p[:, None, None, :])
    k_a = partial_rope(k_a.reshape(B, L, DIFF_HEADS, 2, DIFF_HEAD_DIM), cos_p[:, None, None, :], sin_p[:, None, None, :])
    v_a = v_a.reshape(B, L, DIFF_HEADS, DIFF_V_DIM)
    lam = (jnp.exp(jnp.sum(lq1.astype(jnp.float32) * lk1.astype(jnp.float32)))
           - jnp.exp(jnp.sum(lq2.astype(jnp.float32) * lk2.astype(jnp.float32))) + lambda_init)
    o_a = diff_attention(q_a, k_a, v_a, lam, k_valid)
    o_a = (rms_norm(o_a, subln, DIFF_EPS) * (1.0 - lambda_init)).reshape(B, L, DIFF_V_COLS)
    q_b = (rms_norm(c_q, q_norm) @ w_uq).reshape(B, L, MLA_HEADS, MLA_NOPE + MLA_ROPE)
    qn = q_b[..., :MLA_NOPE]
    qr = apply_rope(q_b[..., MLA_NOPE:], cos_m[:, None, :], sin_m[:, None, :])
    kv = (rms_norm(c_kv, kv_norm) @ w_ukv).reshape(B, L, MLA_HEADS, MLA_NOPE + MLA_V)
    kn = kv[..., :MLA_NOPE]
    v_b = kv[..., MLA_NOPE:]
    kr = apply_rope(k_r, cos_m, sin_m)
    o_b = mla_attention(qn, qr, kn, kr, v_b, k_valid).reshape(B, L, MLA_HEADS * MLA_V)
    return jnp.concatenate([o_a, o_b], axis=-1) @ w_out

def swa_mixer(h, w_qkv, b_qkv, sinks, w_out, b_out, cos_p, sin_p, k_valid):
    B, L, _ = h.shape
    proj = h @ w_qkv + b_qkv
    q, k, v = jnp.split(proj, [SWA_Q_COLS, SWA_Q_COLS + SWA_KV_COLS], axis=-1)
    q = partial_rope(q.reshape(B, L, SWA_HEADS, SWA_HEAD_DIM), cos_p[:, None, :], sin_p[:, None, :])
    k = partial_rope(k.reshape(B, L, SWA_KV_HEADS, SWA_HEAD_DIM), cos_p[:, None, :], sin_p[:, None, :])
    v = v.reshape(B, L, SWA_KV_HEADS, SWA_HEAD_DIM)
    q = q.reshape(B, L, SWA_KV_HEADS, SWA_GROUP, SWA_HEAD_DIM)
    o = swa_sink_attention(q, k, v, sinks, k_valid).reshape(B, L, SWA_Q_COLS)
    return o @ w_out + b_out

def setup_inputs(seed: int = 0) -> dict:
    key = jax.random.key(seed)
    ks = iter(jax.random.split(key, 40))

    def nrm(shape, scale):
        return jax.random.normal(next(ks), shape, jnp.float32) * scale

    def gain(shape):
        return 1.0 + nrm(shape, 0.02)

    D, F = D_MODEL, D_FF
    return {
        "x": nrm((BATCH, SEQ, D), 1.0),
        "meta_tokens": nrm((N_META, D), 1.0),
        "ffn1_norm": gain((DEPTH, D)),
        "ffn1_w_gate": nrm((DEPTH, D, F), D ** -0.5),
        "ffn1_w_up": nrm((DEPTH, D, F), D ** -0.5),
        "ffn1_w_down": nrm((DEPTH, F, D), F ** -0.5),
        "mix_norm": gain((DEPTH, D)),
        "ab_w_in": nrm((N_EVEN, D, AB_IN_COLS), D ** -0.5),
        "diff_lambda_q1": nrm((N_EVEN, DIFF_HEAD_DIM), 0.1),
        "diff_lambda_k1": nrm((N_EVEN, DIFF_HEAD_DIM), 0.1),
        "diff_lambda_q2": nrm((N_EVEN, DIFF_HEAD_DIM), 0.1),
        "diff_lambda_k2": nrm((N_EVEN, DIFF_HEAD_DIM), 0.1),
        "diff_subln": gain((N_EVEN, DIFF_V_DIM)),
        "mla_q_norm": gain((N_EVEN, MLA_Q_RANK)),
        "mla_w_uq": nrm((N_EVEN, MLA_Q_RANK, MLA_HEADS * (MLA_NOPE + MLA_ROPE)), MLA_Q_RANK ** -0.5),
        "mla_kv_norm": gain((N_EVEN, MLA_KV_RANK)),
        "mla_w_ukv": nrm((N_EVEN, MLA_KV_RANK, MLA_HEADS * (MLA_NOPE + MLA_V)), MLA_KV_RANK ** -0.5),
        "ab_w_out": nrm((N_EVEN, AB_OUT_COLS, D), AB_OUT_COLS ** -0.5),
        "swa_w_qkv": nrm((N_ODD, D, SWA_IN_COLS), D ** -0.5),
        "swa_b_qkv": nrm((N_ODD, SWA_IN_COLS), 0.02),
        "swa_sinks": nrm((N_ODD, SWA_HEADS), 0.5),
        "swa_w_out": nrm((N_ODD, SWA_Q_COLS, D), SWA_Q_COLS ** -0.5),
        "swa_b_out": nrm((N_ODD, D), 0.02),
        "ffn2_norm": gain((DEPTH, D)),
        "ffn2_w_gate": nrm((DEPTH, D, F), D ** -0.5),
        "ffn2_w_up": nrm((DEPTH, D, F), D ** -0.5),
        "ffn2_w_down": nrm((DEPTH, F, D), F ** -0.5),
        "final_norm": gain((D,)),
    }

def reference(x, meta_tokens, ffn1_norm, ffn1_w_gate, ffn1_w_up, ffn1_w_down, mix_norm,
              ab_w_in, diff_lambda_q1, diff_lambda_k1, diff_lambda_q2, diff_lambda_k2, diff_subln,
              mla_q_norm, mla_w_uq, mla_kv_norm, mla_w_ukv, ab_w_out,
              swa_w_qkv, swa_b_qkv, swa_sinks, swa_w_out, swa_b_out,
              ffn2_norm, ffn2_w_gate, ffn2_w_up, ffn2_w_down, final_norm):
    B = x.shape[0]
    meta = jnp.broadcast_to(meta_tokens[None].astype(x.dtype), (B, N_META, D_MODEL))
    h = jnp.concatenate([jnp.zeros((B, N_FRONT, D_MODEL), x.dtype), meta, x], axis=1)
    L = h.shape[1]
    idx = jnp.arange(L)
    k_valid = idx >= N_FRONT
    pos = jnp.maximum(idx - N_FRONT, 0)
    cos_p, sin_p = rope_tables(pos, DIFF_HEAD_DIM // ROT_FRAC_DIV)
    cos_m, sin_m = rope_tables(pos, MLA_ROPE)
    for l in range(DEPTH):
        h = h + 0.5 * swiglu(rms_norm(h, ffn1_norm[l]), ffn1_w_gate[l], ffn1_w_up[l], ffn1_w_down[l])
        hn = rms_norm(h, mix_norm[l])
        if l % 2 == 0:
            e = l // 2
            lambda_init = 0.8 - 0.6 * math.exp(-0.3 * l)
            h = h + ab_mixer(hn, ab_w_in[e], diff_lambda_q1[e], diff_lambda_k1[e], diff_lambda_q2[e],
                             diff_lambda_k2[e], diff_subln[e], mla_q_norm[e], mla_w_uq[e],
                             mla_kv_norm[e], mla_w_ukv[e], ab_w_out[e], lambda_init,
                             cos_p, sin_p, cos_m, sin_m, k_valid)
        else:
            o = l // 2
            h = h + swa_mixer(hn, swa_w_qkv[o], swa_b_qkv[o], swa_sinks[o], swa_w_out[o], swa_b_out[o],
                              cos_p, sin_p, k_valid)
        h = h + 0.5 * swiglu(rms_norm(h, ffn2_norm[l]), ffn2_w_gate[l], ffn2_w_up[l], ffn2_w_down[l])
    h = rms_norm(h, final_norm)
    return h[:, BLOCK:]


_drawn_inputs = setup_inputs


def setup_inputs(seed=0):
    import zlib

    import numpy as np

    out = dict(_drawn_inputs(seed))
    spreads = {}
    factors = {'ffn1_norm': 4.286,
     'mix_norm': 2.82,
     'diff_lambda_k1': 8.0,
     'diff_lambda_q2': 8.0,
     'diff_subln': 26.82,
     'mla_q_norm': 8.0,
     'mla_kv_norm': 8.0,
     'swa_b_qkv': 16.314,
     'swa_sinks': 64.0,
     'swa_b_out': 28.616,
     'ffn2_norm': 5.901,
     'final_norm': 9.779}
    for name, (base, spread) in spreads.items():
        noise = np.random.default_rng([zlib.crc32(name.encode()), seed]).standard_normal(out[name].shape)
        drawn = base * np.exp(spread * noise) if base else spread * noise
        out[name] = jnp.asarray(drawn.astype(out[name].dtype))
    for name, factor in factors.items():
        out[name] = (out[name] * factor).astype(out[name].dtype)
    return out
```

```python
from contextlib import ExitStack

import numpy as np

import concourse.bass as bass
from concourse import mybir

F32 = mybir.dt.float32
F32R = mybir.dt.float32r
BF16 = mybir.dt.bfloat16
ACT = mybir.ActivationFunctionType
ALU = mybir.AluOpType
AX = mybir.AxisListType

P = 128
D = 1024
KD = D // P
META = 16
SEQ = 512
T = META + SEQ
HALF_T = T // 2
F = 2816
FH = F // P // 2
EPS = 1e-6
DIFF_EPS = 1e-5
LAMBDA_INIT = 0.8 - 0.6 * 1.0
DH, DV = 4, 128
MH = 4
SH, SD = 16, 64
KT_MAX = FH
TILE_START = [0] + [META + P * i for i in range(4)]
MASKED = -1e30

NORMS = 7
C_QN, C_KVN, C_SUBLN = NORMS * KD, NORMS * KD + 2, NORMS * KD + 4
C_BQKV = C_SUBLN + 1
C_BOUT = C_BQKV + 10
N_PARAMS = C_BOUT + KD
N_ROW = 4 * 64 + SH


class Span:

    def __init__(self, first):
        self.first, self.n = first, T - first
        if first == 0:
            self.width, self.chunks = HALF_T, [(0, 0), (1, HALF_T)]
            self.stat_starts = [c * HALF_T + s for c in range(2) for s in (0, P, HALF_T - P)]
        else:
            self.width, self.chunks = SEQ, [(0, first)]
            self.stat_starts = [first + P * s for s in range(SEQ // P)]

    def ps(self, pair):
        return pair[:, 0:len(self.chunks), 0:self.width]

    def sb(self, row):
        return row[:, self.first:T].rearrange("p (c n) -> p c n", c=len(self.chunks))

    def ps_at(self, pair, token, n):
        bank = (token - self.first) // self.width
        col = (token - self.first) % self.width
        return pair[:, bank, col:col + n]


ALL = Span(0)
OUT = Span(META)


class Tile:

    def __init__(self, kind, dst, index=0, k=KD, src="x", bias=None):
        self.kind, self.dst, self.index = kind, dst, index
        self.k, self.src, self.bias = k, src, bias
        self.jobs = []
        self.beats = None


class Item:

    def __init__(self, kind, i, hd, g, p):
        self.kind, self.i, self.hd, self.g, self.p = kind, i, hd, g, p
        self.scale = (192 if kind == "mla" else 64) ** -0.5
        if kind == "swa":
            self.blocks = [(kv, 3 * kv + b, b * P, kt) for kv in range(2)
                           for b, kt in ((0, i - 1), (1, i), (2, 0)) if b or i > 1]
            per = len(self.blocks) // 2
        else:
            self.blocks = [(0, j, TILE_START[j], j) for j in range(i + 1)]
            per = 4
        self.turns = [self.blocks[j:j + per] for j in range(0, len(self.blocks), per)]
        self.width = META + P * i if i else P
        self.chunks = ([(0, 0, self.width)] if self.width <= 512 else
                       [(c, c * HALF_T, HALF_T) for c in range(2)])


def ab_units():
    units = [[Tile("low_rank", "craw", i)] for i in range(4)]
    units += [[Tile("rope_m", "kr")]]
    uq = [Tile("plain", "mqn", i, 2, "cq") for i in range(4)]
    uq += [Tile("rope_m", "mqr", i, 2, "cq") for i in range(2)]
    ukv = [Tile("plain", "mkn", i, 2, "ckv") for i in range(4)]
    ukv += [Tile("value", "mv", i, 2, "ckv") for i in range(4)]
    units += [uq[0:3], uq[3:6], ukv[0:4], ukv[4:8]]
    for i in range(4):
        units += [[Tile("rope_p", "dq", i)], [Tile("rope_p", "dk", i)], [Tile("value", "dv", i)]]
    for n, unit in enumerate(units[9:]):
        unit[0].beats = [(), (True, True)] if n == 0 else [(4,), (True, True)] if n < 9 else [(), (True, True)]
    return units


def swa_units():
    units = [[Tile("rope_p", "sk", bias=0)], [Tile("value", "sv", bias=1)]]
    units += [[Tile("rope_p", "sq", i, bias=2 + i)] for i in range(8)]
    for n, unit in enumerate(units[2:]):
        unit[0].beats = [(), (False, False)] if n == 0 else [(2, 5), (True, True)]
    return units


def attention_items(which):
    items = []
    if which == "ab":
        for kind, g0 in (("mla", 0), ("diff", 5)):
            items += [Item(kind, i, hd, g0 + hd, i - 1) for hd in range(4) for i in range(1, 5)]
            items += [Item(kind, 0, hd, g0 + 4, hd) for hd in range(4)]
    else:
        items += [Item("swa", i, j, 10 + j, i - 1) for j in range(8) for i in range(1, 5)]
    return items


def outputs_at(at, m):
    if at(m - 3) and at(m - 3).last and at(m - 3).kind != "diff":
        return at(m - 3)
    if at(m - 4) and at(m - 4).last and at(m - 4).kind == "diff":
        return at(m - 4)
    return None


def plan():
    unit_k, unit_last, stages = [], [], []
    at = dict(o=0, a=0, r=0, sq=KD, norm=0, rope=0, bias=0, low=0)
    att = dict(n=0, x=0, t=0, mix=0, g=0)

    def units(kind, ks, tiles_each, **more):
        st = dict(kind=kind, u0=len(unit_k), o0=at["o"], **more)
        for k, n in zip(ks, tiles_each):
            at["o"] += n
            unit_k.append(k)
            unit_last.append(at["o"] - 1)
        stages.append(st)
        return st

    def stats(span, sq):
        s = dict(span=span, a=at["a"], r=at["r"], sq=sq)
        at["a"] += 2
        at["r"] += 1
        return s

    def splits_h(st):
        at["norm"] += 1
        st.update(last=True, norm=at["norm"], sq0=at["sq"])
        at["sq"] += KD

    def ffn(n, span):
        for half in range(2):
            first = half == 0
            units("gu", [KD] * 2 * FH, [1] * 2 * FH, w0=(2 * n + half) * 2 * FH, f0=(2 * n + half) * FH,
                  norm=at["norm"], span=span, stats=stats(span, at["sq"]) if first else None)
            st = units("dn", [FH] * KD, [1] * KD, k=FH, span=span, scale=0.5, weights="dn",
                       w0=(2 * n + half) * KD, act_lo=(2 * n + half + 1) * FH, last=False)
        splits_h(st)

    def projections(which, its_units):
        st = units("proj", [sum(t.k for t in ts) for ts in its_units], [len(ts) for ts in its_units],
                   which=which, units=its_units, norm=at["norm"], stats=stats(ALL, at["sq"]))
        flat = [t for ts in its_units for t in ts]
        for n, t in enumerate(flat):
            t.o = st["o0"] + n
            if t.bias is not None:
                at["bias"] += 1
                t.biased = at["bias"]
        for n, t in enumerate(flat):
            before = flat[n - 1] if n else None
            if before and before.kind == "low_rank" and before.index % 2:
                t.jobs.append(("spread", at["a"], at["r"]))
                at["a"] += 1
                at["r"] += 1
            if t.kind == "low_rank":
                at["sq"] += 1
                at["low"] += 1
                t.sq, t.low = at["sq"], at["low"]
                if t.index % 2:
                    t.jobs.append(("columns", at["a"], at["sq"]))
                    at["a"] += 1
            elif t.kind in ("rope_p", "rope_m"):
                at["rope"] += 1
                t.rope = at["rope"]
                t.jobs.append(("rotate", at["a"], t))
                at["a"] += 1
            elif t.kind == "value":
                t.jobs.append(("turn", at["a"], t))
                at["a"] += 1
        tiles = {(t.dst, t.index): t for t in flat}
        items = attention_items(which)
        in_pair = [None, None]
        for m, it in enumerate(items):
            it.m, it.n = m, att["n"]
            att["n"] += 1
            pairs = (0, 1) if it.kind == "diff" else (m % 2,)
            it.sets = []
            for pair in pairs:
                it.sets.append((att["x"], pair, in_pair[pair]))
                in_pair[pair] = att["x"]
                att["x"] += 1
            it.t0 = att["t"]
            att["t"] += len(it.turns)
            it.t_end = att["t"]
            if it.kind == "diff":
                att["mix"] += 1
                it.mix = att["mix"]
            it.last = m + 1 == len(items) or items[m + 1].g != it.g
            it.after = None
            if it.kind == "mla" and m == 0:
                it.after = tiles["mv", 3], tiles["mqr", 1], tiles["mv", 3]
            elif it.kind == "diff" and it.i == 1:
                it.after = None, tiles["dk", it.hd], tiles["dv", it.hd]
            elif it.kind == "swa" and it.i == 1:
                it.after = None, tiles["sq", it.hd], tiles["sv", 0]
            it.before = [items[m - k] if m >= k else None for k in range(5)]
        att["g"] = items[-1].g + 1
        st.update(flat=flat, items=items, a_end=at["a"], groups=att["g"])

    def out_projection(weights, span, bias):
        st = units("dn", [KD] * KD, [1] * KD, k=KD, span=span, scale=1.0, bias=bias,
                   weights=weights, w0=0, act_lo=None, o_lo=att["g"])
        splits_h(st)

    ffn(0, ALL)
    projections("ab", ab_units())
    out_projection("abo", ALL, False)
    ffn(1, ALL)
    ffn(2, ALL)
    projections("swa", swa_units())
    out_projection("swo", OUT, True)
    ffn(3, OUT)
    stages.append(dict(kind="final", stats=stats(OUT, at["sq"])))
    return stages, unit_k, unit_last


def build(nc, x_t, w_gu, w_dn, w_ab, w_uq, w_ukv, w_abo, w_swa, w_swo, params, row, consts,
          tables, masks, out):
    stages, unit_k, unit_last = plan()
    ab, swa = (st for st in stages if st["kind"] == "proj")
    stats_of_ab = ab["stats"]["r"]
    ctx = ExitStack()
    with ctx:
        cursor = [(nc.sbuf_base + 31) // 32 * 32]

        def place(name, shape, dt, at=None):
            n = int(np.prod(shape[1:])) * (2 if dt == BF16 else 4)
            offset = cursor[0] if at is None else at
            if at is None:
                cursor[0] = (offset + n + 31) // 32 * 32
            return nc.alloc_sbuf_tensor_at(name, shape, dt, offset=offset)

        ROW = T * 4
        h = place("h", [P, KD, T], F32)
        at_xg = cursor[0]
        xg_hi = place("xg_hi", [P, KD, T], F32R)
        xg_lo = place("xg_lo", [P, KD, T], F32R)
        at_act = cursor[0]
        act_hi = place("act_hi", [P, FH, T], F32R)
        act_lo = place("act_lo", [P, FH, T], F32R)
        raw = place("raw", [P, 2, KT_MAX * P], F32)
        w_hi = place("w_hi", [P, 2, KT_MAX * P], F32R)
        w_lo = place("w_lo", [P, 2, KT_MAX * P], F32R)
        at_square = cursor[0]
        square = place("square", [P, T], F32)
        at_square_sum = cursor[0]
        square_sum = place("square_sum", [P, T], F32)
        rbc = place("rbc", [P, T], F32)
        con = place("con", [P, 3 * P + 2], F32)
        mask_bf = place("mask_bf", [P, 3 * P], BF16)
        par = place("par", [P, N_PARAMS], F32)
        rows = place("rows", [P, N_ROW], F32)
        mean_sq = place("mean_sq", [P, 8], F32)
        rstd = place("rstd", [P, 8], F32)
        lam = place("lam", [P, 8], F32)
        lam_prod = place("lam_prod", [P, 64], F32)
        gain_sub = place("gain_sub", [P, 1], F32)
        neg_max = place("neg_max", [P, 2, 8], F32)
        row_max = place("row_max", [P, 2, 8], F32)
        row_sum = place("row_sum", [P, 2, 8], F32)
        inv_sum = place("inv_sum", [P, 2, 8], F32)
        coef = place("coef", [P, 2], F32)
        sink_s = place("sink_s", [P, 8], F32)
        sink_e = place("sink_e", [P, 8], F32)
        neg_sink = place("neg_sink", [P, 16], F32)
        o_ms = place("o_ms", [P, 4], F32)
        o_mse = place("o_mse", [P, 4], F32)
        o_rstd = place("o_rstd", [P, 4], F32)

        ident, rot_p, rot_m = con[:, 0:P], con[:, P:2 * P], con[:, 2 * P:3 * P]
        one_col, minus_half = con[:, 3 * P:3 * P + 1], con[:, 3 * P + 1:3 * P + 2]
        ident_bf, window_bf = mask_bf[:, 0:P], mask_bf[:, P:3 * P]
        causal_bf = mask_bf[:, 2 * P:3 * P]

        tab = place("tab", [P, 4, T], F32)
        pt_ab = place("pt_ab", [P, 2, 5 * P], F32, cursor[0] - 2 * ROW)
        cursor[0] += 2 * 5 * P * 4 - 2 * ROW
        cos_p, sin_p, cos_m, sin_m = (tab[:, i, :] for i in range(4))

        at_att = cursor[0]
        g_buf = place("g_buf", [P, T], F32, at_att)
        u_buf = place("u_buf", [P, T], F32, at_att + ROW)
        s_buf = place("s_buf", [P, T], F32, at_att + 2 * ROW)
        p_buf = place("p_buf", [P, T], F32, at_att + 3 * ROW)
        final = place("final", [P, KD, T], F32, at_att + 4 * ROW)
        att = [place(f"att{i}", [P, T], F32, at_att + i * ROW) for i in range(19)]
        mqn, mqr, mkn = att[9:13], att[13:15], att[15:19]
        kr = [(att[3], att[8])]
        dq = att[0:3] + att[15:16]
        dk = [(att[i], att[i + 1]) for i in (4, 6, 9, 11)]
        dv = place("dv", [P, 5, 512], F32, at_att + 19 * ROW)
        mv = place("mv", [P, 5, 512], F32, at_att + 19 * ROW + 10240)
        sq = place("sq", [P, 8, T], F32, at_att)
        sq = [sq[:, i, :] for i in range(8)]
        sk = [place("sk", [P, T], F32, at_att + 8 * ROW)]
        sv = place("sv", [P, 5, P], F32, at_att + 9 * ROW)
        pt_swa = place("pt_swa", [P, 2, 6 * P], F32, at_att + 9 * ROW + 5 * P * 4)
        e_win = place("e_win", [P, 2, 2, 3 * P], F32, at_att + 9 * ROW + 17 * P * 4)
        sk_win = place("sk_win", [P, 2, 4, 2 * P + META], F32, at_att + 9 * ROW + 29 * P * 4)
        dest = {"dq": dq, "dk": dk, "kr": kr, "mqn": mqn, "mqr": mqr, "mkn": mkn, "dv": dv,
                "mv": mv, "sq": sq, "sk": sk, "sv": sv}
        craw = place("craw", [P, 4, T], F32, at_act + 4 * ROW)
        pre = place("pre", [P, T], F32, at_act + 8 * ROW)
        turned = place("turned", [P, T], F32, at_act + 9 * ROW)
        rbc_q = place("rbc_q", [P, T], F32, at_act + 10 * ROW)
        rbc_kv = place("rbc_kv", [P, T], F32, at_act + (FH + 8) * ROW)
        rbcs = {"x": rbc, "cq": rbc_q, "ckv": rbc_kv}
        dest["craw"] = [craw[:, i, :] for i in range(4)]
        e_buf = place("e_buf", [P, 1, T], F32, at_act + 10 * ROW), \
            place("e_buf1", [P, 1, T], F32, at_act + (FH + 8) * ROW)
        mix = place("mix", [P, 2, T], F32, at_act + (FH + 9) * ROW)
        o_sq = place("o_sq", [P, 512], F32, at_square)
        o_nat = place("o_nat", [P, 512], F32, at_square_sum)

        tiles_ps = [ctx.enter_context(nc.psum_tensor(f"tile{i}", [P, 2, 512], F32)) for i in range(2)]
        aux_ps = [ctx.enter_context(nc.psum_tensor(f"aux{i}", [P, 2, 512], F32)) for i in range(2)]

        scores_ps = [tiles_ps[1], aux_ps[0]]
        turn_ps, value_ps = aux_ps[1][:, 0, :], aux_ps[1][:, 1, :]

        def sem(name):
            return ctx.enter_context(nc.semaphore(name))

        consts_in, tables_in, h_in = sem("consts_in"), sem("tables_in"), sem("h_in")
        landed = [sem("landed0"), sem("landed1")]
        hi_ready = sem("hi_ready")
        lo_ready = sem("lo_ready")
        tile_full = sem("tile_full")
        tile_out = sem("tile_out")
        aux_full = sem("aux_full")
        aux_out = sem("aux_out")
        xg_hi_ready = sem("xg_hi_ready")
        xg_lo_ready = sem("xg_lo_ready")
        squared = sem("squared")
        sum_clear = sem("sum_clear")
        summed = sem("summed")
        rstd_ready = sem("rstd_ready")
        silu_ready = sem("silu_ready")
        gated = sem("gated")
        act_hi_ready = sem("act_hi_ready")
        act_lo_ready = sem("act_lo_ready")
        lam_ready = sem("lam_ready")
        lam_exp = sem("lam_exp")
        low_hi_ready = sem("low_hi_ready")
        low_lo_ready = sem("low_lo_ready")
        biased = sem("biased")
        rope_done = sem("rope_done")
        scores_full = sem("scores_full")
        max_ready = sem("max_ready")
        exp_done = sem("exp_done")
        mix_ready = sem("mix_ready")
        pt_full = sem("pt_full")
        pt_out = sem("pt_out")
        pv_done = sem("pv_done")
        sink_sum = sem("sink_sum")
        sink_exp = sem("sink_exp")
        o_mean = sem("o_mean")
        o_rstd_ready = sem("o_rstd_ready")
        o_taken = sem("o_taken")
        o_ready = sem("o_ready")
        o_turned = sem("o_turned")
        o_hi = sem("o_hi")
        o_lo = sem("o_lo")
        final_ready = sem("final_ready")
        stored = sem("stored")
        vec_step = sem("vec_step")

        def landed_count(u):
            return 16 * (u // 2 + 1)

        block = ctx.enter_context(nc.Block())

        @block.sync
        def _(sp):
            sp.dma_start(par[:, :], params).then_inc(consts_in, 16)
            for part in range(2):
                ks = slice(part * KD // 2, (part + 1) * KD // 2)
                sp.dma_start(h[:, ks, :], x_t[:, ks, :]).then_inc(h_in, 16)
            for u in range(2):
                sp.dma_start(raw[:, u, 0:KD * P], w_gu[u, :, :]).then_inc(landed[u], 16)
            sp.dma_start(con[:, :], consts).then_inc(consts_in, 16)
            sp.dma_start(mask_bf[:, :], masks).then_inc(consts_in, 16)
            sp.dma_start(rows[:, :], row.partition_broadcast(P)).then_inc(consts_in, 16)
            sp.dma_start(tab[:, :, :], tables).then_inc(tables_in, 16)
            sources = {"dn": w_dn, "abo": w_abo, "swo": w_swo}

            def load_pairs(src, w0, u0, k, first, last):
                with sp.Fori(first, last) as i:
                    for c in range(2):
                        sp.wait_ge(lo_ready, i * 2 + (u0 + c - 1))
                        sp.dma_start(raw[:, (u0 + c) % 2, 0:k * P],
                                     src[bass.ds(i * 2 + (w0 + c), 1), :, :].rearrange("a p n -> (a p) n")
                                     ).then_inc(landed[(u0 + c) % 2], 16)

            for st in stages:
                if st["kind"] == "gu":
                    load_pairs(w_gu, st["w0"], st["u0"], KD, 0 if st["u0"] else 1, FH)
                elif st["kind"] == "dn":
                    load_pairs(sources[st["weights"]], st["w0"], st["u0"], st["k"], 0, KD // 2)
                elif st["kind"] == "proj" and st["which"] == "swa":
                    load_pairs(w_swa, 0, st["u0"], KD, 0, 5)
                elif st["kind"] == "proj":
                    u0 = st["u0"]
                    load_pairs(w_ab, 0, u0, KD, 0, 2)
                    for n, src in ((4, w_ab[4, :, :]), (5, w_uq[0, :, :]), (6, w_uq[1, :, :]),
                                   (7, w_ukv[0, :, :]), (8, w_ukv[1, :, :])):
                        sp.wait_ge(lo_ready, u0 + n - 1)
                        sp.dma_start(raw[:, (u0 + n) % 2, 0:unit_k[u0 + n] * P], src
                                     ).then_inc(landed[(u0 + n) % 2], 16)
                    load_pairs(w_ab, 5, u0 + 9, KD, 0, 6)
            for d in range(KD):
                sp.wait_ge(final_ready, d + 1)
                sp.dma_start(out[:, d, :], final[:, d, META:T]).then_inc(stored, 16)
            sp.wait_ge(stored, 16 * KD)

        @block.tensor
        def _(pe):
            def product(pair, span, blk, slot, x_hi, x_lo, start, stop):
                wh = w_hi[:, slot, blk * P:(blk + 1) * P]
                wl = w_lo[:, slot, blk * P:(blk + 1) * P]
                for n, (w, x) in enumerate(((wh, x_hi), (wh, x_lo), (wl, x_hi))):
                    for bank, t0 in span.chunks:
                        mm = pe.matmul(pair[:, bank, 0:span.width], w, x[:, t0:t0 + span.width],
                                       start=start and n == 0, stop=stop and n == 2)
                return mm

            def stats_columns(a, span, sq_done):
                pe.wait_ge(summed, sq_done)
                if a >= 2:
                    pe.wait_ge(aux_out, a - 1)
                for j, t0 in enumerate(span.stat_starts):
                    mm = pe.matmul(aux_ps[a % 2][:, 0, j:j + 1], square_sum[:, t0:t0 + P], one_col,
                                   start=True, stop=True)
                mm.then_inc(aux_full, 1)

            def stats_spread(a, span, r):
                pe.wait_ge(rstd_ready, r + 1)
                if a >= 2:
                    pe.wait_ge(aux_out, a - 1)
                for j, t0 in enumerate(span.stat_starts):
                    mm = pe.matmul(span.ps_at(aux_ps[a % 2], t0, P),
                                   rstd[:, j:j + 1].to_broadcast([P, P]), ident, start=True, stop=True)
                mm.then_inc(aux_full, 1)

            pe.wait_ge(consts_in, 64)

            def gate_up(st):
                u0, o0, span, norm, s = st["u0"], st["o0"], st["span"], st["norm"], st["stats"]
                first = 0
                if s:
                    for c in range(2):
                        pe.wait_ge(lo_ready, u0 + c + 1)
                        if o0 + c >= 2:
                            pe.wait_ge(tile_out, o0 + c - 1)
                        for k in range(KD):
                            if c == 0:
                                pe.wait_ge(xg_lo_ready, KD * norm + k + 1)
                            mm = product(tiles_ps[(o0 + c) % 2], span, k, (u0 + c) % 2,
                                         xg_hi[:, k, :], xg_lo[:, k, :], k == 0, k == KD - 1)
                            if c == 1 and k == KD // 2:
                                stats_spread(s["a"] + 1, span, s["r"])
                        mm.then_inc(tile_full, 1)
                        if c == 0:
                            stats_columns(s["a"], span, s["sq"])
                    first = 1
                with pe.Fori(first, FH) as f:
                    for c in range(2):
                        pe.wait_ge(lo_ready, f * 2 + (u0 + c + 1))
                        pe.wait_ge(tile_out, f * 2 + (o0 + c - 1))
                        for k in range(KD):
                            mm = product(tiles_ps[(o0 + c) % 2], span, k, (u0 + c) % 2,
                                         xg_hi[:, k, :], xg_lo[:, k, :], k == 0, k == KD - 1)
                        mm.then_inc(tile_full, 1)

            def down(st):
                u0, o0, span, nk = st["u0"], st["o0"], st["span"], st["k"]
                if st["act_lo"]:
                    pe.wait_ge(act_lo_ready, st["act_lo"] - 1)
                else:
                    pe.wait_ge(o_lo, st["o_lo"])
                with pe.Fori(0, KD // 2) as i:
                    for c in range(2):
                        pe.wait_ge(lo_ready, i * 2 + (u0 + c + 1))
                        pe.wait_ge(tile_out, i * 2 + (o0 + c - 1))
                        for k in range(nk):
                            if k == nk - 1 and c == 0 and st["act_lo"]:
                                pe.wait_ge(act_lo_ready, st["act_lo"])
                            mm = product(tiles_ps[(o0 + c) % 2], span, k, (u0 + c) % 2,
                                         act_hi[:, k, :], act_lo[:, k, :], k == 0, k == nk - 1)
                        mm.then_inc(tile_full, 1)

            def auxiliary(jobs, pair=None):
                for what, a, of in jobs:
                    if what == "columns":
                        stats_columns(a, ALL, of)
                    elif what == "spread":
                        stats_spread(a, ALL, of)
                    else:
                        if of.bias is None:
                            pe.wait_ge(tile_out, of.o + 1)
                        else:
                            pe.wait_ge(biased, of.biased)
                        pe.wait_ge(aux_out, a - 1)
                        to = pair or aux_ps[a % 2]
                        if what == "rotate":
                            rot = rot_p if of.kind == "rope_p" else rot_m
                            for bank, t0 in ALL.chunks:
                                mm = pe.matmul(to[:, bank, 0:HALF_T], rot, pre[:, t0:t0 + HALF_T],
                                               start=True, stop=True)
                        else:
                            for j in range(1, 5):
                                pe.transpose(to[:, 0, (j - 1) * P:j * P],
                                             pre[:, TILE_START[j]:TILE_START[j] + P], ident)
                            mm = pe.transpose(to[:, 1, 0:P], pre[:, 0:P], ident)
                        mm.then_inc(aux_full, 1)

            def scores(it):
                q0 = TILE_START[it.i]
                if it.after:
                    plain, rope, value = it.after
                    if plain:
                        pe.wait_ge(tile_out, plain.o + 1)
                        pe.wait_ge(aux_out, plain.jobs[0][1] + 1)
                    pe.wait_ge(rope_done, rope.rope)
                    pe.wait_ge(aux_out, value.jobs[0][1] + 1)
                for c, (x, pair, before) in enumerate(it.sets):
                    slot = scores_ps[pair]
                    if before is not None:
                        pe.wait_ge(exp_done, before + 1)
                    if it.kind == "swa":
                        lo = 0 if it.i > 1 else P
                        for kv in range(2):
                            pe.matmul(slot[:, kv, lo:2 * P + META], sq[it.hd][:, q0:q0 + P],
                                      sk_win[:, kv, it.i - 1, lo:2 * P + META], start=True, stop=True)
                            mm = pe.matmul(slot[:, kv, lo:2 * P], ident_bf,
                                           window_bf if lo == 0 else causal_bf, start=False, stop=True,
                                           skip_group_check=True)
                    else:
                        for bank, k0, kn in it.chunks:
                            diagonal = k0 + kn == it.width
                            cols = slot[:, bank, 0:kn]
                            if it.kind == "diff":
                                mm = pe.matmul(cols, dq[it.hd][:, q0:q0 + P], dk[it.hd][c][:, k0:k0 + kn],
                                               start=True, stop=True)
                            else:
                                pe.matmul(cols, mqn[it.hd][:, q0:q0 + P], mkn[it.hd][:, k0:k0 + kn],
                                          start=True, stop=False)
                                mm = pe.matmul(cols, mqr[it.hd // 2][:, q0:q0 + P],
                                               kr[0][it.hd % 2][:, k0:k0 + kn], start=False, stop=True)
                            if diagonal:
                                mm = pe.matmul(slot[:, bank, kn - P:kn], ident_bf, causal_bf,
                                               start=False, stop=True, skip_group_check=True)
                    mm.then_inc(scores_full, 1)

            turn_free = []

            def turn_probabilities(it, part):
                if part == 0:
                    if it.kind == "diff":
                        pe.wait_ge(mix_ready, it.mix)
                    else:
                        pe.wait_ge(exp_done, it.sets[0][0] + 1)
                if turn_free:
                    pe.wait_ge(*turn_free.pop())
                for place_in_bank, (kv, _, col, _) in enumerate(it.turns[part]):
                    if it.kind == "swa":
                        src = e_win[:, it.m % 2, kv, col:col + P]
                    elif it.kind == "diff":
                        src = mix[:, it.m % 2, col:col + P]
                    else:
                        src = e_buf[it.m % 2][:, 0, col:col + P]
                    mm = pe.transpose(turn_ps[:, place_in_bank * P:(place_in_bank + 1) * P], src, ident)
                mm.then_inc(pt_full, 1)
                turn_free.append((pt_out, it.t0 + part + 1))

            def values(it):
                pe.wait_ge(pt_out, it.t_end)
                if it.p == 0 and it.g:
                    pe.wait_ge(o_taken, it.g)
                pt = (pt_swa if it.kind == "swa" else pt_ab)[:, it.m % 2, :]
                for kv in range(2 if it.kind == "swa" else 1):
                    blocks = [b for b in it.blocks if b[0] == kv]
                    for m, (_, pos, _, kt) in enumerate(blocks):
                        if it.kind == "swa":
                            to = value_ps[:, it.p * P + SD * kv:it.p * P + SD * (kv + 1)]
                            v = sv[:, kt, SD * kv:SD * (kv + 1)]
                        else:
                            to = value_ps[:, it.p * P:(it.p + 1) * P]
                            v = (dv if it.kind == "diff" else mv)[:, kt, it.hd * P:(it.hd + 1) * P]
                        mm = pe.matmul(to, pt[:, pos * P:(pos + 1) * P], v, start=m == 0,
                                       stop=m == len(blocks) - 1)
                mm.then_inc(pv_done, 1)

            def turn_output(it):
                if it.kind == "diff":
                    pe.wait_ge(o_ready, it.g - 4)
                else:
                    pe.wait_ge(o_taken, it.g + 1)
                pe.wait_ge(*turn_free.pop())
                for b in range(4):
                    mm = pe.transpose(turn_ps[:, b * P:(b + 1) * P], o_nat[:, b * P:(b + 1) * P], ident)
                mm.then_inc(o_turned, 1)
                turn_free.append((o_lo, it.g + 1))

            def beat(items, m):
                at = lambda k: items[k] if 0 <= k < len(items) else None
                output = outputs_at(at, m)
                if output:
                    turn_output(output)
                if at(m):
                    scores(at(m))
                if at(m - 1):
                    turn_probabilities(at(m - 1), 0)
                if at(m - 2):
                    values(at(m - 2))
                if at(m - 1) and len(at(m - 1).turns) > 1:
                    turn_probabilities(at(m - 1), 1)

            def projections(st):
                s, items = st["stats"], st["items"]
                n, m = 0, 0
                for at, its_tiles in enumerate(st["units"]):
                    u = st["u0"] + at
                    pe.wait_ge(lo_ready, u + 1)
                    blk = 0
                    for t in its_tiles:
                        if t.beats is None:
                            pe.wait_ge(tile_out, t.o - 1)
                            pair = tiles_ps[t.o % 2]
                        else:
                            pe.wait_ge(tile_out, t.o)
                            if n and st["flat"][n - 1].beats is not None:
                                pe.wait_ge(aux_out, st["flat"][n - 1].jobs[-1][1] + 1)
                            pair = tiles_ps[0]
                        if t.src == "x":
                            src_hi, src_lo, k0 = xg_hi, xg_lo, 0
                        else:
                            src_hi, src_lo, k0 = act_hi, act_lo, 0 if t.src == "cq" else 2
                            pe.wait_ge(low_lo_ready, k0 + 2)
                        for k in range(t.k):
                            if n == 0:
                                pe.wait_ge(xg_lo_ready, KD * st["norm"] + k + 1)
                            mm = product(pair, ALL, blk, u % 2, src_hi[:, k0 + k, :],
                                         src_lo[:, k0 + k, :], k == 0, k == t.k - 1)
                            blk += 1
                            if k == (t.k - 1) // 2:
                                if n == 1:
                                    stats_spread(s["a"] + 1, ALL, s["r"])
                                if n and st["flat"][n - 1].beats is None:
                                    auxiliary(st["flat"][n - 1].jobs)
                            if t.beats and k + 1 in t.beats[0]:
                                beat(items, m)
                                m += 1
                        mm.then_inc(tile_full, 1)
                        if n == 0:
                            stats_columns(s["a"], ALL, s["sq"])
                        if t.beats:
                            if t.beats[1][0]:
                                beat(items, m)
                                m += 1
                            auxiliary(t.jobs, tiles_ps[0])
                            if t.beats[1][1]:
                                beat(items, m)
                                m += 1
                        n += 1
                while m < len(items) + 4:
                    beat(items, m)
                    m += 1

            for st in stages:
                if st["kind"] == "gu":
                    gate_up(st)
                elif st["kind"] == "dn":
                    down(st)
                elif st["kind"] == "proj":
                    projections(st)
                else:
                    s = st["stats"]
                    stats_columns(s["a"], OUT, s["sq"])
                    stats_spread(s["a"] + 1, OUT, s["r"])

        @block.scalar
        def _(act):
            def split_hi(u, k, i=0):
                act.wait_ge(landed[u % 2], i * 16 + landed_count(u))
                if u >= 2:
                    act.wait_ge(tile_full, i * 2 + (unit_last[u - 2] + 1))
                act.activation(w_hi[:, u % 2, 0:k * P], raw[:, u % 2, 0:k * P], ACT.Copy
                               ).then_inc(hi_ready, 1)

            def residual_hi(norm, d, span):
                row = h[:, bass.ds(d, 1), span.first:T].rearrange("p a n -> p (a n)")
                act.activation(xg_hi[:, bass.ds(d, 1), span.first:T].rearrange("p a n -> p (a n)"), row,
                               ACT.Copy, scale=par[:, bass.ds(d + norm * KD, 1)]).then_inc(xg_hi_ready, 1)

            act.wait_ge(consts_in, 64)
            for u in range(2):
                if u == 0:
                    split_hi(0, KD)
                for d in range(4 * u, 4 * u + 4):
                    act.wait_ge(h_in, 32)
                    residual_hi(0, d, ALL)
                if u == 1:
                    split_hi(1, KD)
            act.wait_ge(lam_ready, 1)
            act.activation(lam[:, 2:4], lam[:, 0:2], ACT.Exp).then_inc(lam_exp, 1)

            def gate_up(st):
                u0, o0, f0 = st["u0"], st["o0"], st["f0"]
                span = st["span"]

                def feature(f, i, ks):
                    split_hi(u0 + 2, ks[0], i)
                    act.wait_ge(tile_out, i * 2 + (o0 + 1))
                    act.activation(s_buf[:, span.first:T], g_buf[:, span.first:T], ACT.Silu
                                   ).then_inc(silu_ready, 1)
                    split_hi(u0 + 3, ks[1], i)
                    act.wait_ge(gated, i + (f0 + 1))
                    act.nop()
                    act.activation(act_hi[:, bass.ds(f, 1), span.first:T].rearrange("p a n -> p (a n)"),
                                   p_buf[:, span.first:T], ACT.Copy).then_inc(act_hi_ready, 1)

                with act.Fori(0, FH - 1) as f:
                    feature(f, f, (KD, KD))
                feature(FH - 1, FH - 1, (FH, FH))

            def down(st):
                u0, o0, span = st["u0"], st["o0"], st["span"]

                def pair(i, ks):
                    for c in range(2):
                        if ks:
                            split_hi(u0 + c + 2, ks[c], i)
                        if st["last"] and st["norm"] < NORMS - 1:
                            act.wait_ge(tile_out, i * 2 + (o0 + c + 1))
                            act.nop()
                            residual_hi(st["norm"], i * 2 + c, span)

                with act.Fori(0, KD // 2 - 1) as i:
                    pair(i, (st["k"], st["k"]))
                pair(KD // 2 - 1, unit_k[u0 + KD:u0 + KD + 2])

            def exponentials(it):
                for c, (x, pair, _) in enumerate(it.sets):
                    slot = scores_ps[pair]
                    act.wait_ge(max_ready, x + 1)
                    if it.kind == "diff":
                        if it.before[1].kind == "diff":
                            act.wait_ge(mix_ready, it.before[1].mix)
                        else:
                            act.wait_ge(pt_full, it.before[1].t_end)
                    elif it.before[2]:
                        act.wait_ge(pt_full, it.before[2].t_end)
                    if it.kind == "swa":
                        lo = 0 if it.i > 1 else P
                        for kv in range(2):
                            k = 2 * it.p + kv
                            ex = act.activation(e_win[:, it.m % 2, kv, lo:2 * P + META],
                                                slot[:, kv, lo:2 * P + META], ACT.Exp,
                                                bias=neg_max[:, it.g % 2, k:k + 1], scale=it.scale,
                                                accum_out=row_sum[:, it.g % 2, k:k + 1])
                    else:
                        k = 2 * it.p + c
                        e = e_buf[c if it.kind == "diff" else it.m % 2][:, 0, :]
                        if len(it.chunks) == 1:
                            dst, src = e[:, 0:it.width], slot[:, 0, 0:it.width]
                        else:
                            dst = e[:, 0:it.width].rearrange("p (c n) -> p c n", c=2)
                            src = slot[:, :, 0:HALF_T]
                        ex = act.activation(dst, src, ACT.Exp, bias=neg_max[:, it.g % 2, k:k + 1],
                                            scale=it.scale, accum_out=row_sum[:, it.g % 2, k:k + 1])
                    ex.then_inc(exp_done, 1)
                if it.kind == "swa" and it.last:
                    act.wait_ge(sink_sum, it.hd + 1)
                    act.activation(sink_e[:, :], sink_s[:, :], ACT.Exp).then_inc(sink_exp, 1)

            def copy_probabilities(it, part):
                pt = (pt_swa if it.kind == "swa" else pt_ab)[:, it.m % 2, :]
                if part == 0 and it.before[2]:
                    act.wait_ge(pv_done, it.before[2].n + 1)
                act.wait_ge(pt_full, it.t0 + part + 1)
                pos, nb = it.turns[part][0][1], len(it.turns[part])
                act.activation(pt[:, pos * P:(pos + nb) * P], turn_ps[:, 0:nb * P], ACT.Copy
                               ).then_inc(pt_out, 1)

            def output_hi(it):
                act.wait_ge(o_turned, it.g + 1)
                src = turn_ps
                if it.i == 0:
                    k0 = 0 if it.kind == "diff" else 4
                    dst = act_hi[:, k0:k0 + 4, 0:META]
                    src = turn_ps.rearrange("p (f q) -> p f q", q=P)[:, :, 0:META]
                else:
                    dst = act_hi[:, it.hd + (4 if it.kind == "mla" else 0), META:T]
                if it.kind == "diff":
                    act.activation(dst, src, ACT.Copy, scale=gain_sub[:, 0:1]).then_inc(o_hi, 1)
                else:
                    act.activation(dst, src, ACT.Copy).then_inc(o_hi, 1)

            def beat(items, m):
                at = lambda k: items[k] if 0 <= k < len(items) else None
                output = outputs_at(at, m)
                if output:
                    output_hi(output)
                if at(m - 1):
                    copy_probabilities(at(m - 1), 0)
                if at(m):
                    exponentials(at(m))
                if at(m - 1) and len(at(m - 1).turns) > 1:
                    copy_probabilities(at(m - 1), 1)

            def projections(st):
                items, m = st["items"], 0
                for at, its_tiles in enumerate(st["units"]):
                    u = st["u0"] + at
                    for _ in (its_tiles[0].beats or [()])[0]:
                        beat(items, m)
                        m += 1
                    split_hi(u + 2, unit_k[u + 2])
                    for t in its_tiles:
                        if t.kind == "low_rank":
                            act.wait_ge(tile_out, t.o + 1)
                            col = (C_QN, C_QN + 1, C_KVN, C_KVN + 1)[t.index]
                            act.activation(act_hi[:, t.index, :], craw[:, t.index, :], ACT.Copy,
                                           scale=par[:, col:col + 1]).then_inc(low_hi_ready, 1)
                            act.wait_ge(summed, t.sq - 1)
                            act.activation(square[:, :], craw[:, t.index, :], ACT.Square
                                           ).then_inc(squared, 1)
                        if t.beats:
                            for there in t.beats[1]:
                                if there:
                                    beat(items, m)
                                    m += 1
                while m < len(items) + 4:
                    beat(items, m)
                    m += 1

            for st in stages:
                if st["kind"] == "gu":
                    gate_up(st)
                elif st["kind"] == "dn":
                    down(st)
                elif st["kind"] == "proj":
                    projections(st)

        @block.vector
        def _(dve):
            steps = [0]

            def step(ins):
                steps[0] += 1
                ins.then_inc(vec_step, 1)
                dve.wait_ge(vec_step, steps[0])

            def split_lo(u, k, i=0):
                dve.wait_ge(hi_ready, i * 2 + (u + 1))
                dve.tensor_tensor(w_lo[:, u % 2, 0:k * P], raw[:, u % 2, 0:k * P],
                                  w_hi[:, u % 2, 0:k * P], ALU.subtract).then_inc(lo_ready, 1)

            def residual_lo(norm, d, span):
                dve.wait_ge(xg_hi_ready, d + (norm * KD + 1))
                cols = slice(span.first, T)
                dve.scalar_tensor_tensor(
                    out=xg_lo[:, bass.ds(d, 1), cols].rearrange("p a n -> p (a n)"),
                    in0=h[:, bass.ds(d, 1), cols].rearrange("p a n -> p (a n)"),
                    scalar=par[:, bass.ds(d + norm * KD, 1)],
                    in1=xg_hi[:, bass.ds(d, 1), cols].rearrange("p a n -> p (a n)"),
                    op0=ALU.mult, op1=ALU.subtract).then_inc(xg_lo_ready, 1)

            def residual_square(sq0, d, span):
                row = h[:, bass.ds(d, 1), span.first:T].rearrange("p a n -> p (a n)")
                if sq0 or d:
                    dve.wait_ge(summed, d + sq0)
                dve.tensor_tensor(square[:, span.first:T], row, row, ALU.mult).then_inc(squared, 1)

            def stats_mean(a, span, n_features):
                dve.wait_ge(aux_full, a + 1)
                n = len(span.stat_starts)
                dve.tensor_scalar(mean_sq[:, 0:n], aux_ps[a % 2][:, 0, 0:n], 1.0 / n_features, EPS,
                                  ALU.mult, ALU.add).then_inc(aux_out, 1)

            def stats_take(a, span, dst):
                dve.wait_ge(aux_full, a + 1)
                dve.tensor_copy(span.sb(dst[:, :]), span.ps(aux_ps[a % 2])).then_inc(aux_out, 1)
                dve.wait_ge(aux_out, a + 1)

            dve.wait_ge(consts_in, 64)
            dve.wait_ge(h_in, 32)
            for u in range(2):
                if u == 0:
                    split_lo(0, KD)
                for d in range(4 * u, 4 * u + 4):
                    residual_square(0, d, ALL)
                    residual_lo(0, d, ALL)
                if u == 1:
                    split_lo(1, KD)
            for n in range(2):
                step(dve.tensor_tensor(lam_prod[:, :], rows[:, 128 * n:128 * n + 64],
                                       rows[:, 128 * n + 64:128 * n + 128], ALU.mult))
                ins = dve.tensor_reduce(lam[:, n:n + 1], lam_prod[:, :], AX.X, ALU.add)
                if n == 0:
                    step(ins)
            ins.then_inc(lam_ready, 1)
            dve.wait_ge(lam_exp, 1)
            step(dve.tensor_tensor(lam[:, 4:5], lam[:, 3:4], lam[:, 2:3], ALU.subtract))
            step(dve.tensor_scalar(lam[:, 5:6], lam[:, 4:5], LAMBDA_INIT, None, ALU.subtract))
            step(dve.tensor_scalar(gain_sub[:, :], par[:, C_SUBLN:C_SUBLN + 1], 1.0 - LAMBDA_INIT, None,
                                   ALU.mult))
            step(dve.tensor_scalar(neg_sink[:, :], rows[:, 256:256 + SH], -1.0, None, ALU.mult))

            def gate_up(st):
                u0, o0, f0, span, s = st["u0"], st["o0"], st["f0"], st["span"], st["stats"]
                cols = slice(span.first, T)
                if s:
                    stats_mean(s["a"], span, D)
                    stats_take(s["a"] + 1, span, rbc)

                def feature(f, i, ks):
                    pair = [tiles_ps[(o0 + c) % 2] for c in range(2)]
                    dve.wait_ge(tile_full, i * 2 + (o0 + 1))
                    dve.tensor_tensor(span.sb(g_buf[:, :]), span.ps(pair[0]), span.sb(rbc[:, :]), ALU.mult
                                      ).then_inc(tile_out, 1)
                    split_lo(u0 + 2, ks[0], i)
                    dve.wait_ge(tile_full, i * 2 + (o0 + 2))
                    dve.tensor_tensor(span.sb(u_buf[:, :]), span.ps(pair[1]), span.sb(rbc[:, :]), ALU.mult
                                      ).then_inc(tile_out, 1)
                    dve.wait_ge(silu_ready, i + (f0 + 1))
                    dve.wait_ge(tile_out, i * 2 + (o0 + 2))
                    dve.tensor_tensor(p_buf[:, cols], s_buf[:, cols], u_buf[:, cols], ALU.mult
                                      ).then_inc(gated, 1)
                    split_lo(u0 + 3, ks[1], i)
                    dve.wait_ge(act_hi_ready, i + (f0 + 1))
                    dve.tensor_tensor(act_lo[:, bass.ds(f, 1), cols].rearrange("p a n -> p (a n)"),
                                      p_buf[:, cols],
                                      act_hi[:, bass.ds(f, 1), cols].rearrange("p a n -> p (a n)"),
                                      ALU.subtract).then_inc(act_lo_ready, 1)

                with dve.Fori(0, FH - 1) as f:
                    feature(f, f, (KD, KD))
                feature(FH - 1, FH - 1, (FH, FH))

            def down(st):
                u0, o0, span = st["u0"], st["o0"], st["span"]

                def pair(i, ks):
                    for c in range(2):
                        d = i * 2 + c
                        row = span.sb(h[:, bass.ds(d, 1), :].rearrange("p a n -> p (a n)"))
                        ps = span.ps(tiles_ps[(o0 + c) % 2])
                        dve.wait_ge(tile_full, i * 2 + (o0 + c + 1))
                        if st["weights"] == "dn":
                            ins = dve.scalar_tensor_tensor(out=row, in0=ps, scalar=0.5, in1=row,
                                                           op0=ALU.mult, op1=ALU.add)
                        elif st["bias"]:
                            ins = dve.scalar_tensor_tensor(out=row, in0=ps, scalar=par[:, bass.ds(d + C_BOUT, 1)],
                                                           in1=row, op0=ALU.add, op1=ALU.add)
                        else:
                            ins = dve.tensor_tensor(row, ps, row, ALU.add)
                        ins.then_inc(tile_out, 1)
                        if st["last"]:
                            dve.wait_ge(tile_out, i * 2 + (o0 + c + 1))
                            residual_square(st["sq0"], d, span)
                        if ks:
                            split_lo(u0 + c + 2, ks[c], i)
                        if st["last"] and st["norm"] < NORMS - 1:
                            residual_lo(st["norm"], d, span)

                with dve.Fori(0, KD // 2 - 1) as i:
                    pair(i, (st["k"], st["k"]))
                pair(KD // 2 - 1, unit_k[u0 + KD:u0 + KD + 2])

            def auxiliary(jobs, pair=None):
                for what, a, of in jobs:
                    src = pair or aux_ps[a % 2]
                    if what == "columns":
                        stats_mean(a, ALL, 256)
                    elif what == "spread":
                        stats_take(a, ALL, rbc_q if of == stats_of_ab + 1 else rbc_kv)
                    elif what == "rotate":
                        cos, sin = (cos_p, sin_p) if of.kind == "rope_p" else (cos_m, sin_m)
                        dst = dest[of.dst][of.index]
                        if of.dst in ("dk", "kr"):
                            dve.memset(dst[0][64:P, :], 0.0)
                            dve.memset(dst[1][0:64, :], 0.0)
                        elif of.dst == "sk":
                            dve.memset(sk_win[64:P, 0, :, :], 0.0)
                            dve.memset(sk_win[0:64, 1, :, :], 0.0)
                        dve.wait_ge(tile_out, of.o + 1)
                        step(dve.tensor_tensor(turned[:, :], pre[:, :], cos, ALU.mult))
                        dve.wait_ge(aux_full, a + 1)
                        dve.tensor_tensor(ALL.sb(pre[:, :]), ALL.ps(src), ALL.sb(sin), ALU.mult
                                          ).then_inc(aux_out, 1)
                        dve.wait_ge(aux_out, a + 1)
                        if of.dst in ("dk", "kr"):
                            dve.tensor_tensor(dst[0][0:64, :], pre[0:64, :], turned[0:64, :], ALU.add)
                            dve.tensor_tensor(dst[1][64:P, :], pre[64:P, :], turned[64:P, :], ALU.add
                                              ).then_inc(rope_done, 1)
                        elif of.dst == "sk":
                            step(dve.tensor_tensor(dst[:, :], pre[:, :], turned[:, :], ALU.add))
                            for kv in range(2):
                                half = slice(64 * kv, 64 * (kv + 1))
                                dve.tensor_copy(sk_win[half, kv, :, 2 * P:2 * P + META],
                                                dst[half, 0:META].unsqueeze(1).to_broadcast([64, 4, META]))
                                for i in range(1, 5):
                                    lo = 0 if i > 1 else P
                                    k0 = TILE_START[i] - P + lo
                                    cp = dve.tensor_copy(sk_win[half, kv, i - 1, lo:2 * P],
                                                         dst[half, k0:k0 + 2 * P - lo])
                            cp.then_inc(rope_done, 1)
                        else:
                            dve.tensor_tensor(dst[:, :], pre[:, :], turned[:, :], ALU.add
                                              ).then_inc(rope_done, 1)
                    else:
                        dst = dest[of.dst]
                        cols = slice(of.index * P, (of.index + 1) * P)
                        dve.wait_ge(aux_full, a + 1)
                        dve.tensor_copy(dst[0:META, 0, cols], src[0:META, 1, 0:P])
                        dve.tensor_copy(dst[:, 1:5, cols],
                                        src[:, 0, :].rearrange("p (j n) -> p j n", j=4)
                                        ).then_inc(aux_out, 1)

            def maxima(it):
                for c, (x, pair, _) in enumerate(it.sets):
                    slot = scores_ps[pair]
                    dve.wait_ge(scores_full, x + 1)
                    if it.kind == "swa":
                        lo = 0 if it.i > 1 else P
                        k = slice(2 * it.p, 2 * it.p + 2)
                        step(dve.tensor_reduce(row_max[:, it.g % 2, k], slot[:, :, lo:2 * P + META],
                                               AX.X, ALU.max))
                        dve.scalar_tensor_tensor(out=neg_max[:, it.g % 2, k], in0=row_max[:, it.g % 2, k],
                                                 scalar=-it.scale,
                                                 in1=neg_sink[:, 2 * it.hd:2 * it.hd + 2],
                                                 op0=ALU.mult, op1=ALU.min).then_inc(max_ready, 1)
                    else:
                        k = 2 * it.p + c
                        src, axis = ((slot[:, 0, 0:it.width], AX.X) if len(it.chunks) == 1 else
                                     (slot[:, :, 0:HALF_T], AX.XY))
                        step(dve.tensor_reduce(row_max[:, it.g % 2, k:k + 1], src, axis, ALU.max))
                        dve.tensor_scalar(neg_max[:, it.g % 2, k:k + 1], row_max[:, it.g % 2, k:k + 1],
                                          -it.scale, None, ALU.mult).then_inc(max_ready, 1)
                if it.kind == "swa" and it.last:
                    dve.wait_ge(max_ready, it.sets[0][0] + 1)
                    two = rows[:, 256 + 2 * it.hd:258 + 2 * it.hd].unsqueeze(1).to_broadcast([P, 4, 2])
                    dve.tensor_tensor(sink_s[:, :].rearrange("p (i v) -> p i v", v=2),
                                      neg_max[:, it.g % 2, :].rearrange("p (i v) -> p i v", v=2),
                                      two, ALU.add).then_inc(sink_sum, 1)

            def combine(it):
                k = 2 * it.p
                dve.wait_ge(exp_done, it.sets[1][0] + 1)
                step(dve.reciprocal(coef[:, 0:1], row_sum[:, it.g % 2, k + 1:k + 2]))
                step(dve.scalar_tensor_tensor(out=coef[:, 1:2], in0=row_sum[:, it.g % 2, k:k + 1],
                                              scalar=lam[:, 5:6], in1=coef[:, 0:1],
                                              op0=ALU.mult, op1=ALU.mult))
                if it.before[2].kind == "diff":
                    dve.wait_ge(pt_full, it.before[2].t_end)
                w = it.width
                dve.scalar_tensor_tensor(out=mix[:, it.m % 2, 0:w], in0=e_buf[1][:, 0, 0:w],
                                         scalar=coef[:, 1:2], in1=e_buf[0][:, 0, 0:w],
                                         op0=ALU.mult, op1=ALU.add).then_inc(mix_ready, 1)

            def normalise(it):
                sums = row_sum[:, it.g % 2, :]
                if it.kind == "swa":
                    dve.wait_ge(sink_exp, it.hd + 1)
                    step(dve.tensor_tensor(inv_sum[:, 0, :], sums, sink_e[:, :], ALU.add))
                    step(dve.reciprocal(inv_sum[:, 1, :], inv_sum[:, 0, :]))
                    n, d = 8, SD
                else:
                    n, d = 4, P
                    dve.wait_ge(exp_done, it.sets[-1][0] + 1)
                    step(dve.reciprocal(inv_sum[:, 1, 0:4], sums[:, 0:8:2]))
                o = o_nat[:, :].rearrange("p (f d) -> p f d", d=d)
                dve.wait_ge(pv_done, it.n + 1)
                dve.tensor_tensor(o, value_ps.rearrange("p (f d) -> p f d", d=d),
                                  inv_sum[:, 1, 0:n].unsqueeze(2).to_broadcast([P, n, d]), ALU.mult
                                  ).then_inc(o_taken, 1)
                if it.kind != "diff":
                    return
                dve.wait_ge(o_taken, it.g + 1)
                step(dve.tensor_tensor(o_sq[:, :], o_nat[:, :], o_nat[:, :], ALU.mult))
                step(dve.tensor_reduce(o_ms[:, :], o_sq[:, :].rearrange("p (f d) -> p f d", d=P),
                                       AX.X, ALU.add))
                dve.tensor_scalar(o_mse[:, :], o_ms[:, :], 1.0 / DV, DIFF_EPS, ALU.mult, ALU.add
                                  ).then_inc(o_mean, 1)

            def output_norm(it):
                dve.wait_ge(o_rstd_ready, it.g - 4)
                o = o_nat[:, :].rearrange("p (f d) -> p f d", d=P)
                dve.tensor_tensor(o, o, o_rstd[:, :].unsqueeze(2).to_broadcast([P, 4, P]), ALU.mult
                                  ).then_inc(o_ready, 1)

            def output_lo(it):
                dve.wait_ge(o_hi, it.g + 1)
                src = turn_ps
                if it.i == 0:
                    k0 = 0 if it.kind == "diff" else 4
                    hi, lo = (x[:, k0:k0 + 4, 0:META] for x in (act_hi, act_lo))
                    src = turn_ps.rearrange("p (f q) -> p f q", q=P)[:, :, 0:META]
                else:
                    hi, lo = (x[:, it.hd + (4 if it.kind == "mla" else 0), META:T] for x in (act_hi, act_lo))
                if it.kind == "diff":
                    dve.scalar_tensor_tensor(out=lo, in0=src, scalar=gain_sub[:, 0:1], in1=hi,
                                             op0=ALU.mult, op1=ALU.subtract).then_inc(o_lo, 1)
                else:
                    dve.tensor_tensor(lo, src, hi, ALU.subtract).then_inc(o_lo, 1)

            def beat(items, m):
                at = lambda k: items[k] if 0 <= k < len(items) else None
                output = outputs_at(at, m)
                if output:
                    output_lo(output)
                if at(m - 1) and at(m - 1).kind == "diff":
                    combine(at(m - 1))
                if at(m - 3) and at(m - 3).last and at(m - 3).kind == "diff":
                    output_norm(at(m - 3))
                if at(m):
                    maxima(at(m))
                if at(m - 2) and at(m - 2).last:
                    normalise(at(m - 2))

            def projections(st):
                for v in (("dv", "mv") if st["which"] == "ab" else ("sv",)):
                    step(dve.memset(dest[v][:, 0, :], 0.0))
                if st["which"] == "swa":
                    step(dve.memset(e_win[:, :, :, 2 * P + META:3 * P], 0.0))
                turned_last = 0
                s, items, m = st["stats"], st["items"], 0
                stats_mean(s["a"], ALL, D)
                stats_take(s["a"] + 1, ALL, rbc)
                for at, its_tiles in enumerate(st["units"]):
                    u = st["u0"] + at
                    for t in its_tiles:
                        for _ in (t.beats or [()])[0]:
                            beat(items, m)
                            m += 1
                        pair = tiles_ps[t.o % 2 if t.beats is None else 0]
                        dve.wait_ge(tile_full, t.o + 1)
                        if t.kind in ("rope_p", "rope_m", "value"):
                            dst = pre
                        else:
                            dst = dest[t.dst][t.index]
                        r = rbcs[t.src]
                        if dst is pre and turned_last:
                            dve.wait_ge(rope_done, turned_last)
                        dve.tensor_tensor(ALL.sb(dst[:, :]), ALL.ps(pair), ALL.sb(r[:, :]), ALU.mult
                                          ).then_inc(tile_out, 1)
                        if t.bias is not None:
                            col = C_BQKV + t.bias
                            dve.wait_ge(tile_out, t.o + 1)
                            dve.tensor_scalar(pre[:, :], pre[:, :], par[:, col:col + 1], None, ALU.add
                                              ).then_inc(biased, 1)
                            dve.wait_ge(biased, t.biased)
                        if t.beats and t.beats[1][0]:
                            beat(items, m)
                            m += 1
                        if t is its_tiles[-1] and t.beats is None:
                            split_lo(u + 2, unit_k[u + 2])
                        if t.kind == "low_rank":
                            col = (C_QN, C_QN + 1, C_KVN, C_KVN + 1)[t.index]
                            dve.wait_ge(low_hi_ready, t.low)
                            dve.scalar_tensor_tensor(out=act_lo[:, t.index, :], in0=craw[:, t.index, :],
                                                     scalar=par[:, col:col + 1], in1=act_hi[:, t.index, :],
                                                     op0=ALU.mult, op1=ALU.subtract).then_inc(low_lo_ready, 1)
                        auxiliary(t.jobs, None if t.beats is None else tiles_ps[0])
                        if t.kind in ("rope_p", "rope_m"):
                            turned_last = t.rope
                        if t.beats:
                            split_lo(u + 2, unit_k[u + 2])
                            if t.beats[1][1]:
                                beat(items, m)
                                m += 1
                while m < len(items) + 4:
                    beat(items, m)
                    m += 1

            dve.wait_ge(tables_in, 16)
            for st in stages:
                if st["kind"] == "gu":
                    gate_up(st)
                elif st["kind"] == "dn":
                    down(st)
                elif st["kind"] == "proj":
                    projections(st)
                else:
                    s = st["stats"]
                    stats_mean(s["a"], OUT, D)
                    stats_take(s["a"] + 1, OUT, rbc)
                    for d in range(KD):
                        col = (NORMS - 1) * KD + d
                        dve.scalar_tensor_tensor(out=final[:, d, META:T], in0=h[:, d, META:T],
                                                 scalar=par[:, col:col + 1], in1=rbc[:, META:T],
                                                 op0=ALU.mult, op1=ALU.mult).then_inc(final_ready, 1)

        @block.gpsimd
        def _(pool):
            cleared = [0]

            def sum_squares(sq0, n, span, taken):
                if taken:
                    pool.wait_ge(aux_full, taken)
                cleared[0] += 1
                pool.memset(square_sum[:, :], 0.0).then_inc(sum_clear, 1)
                pool.wait_ge(sum_clear, cleared[0])
                cols = slice(span.first, T)
                with pool.Fori(0, n) as d:
                    pool.wait_ge(squared, d + (sq0 + 1))
                    pool.tensor_tensor(square_sum[:, cols], square_sum[:, cols], square[:, cols], ALU.add
                                       ).then_inc(summed, 1)
                    pool.wait_ge(summed, d + (sq0 + 1))

            def rstd_of(a, r, n):
                pool.wait_ge(aux_out, a + 1)
                pool.tensor_tensor(rstd[:, 0:n], mean_sq[:, 0:n], minus_half.to_broadcast([P, n]), ALU.pow
                                   ).then_inc(rstd_ready, 1)

            pool.wait_ge(consts_in, 64)
            sum_squares(0, KD, ALL, 0)
            taken = 0
            for st in stages:
                s = st.get("stats")
                if s:
                    rstd_of(s["a"], s["r"], len(s["span"].stat_starts))
                    taken = s["a"] + 1
                if st["kind"] == "dn" and st["last"]:
                    if not st["act_lo"]:
                        pool.wait_ge(o_lo, st["o_lo"])
                    sum_squares(st["sq0"], KD, st["span"], taken)
                elif st["kind"] == "proj" and st["which"] == "ab":
                    for t in st["flat"]:
                        if t.kind == "low_rank" and t.index % 2 == 1:
                            sum_squares(t.sq - 2, 2, ALL, taken)
                            a = t.jobs[-1][1]
                            rstd_of(a, stats_of_ab + 1 + t.index // 2, 6)
                            taken = a + 1
                    for g in range(5):
                        pool.wait_ge(o_mean, g + 1)
                        pool.tensor_tensor(o_rstd[:, :], o_mse[:, :], minus_half.to_broadcast([P, 4]), ALU.pow
                                           ).then_inc(o_rstd_ready, 1)
    return nc


def shape_constants():
    f = np.float32
    rot = np.zeros((2, P, P), f)
    for n, half, width in ((0, 8, 16), (1, 32, 64)):
        for start in (0, 64):
            for j in range(half):
                rot[n, start + half + j, start + j] = -1.0
                rot[n, start + j, start + half + j] = 1.0
    con = np.concatenate([np.eye(P, dtype=f), rot[0], rot[1], np.ones((P, 1), f),
                          np.full((P, 1), -0.5, f)], axis=1)
    tab = np.zeros((P, 4, T), f)
    pos = np.arange(T, dtype=f)
    for n, width in ((0, 16), (1, 64)):
        inv = np.power(f(500000.0), -np.arange(0, width, 2, dtype=f) / f(width)).astype(f)
        ang = pos[:, None] * inv[None, :]
        cos, sin = np.cos(ang).astype(f), np.sin(ang).astype(f)
        for p in range(P):
            d = p % 64
            if d < width:
                tab[p, 2 * n] = cos[:, d % (width // 2)]
                tab[p, 2 * n + 1] = sin[:, d % (width // 2)]
            else:
                tab[p, 2 * n] = 1.0
    q, k = np.arange(P)[:, None], np.arange(P)[None, :]
    masks = np.concatenate([np.eye(P), np.where(k > q, 0.0, MASKED), np.where(k <= q, 0.0, MASKED)],
                           axis=1).astype(mybir.dt.np(BF16))
    return con, tab, masks


def kernel(**inputs):
    from concourse import bacc
    from concourse.bass_utils import run_bass_kernel_spmd

    x = {k: np.asarray(v) for k, v in inputs.items()}

    def units(w):
        kk, m = w.shape
        return np.ascontiguousarray(w.reshape(kk // P, P, m // P, P).transpose(2, 1, 0, 3)
                                    ).reshape(m // P, P, kk)

    def cols(v):
        return v.reshape(-1, P).T

    gu, dn = [], []
    for layer, name in ((0, "ffn1"), (0, "ffn2"), (1, "ffn1"), (1, "ffn2")):
        pair = np.stack([units(x[name + "_w_gate"][layer]), units(x[name + "_w_up"][layer])], axis=1)
        gu.append(pair.reshape(2 * pair.shape[0], P, D))
        down = x[name + "_w_down"][layer]
        dn += [units(down[half * FH * P:(half + 1) * FH * P]) for half in range(2)]
    w = x["ab_w_in"][0]
    cut = np.split(w, [512, 1024, 1536, 1792, 2048], axis=1)
    by_head = [part[:, P * i:P * (i + 1)] for i in range(4) for part in cut[0:3]]
    w_ab = np.concatenate([cut[3], cut[4], cut[5], cut[5]] + by_head, axis=1)
    uq = x["mla_w_uq"][0].reshape(256, MH, 192)
    uq = np.concatenate([uq[:, :, :128].reshape(256, 512), uq[:, :, 128:].reshape(256, 256)], axis=1)
    ukv = x["mla_w_ukv"][0].reshape(256, MH, 256)
    ukv = np.concatenate([ukv[:, :, :128].reshape(256, 512), ukv[:, :, 128:].reshape(256, 512)], axis=1)

    def grouped(w, n):
        t = units(w)
        return np.ascontiguousarray(t.reshape(len(t) // n, n, P, 256).transpose(0, 2, 1, 3)
                                    ).reshape(len(t) // n, P, n * 256)

    def by_pair(v):
        lead = v.shape[:-1]
        q = v[..., :1024].reshape(*lead, 2, 8, 64)
        q = np.swapaxes(q, -3, -2).reshape(*lead, 1024)
        return np.concatenate([v[..., 1024:], q], axis=-1)

    swo = np.swapaxes(x["swa_w_out"][0].reshape(2, 8, 64, D), 0, 1).reshape(D, D)
    norms = [x["ffn1_norm"][0], x["mix_norm"][0], x["ffn2_norm"][0], x["ffn1_norm"][1],
             x["mix_norm"][1], x["ffn2_norm"][1], x["final_norm"]]
    params = np.concatenate([cols(v) for v in norms] +
                            [cols(x["mla_q_norm"][0]), cols(x["mla_kv_norm"][0]), cols(x["diff_subln"][0]),
                             cols(by_pair(x["swa_b_qkv"][0])), cols(x["swa_b_out"][0])], axis=1)
    row = np.concatenate([x["diff_lambda_q1"][0], x["diff_lambda_k1"][0], x["diff_lambda_q2"][0],
                          x["diff_lambda_k2"][0], x["swa_sinks"][0].reshape(2, 8).T.reshape(-1)])
    tokens = np.concatenate([x["meta_tokens"], x["x"][0]], axis=0)
    con, tab, masks = shape_constants()
    arrays = {
        "x_t": tokens.T.reshape(KD, P, T).transpose(1, 0, 2),
        "w_gu": np.concatenate(gu), "w_dn": np.concatenate(dn), "w_ab": units(w_ab),
        "w_uq": grouped(uq, 3), "w_ukv": grouped(ukv, 4), "w_abo": units(x["ab_w_out"][0]),
        "w_swa": units(by_pair(x["swa_w_qkv"][0])), "w_swo": units(swo),
        "params": params, "row": row, "consts": con, "tables": tab, "masks": masks,
    }
    nc = bacc.Bacc("TRN2", target_bir_lowering=False, num_devices=1)
    args = {}
    for name, a in arrays.items():
        arrays[name] = np.ascontiguousarray(a)
        args[name] = nc.dram_tensor(name, a.shape, mybir.dt.from_np(a.dtype), kind="ExternalInput").ap()
    args["out"] = nc.dram_tensor("out", (P, KD, SEQ), F32, kind="ExternalOutput").ap()
    build(nc, **args)
    got = run_bass_kernel_spmd(nc, [arrays], core_ids=[0]).results[0]["out"]
    return np.ascontiguousarray(got.transpose(2, 1, 0).reshape(1, SEQ, D))
```

```python
from contextlib import ExitStack

import numpy as np

import concourse.bass as bass
from concourse import mybir

F32 = mybir.dt.float32
F32R = mybir.dt.float32r
BF16 = mybir.dt.bfloat16
ACT = mybir.ActivationFunctionType
ALU = mybir.AluOpType
AX = mybir.AxisListType

P = 128
D = 1024
KD = D // P
META = 16
SEQ = 512
T = META + SEQ
HALF_T = T // 2
F = 2816
FH = F // P // 2
EPS = 1e-6
DIFF_EPS = 1e-5
LAMBDA_INIT = 0.8 - 0.6 * 1.0
DH, DV = 4, 128
MH = 4
MLA_ITEMS = 5 * MH
SH, SD = 16, 64
KT_MAX = FH
ZEROED = {"ab": 8, "late": 12, "swa": 16}
TILE_START = [0] + [META + P * i for i in range(4)]
MASKED = -1e30

NORMS = 7
C_QN, C_KVN, C_SUBLN = NORMS * KD, NORMS * KD + 2, NORMS * KD + 4
C_BQKV = C_SUBLN + 1
C_BOUT = C_BQKV + 10
N_PARAMS = C_BOUT + KD
N_ROW = 4 * 64 + SH


class Span:

    def __init__(self, first):
        self.first, self.n = first, T - first
        if first == 0:
            self.width, self.chunks = HALF_T, [(0, 0), (1, HALF_T)]
            self.stat_starts = [c * HALF_T + s for c in range(2) for s in (0, P, HALF_T - P)]
        else:
            self.width, self.chunks = SEQ, [(0, first)]
            self.stat_starts = [first + P * s for s in range(SEQ // P)]

    def ps(self, pair):
        return pair[:, 0:len(self.chunks), 0:self.width]

    def sb(self, row):
        return row[:, self.first:T].rearrange("p (c n) -> p c n", c=len(self.chunks))

    def ps_at(self, pair, token, n):
        bank = (token - self.first) // self.width
        col = (token - self.first) % self.width
        return pair[:, bank, col:col + n]


ALL = Span(0)
OUT = Span(META)


class Tile:

    def __init__(self, kind, dst, index=0, k=KD, src="x", bias=None):
        self.kind, self.dst, self.index = kind, dst, index
        self.k, self.src, self.bias = k, src, bias
        self.jobs = []
        self.beats = None


class Item:

    def __init__(self, kind, i, hd, g, p):
        self.kind, self.i, self.hd, self.g, self.p = kind, i, hd, g, p
        self.scale = (192 if kind == "mla" else 64) ** -0.5
        if kind == "swa":
            self.blocks = [(kv, 3 * kv + b, b * P, kt) for kv in range(2)
                           for b, kt in ((0, i - 1), (1, i), (2, 0)) if b or i > 1]
            per = len(self.blocks) // 2
        else:
            self.blocks = [(0, j, TILE_START[j], j) for j in range(i + 1)]
            per = 4
        self.turns = [self.blocks[j:j + per] for j in range(0, len(self.blocks), per)]
        self.width = META + P * i if i else P
        self.chunks = ([(0, 0, self.width)] if self.width <= 512 else
                       [(c, c * HALF_T, HALF_T) for c in range(2)])


def ab_units():
    units = [[Tile("low_rank", "craw", i)] for i in range(4)]
    units += [[Tile("rope_m", "kr")]]
    uq = [Tile("plain", "mqn", i, 2, "cq") for i in range(4)]
    uq += [Tile("rope_m", "mqr", i, 2, "cq") for i in range(2)]
    ukv = [Tile("plain", "mkn", i, 2, "ckv") for i in range(4)]
    ukv += [Tile("value", "mv", i, 2, "ckv") for i in range(4)]
    units += [uq[0:3], uq[3:6], ukv[0:4], ukv[4:8]]
    for i in range(4):
        units += [[Tile("rope_p", "dq", i)], [Tile("rope_p", "dk", i)], [Tile("value", "dv", i)]]
    for n, unit in enumerate(units[9:]):
        unit[0].beats = [(), (True, True)] if n == 0 else [(4,), (True, True)] if n < 9 else [(), (True, True)]
    return units


def swa_units():
    units = [[Tile("rope_p", "sk", bias=0)], [Tile("value", "sv", bias=1)]]
    units += [[Tile("rope_p", "sq", i, bias=2 + i)] for i in range(8)]
    for n, unit in enumerate(units[2:]):
        unit[0].beats = [(), (False, False)] if n == 0 else [(2, 5), (True, True)]
    return units


def attention_items(which):
    items = []
    if which == "ab":
        for kind, g0 in (("mla", 0), ("diff", 5)):
            items += [Item(kind, i, hd, g0 + hd, i - 1) for hd in range(4) for i in range(1, 5)]
            items += [Item(kind, 0, hd, g0 + 4, hd) for hd in range(4)]
    else:
        items += [Item("swa", i, j, 10 + j, i - 1) for j in range(8) for i in range(1, 5)]
    return items


def beats_of(items):
    beats = [{} for _ in range(len(items) + 6)]
    for it in items:
        diff = it.kind == "diff"
        turn = it.m + (2 if diff else 1)
        steps = dict(scores=it.m, turn=turn, values=turn + 1)
        if diff:
            steps["combine"] = it.m + 1
        if it.last:
            steps["normalise"] = turn + 1
            if diff:
                steps["output_norm"] = turn + 2
            steps["output"] = turn + (3 if diff else 2)
        for step, beat in steps.items():
            assert step not in beats[beat]
            beats[beat][step] = it
    while not beats[-1]:
        beats.pop()
    return beats


def plan():
    unit_k, unit_last, stages = [], [], []
    at = dict(o=0, a=0, r=0, sq=KD, norm=0, rope=0, bias=0, low=0)
    att = dict(n=0, x=0, t=0, mix=0, g=0)

    def units(kind, ks, tiles_each, **more):
        st = dict(kind=kind, u0=len(unit_k), o0=at["o"], **more)
        for k, n in zip(ks, tiles_each):
            at["o"] += n
            unit_k.append(k)
            unit_last.append(at["o"] - 1)
        stages.append(st)
        return st

    def stats(span, sq):
        s = dict(span=span, a=at["a"], r=at["r"], sq=sq)
        at["a"] += 2
        at["r"] += 1
        return s

    def splits_h(st):
        at["norm"] += 1
        st.update(last=True, norm=at["norm"], sq0=at["sq"])
        at["sq"] += KD

    def ffn(n, span):
        at["gated"] = 2 * FH * (n + 1)
        for half in range(2):
            first = half == 0
            units("gu", [KD] * 2 * FH, [1] * 2 * FH, w0=(2 * n + half) * 2 * FH, f0=(2 * n + half) * FH,
                  norm=at["norm"], span=span, stats=stats(span, at["sq"]) if first else None)
            st = units("dn", [FH] * KD, [1] * KD, k=FH, span=span, scale=0.5, weights="dn",
                       w0=(2 * n + half) * KD, act_lo=(2 * n + half + 1) * FH, last=False)
        splits_h(st)

    def projections(which, its_units):
        st = units("proj", [sum(t.k for t in ts) for ts in its_units], [len(ts) for ts in its_units],
                   which=which, units=its_units, norm=at["norm"], act_lo=at["gated"], stats=stats(ALL, at["sq"]))
        flat = [t for ts in its_units for t in ts]
        for n, t in enumerate(flat):
            t.o = st["o0"] + n
            if t.bias is not None:
                at["bias"] += 1
                t.biased = at["bias"]
        for n, t in enumerate(flat):
            before = flat[n - 1] if n else None
            if before and before.kind == "low_rank" and before.index % 2:
                t.jobs.append(("spread", at["a"], at["r"]))
                at["a"] += 1
                at["r"] += 1
            if t.kind == "low_rank":
                at["sq"] += 1
                at["low"] += 1
                t.sq, t.low = at["sq"], at["low"]
                if t.index % 2:
                    t.jobs.append(("columns", at["a"], at["sq"]))
                    at["a"] += 1
            elif t.kind in ("rope_p", "rope_m"):
                at["rope"] += 1
                t.rope = at["rope"]
                t.jobs.append(("rotate", at["a"], t))
                at["a"] += 1
            elif t.kind == "value":
                t.jobs.append(("turn", at["a"], t))
                at["a"] += 1
        tiles = {(t.dst, t.index): t for t in flat}
        items = attention_items(which)
        in_pair = [None, None]
        for m, it in enumerate(items):
            it.m, it.n = m, att["n"]
            att["n"] += 1
            pairs = (0, 1) if it.kind == "diff" else (m % 2,)
            it.sets = []
            for pair in pairs:
                it.sets.append((att["x"], pair, in_pair[pair]))
                in_pair[pair] = att["x"]
                att["x"] += 1
            it.t0 = att["t"]
            att["t"] += len(it.turns)
            it.t_end = att["t"]
            if it.kind == "diff":
                att["mix"] += 1
                it.mix = att["mix"]
            it.last = m + 1 == len(items) or items[m + 1].g != it.g
            it.after = None
            if it.kind == "mla" and m == 0:
                it.after = tiles["mv", 3], tiles["mqr", 1], tiles["mv", 3]
            elif it.kind == "diff" and it.i == 1:
                it.after = None, tiles["dk", it.hd], tiles["dv", it.hd]
            elif it.kind == "swa" and it.i == 1:
                it.after = None, tiles["sq", it.hd], tiles["sv", 0]
            it.before = [items[m - k] if m >= k else None for k in range(5)]
        att["g"] = items[-1].g + 1
        st.update(flat=flat, items=items, beats=beats_of(items), groups=att["g"])

    def out_projection(weights, span, bias):
        st = units("dn", [KD] * KD, [1] * KD, k=KD, span=span, scale=1.0, bias=bias,
                   weights=weights, w0=0, act_lo=None, o_lo=att["g"])
        splits_h(st)

    ffn(0, ALL)
    projections("ab", ab_units())
    out_projection("abo", ALL, False)
    ffn(1, ALL)
    ffn(2, ALL)
    projections("swa", swa_units())
    out_projection("swo", OUT, True)
    ffn(3, OUT)
    stages.append(dict(kind="final", stats=stats(OUT, at["sq"])))
    return stages, unit_k, unit_last


def build(nc, x_t, w_gu, w_dn, w_ab, w_uq, w_ukv, w_abo, w_swa, w_swo, params, row, consts,
          tables, masks, out):
    stages, unit_k, unit_last = plan()
    ab, swa = (st for st in stages if st["kind"] == "proj")
    stats_of_ab = ab["stats"]["r"]
    ctx = ExitStack()
    with ctx:
        cursor = [(nc.sbuf_base + 31) // 32 * 32]

        def place(name, shape, dt, at=None):
            n = int(np.prod(shape[1:])) * (2 if dt == BF16 else 4)
            offset = cursor[0] if at is None else at
            if at is None:
                cursor[0] = (offset + n + 31) // 32 * 32
            return nc.alloc_sbuf_tensor_at(name, shape, dt, offset=offset)

        ROW = T * 4
        h = place("h", [P, KD, T], F32)
        at_xg = cursor[0]
        xg_hi = place("xg_hi", [P, KD, T], F32R)
        xg_lo = place("xg_lo", [P, KD, T], F32R)
        at_act = cursor[0]
        act_hi = place("act_hi", [P, FH, T], F32R)
        act_lo = place("act_lo", [P, FH, T], F32R)
        raw = place("raw", [P, 2, KT_MAX * P], F32)
        w_hi = place("w_hi", [P, 2, KT_MAX * P], F32R)
        w_lo = place("w_lo", [P, 2, KT_MAX * P], F32R)
        at_square = cursor[0]
        square = place("square", [P, T], F32)
        at_square_sum = cursor[0]
        square_sum = place("square_sum", [P, T], F32)
        rbc = place("rbc", [P, T], F32)
        con = place("con", [P, 3 * P + 2], F32)
        mask_bf = place("mask_bf", [P, 3 * P], BF16)
        par = place("par", [P, N_PARAMS], F32)
        rows = place("rows", [P, N_ROW], F32)
        mean_sq = place("mean_sq", [P, 8], F32)
        rstd = place("rstd", [P, 8], F32)
        lam = place("lam", [P, 8], F32)
        lam_prod = place("lam_prod", [P, 64], F32)
        gain_sub = place("gain_sub", [P, 1], F32)
        neg_max = place("neg_max", [P, 2, 8], F32)
        row_max = place("row_max", [P, 2, 8], F32)
        row_sum = place("row_sum", [P, 2, 8], F32)
        inv_sum = place("inv_sum", [P, 2, 8], F32)
        coef = place("coef", [P, 2], F32)
        sink_s = place("sink_s", [P, 8], F32)
        sink_e = place("sink_e", [P, 8], F32)
        neg_sink = place("neg_sink", [P, 16], F32)
        o_ms = place("o_ms", [P, 4], F32)
        o_mse = place("o_mse", [P, 4], F32)
        o_rstd = place("o_rstd", [P, 4], F32)

        ident, rot_p, rot_m = con[:, 0:P], con[:, P:2 * P], con[:, 2 * P:3 * P]
        one_col, minus_half = con[:, 3 * P:3 * P + 1], con[:, 3 * P + 1:3 * P + 2]
        ident_bf, window_bf = mask_bf[:, 0:P], mask_bf[:, P:3 * P]
        causal_bf = mask_bf[:, 2 * P:3 * P]

        tab = place("tab", [P, 4, T], F32)
        pt_ab = place("pt_ab", [P, 2, 5 * P], F32, cursor[0] - 2 * ROW)
        cursor[0] += 2 * 5 * P * 4 - 2 * ROW
        cos_p, sin_p, cos_m, sin_m = (tab[:, i, :] for i in range(4))

        at_att = cursor[0]
        g_buf = place("g_buf", [P, T], F32, at_att)
        u_buf = place("u_buf", [P, T], F32, at_att + ROW)
        s_buf = place("s_buf", [P, T], F32, at_att + 2 * ROW)
        p_buf = place("p_buf", [P, T], F32, at_att + 3 * ROW)
        final = place("final", [P, KD, T], F32, at_att + 4 * ROW)
        att = [place(f"att{i}", [P, T], F32, at_att + i * ROW) for i in range(19)]
        mqn, mqr, mkn = att[9:13], att[13:15], att[15:19]
        kr = [(att[3], att[8])]
        first_squares = att[4:12]
        dq = att[0:3] + att[15:16]
        dk = [(att[i], att[i + 1]) for i in (4, 6, 9, 11)]
        dv = place("dv", [P, 5, 512], F32, at_att + 19 * ROW)
        mv = place("mv", [P, 5, 512], F32, at_att + 19 * ROW + 10240)
        sq = place("sq", [P, 8, T], F32, at_att)
        sq = [sq[:, i, :] for i in range(8)]
        sk = [place("sk", [P, T], F32, at_att + 8 * ROW)]
        sv = place("sv", [P, 5, P], F32, at_att + 9 * ROW)
        pt_swa = place("pt_swa", [P, 2, 6 * P], F32, at_att + 9 * ROW + 5 * P * 4)
        e_win = place("e_win", [P, 2, 2, 3 * P], F32, at_att + 9 * ROW + 17 * P * 4)
        sk_win = place("sk_win", [P, 2, 4, 2 * P + META], F32, at_att + 9 * ROW + 29 * P * 4)
        dest = {"dq": dq, "dk": dk, "kr": kr, "mqn": mqn, "mqr": mqr, "mkn": mkn, "dv": dv,
                "mv": mv, "sq": sq, "sk": sk, "sv": sv}
        craw = place("craw", [P, 4, T], F32, at_act + 4 * ROW)
        pre = place("pre", [P, T], F32, at_act + 8 * ROW)
        turned = place("turned", [P, T], F32, at_act + 9 * ROW)
        rbc_q = place("rbc_q", [P, T], F32, at_act + 10 * ROW)
        rbc_kv = place("rbc_kv", [P, T], F32, at_act + (FH + 8) * ROW)
        rbcs = {"x": rbc, "cq": rbc_q, "ckv": rbc_kv}
        dest["craw"] = [craw[:, i, :] for i in range(4)]
        e_buf = place("e_buf", [P, 1, T], F32, at_act + 10 * ROW), \
            place("e_buf1", [P, 1, T], F32, at_act + (FH + 8) * ROW)
        mix = place("mix", [P, 2, T], F32, at_act + (FH + 9) * ROW)
        o_sq = place("o_sq", [P, 512], F32, at_square)
        o_nat = place("o_nat", [P, 512], F32, at_square_sum)

        tiles_ps = [ctx.enter_context(nc.psum_tensor(f"tile{i}", [P, 2, 512], F32)) for i in range(2)]
        aux_ps = [ctx.enter_context(nc.psum_tensor(f"aux{i}", [P, 2, 512], F32)) for i in range(2)]

        scores_ps = [tiles_ps[1], aux_ps[0]]
        turn_ps, value_ps = aux_ps[1][:, 0, :], aux_ps[1][:, 1, :]

        def sem(name):
            return ctx.enter_context(nc.semaphore(name))

        consts_in, tables_in, params_in = sem("consts_in"), sem("tables_in"), sem("params_in")
        h_in = [sem(f"h_in{i}") for i in range(4)]
        landed = [sem("landed0"), sem("landed1")]
        hi_ready = sem("hi_ready")
        lo_ready = sem("lo_ready")
        tile_full = sem("tile_full")
        tile_out = sem("tile_out")
        aux_full = sem("aux_full")
        aux_out = sem("aux_out")
        xg_hi_ready = sem("xg_hi_ready")
        xg_lo_ready = sem("xg_lo_ready")
        squared = sem("squared")
        sum_clear = sem("sum_clear")
        summed = sem("summed")
        rstd_ready = sem("rstd_ready")
        silu_ready = sem("silu_ready")
        gated = sem("gated")
        act_hi_ready = sem("act_hi_ready")
        act_lo_ready = sem("act_lo_ready")
        lam_ready = sem("lam_ready")
        lam_exp = sem("lam_exp")
        low_hi_ready = sem("low_hi_ready")
        low_lo_ready = sem("low_lo_ready")
        biased = sem("biased")
        rope_done = sem("rope_done")
        scores_full = sem("scores_full")
        max_ready = sem("max_ready")
        exp_done = sem("exp_done")
        mix_ready = sem("mix_ready")
        pt_full = sem("pt_full")
        pt_out = sem("pt_out")
        pv_done = sem("pv_done")
        sink_sum = sem("sink_sum")
        sink_exp = sem("sink_exp")
        o_mean = sem("o_mean")
        o_rstd_ready = sem("o_rstd_ready")
        o_taken = sem("o_taken")
        o_ready = sem("o_ready")
        o_turned = sem("o_turned")
        o_hi = sem("o_hi")
        o_lo = sem("o_lo")
        final_ready = sem("final_ready")
        zeroed = sem("zeroed")
        stored = sem("stored")
        vec_step = sem("vec_step")

        def landed_count(u):
            return 16 * (u // 2 + 1)

        block = ctx.enter_context(nc.Block())

        @block.sync
        def _(sp):
            sp.dma_start(raw[:, 0, 0:KD * P], w_gu[0, :, :]).then_inc(landed[0], 16)
            sp.dma_start(par[:, :], params).then_inc(params_in, 16)
            for part in range(4):
                ks = slice(part * KD // 4, (part + 1) * KD // 4)
                sp.dma_start(h[:, ks, :], x_t[:, ks, :]).then_inc(h_in[part], 16)
            sp.dma_start(raw[:, 1, 0:KD * P], w_gu[1, :, :]).then_inc(landed[1], 16)
            sp.dma_start(con[:, :], consts).then_inc(consts_in, 16)
            sp.dma_start(mask_bf[:, :], masks).then_inc(consts_in, 16)
            sp.dma_start(rows[:, :], row.partition_broadcast(P)).then_inc(consts_in, 16)
            sp.dma_start(tab[:, :, :], tables).then_inc(tables_in, 16)
            sources = {"dn": w_dn, "abo": w_abo, "swo": w_swo}

            def load_pairs(src, w0, u0, k, first, last):
                with sp.Fori(first, last) as i:
                    for c in range(2):
                        sp.wait_ge(lo_ready, i * 2 + (u0 + c - 1))
                        sp.dma_start(raw[:, (u0 + c) % 2, 0:k * P],
                                     src[bass.ds(i * 2 + (w0 + c), 1), :, :].rearrange("a p n -> (a p) n")
                                     ).then_inc(landed[(u0 + c) % 2], 16)

            for st in stages:
                if st["kind"] == "gu":
                    load_pairs(w_gu, st["w0"], st["u0"], KD, 0 if st["u0"] else 1, FH)
                elif st["kind"] == "dn":
                    load_pairs(sources[st["weights"]], st["w0"], st["u0"], st["k"], 0, KD // 2)
                elif st["kind"] == "proj" and st["which"] == "swa":
                    load_pairs(w_swa, 0, st["u0"], KD, 0, 5)
                elif st["kind"] == "proj":
                    u0 = st["u0"]
                    load_pairs(w_ab, 0, u0, KD, 0, 2)
                    for n, src in ((4, w_ab[4, :, :]), (5, w_uq[0, :, :]), (6, w_uq[1, :, :]),
                                   (7, w_ukv[0, :, :]), (8, w_ukv[1, :, :])):
                        sp.wait_ge(lo_ready, u0 + n - 1)
                        sp.dma_start(raw[:, (u0 + n) % 2, 0:unit_k[u0 + n] * P], src
                                     ).then_inc(landed[(u0 + n) % 2], 16)
                    load_pairs(w_ab, 5, u0 + 9, KD, 0, 6)
            for d in range(KD):
                sp.wait_ge(final_ready, d + 1)
                sp.dma_start(out[:, d, :], final[:, d, META:T]).then_inc(stored, 16)
            sp.wait_ge(stored, 16 * KD)

        @block.tensor
        def _(pe):
            def product(pair, span, blk, slot, x_hi, x_lo, start, stop):
                wh = w_hi[:, slot, blk * P:(blk + 1) * P]
                wl = w_lo[:, slot, blk * P:(blk + 1) * P]
                for n, (w, x) in enumerate(((wh, x_hi), (wh, x_lo), (wl, x_hi))):
                    for bank, t0 in span.chunks:
                        mm = pe.matmul(pair[:, bank, 0:span.width], w, x[:, t0:t0 + span.width],
                                       start=start and n == 0, stop=stop and n == 2)
                return mm

            def stats_columns(a, span, sq_done):
                pe.wait_ge(summed, sq_done)
                if a >= 2:
                    pe.wait_ge(aux_out, a - 1)
                for j, t0 in enumerate(span.stat_starts):
                    mm = pe.matmul(aux_ps[a % 2][:, 0, j:j + 1], square_sum[:, t0:t0 + P], one_col,
                                   start=True, stop=True)
                mm.then_inc(aux_full, 1)

            def stats_spread(a, span, r):
                pe.wait_ge(rstd_ready, r + 1)
                if a >= 2:
                    pe.wait_ge(aux_out, a - 1)
                for j, t0 in enumerate(span.stat_starts):
                    mm = pe.matmul(span.ps_at(aux_ps[a % 2], t0, P),
                                   rstd[:, j:j + 1].to_broadcast([P, P]), ident, start=True, stop=True)
                mm.then_inc(aux_full, 1)

            def gate_up(st):
                u0, o0, span, norm, s = st["u0"], st["o0"], st["span"], st["norm"], st["stats"]
                first = 0
                if s:
                    for c in range(2):
                        pe.wait_ge(lo_ready, u0 + c + 1)
                        if o0 + c >= 2:
                            pe.wait_ge(tile_out, o0 + c - 1)
                        for k in range(KD):
                            if c == 0:
                                pe.wait_ge(xg_lo_ready, KD * norm + k + 1)
                            mm = product(tiles_ps[(o0 + c) % 2], span, k, (u0 + c) % 2,
                                         xg_hi[:, k, :], xg_lo[:, k, :], k == 0, k == KD - 1)
                            if c == 1 and k == KD // 2:
                                stats_spread(s["a"] + 1, span, s["r"])
                        mm.then_inc(tile_full, 1)
                        if c == 0:
                            if norm == 0:
                                pe.wait_ge(consts_in, 48)
                            stats_columns(s["a"], span, s["sq"])
                    first = 1
                with pe.Fori(first, FH) as f:
                    for c in range(2):
                        pe.wait_ge(lo_ready, f * 2 + (u0 + c + 1))
                        pe.wait_ge(tile_out, f * 2 + (o0 + c - 1))
                        for k in range(KD):
                            mm = product(tiles_ps[(o0 + c) % 2], span, k, (u0 + c) % 2,
                                         xg_hi[:, k, :], xg_lo[:, k, :], k == 0, k == KD - 1)
                        mm.then_inc(tile_full, 1)

            def down(st):
                u0, o0, span, nk = st["u0"], st["o0"], st["span"], st["k"]
                if st["act_lo"]:
                    pe.wait_ge(act_lo_ready, st["act_lo"] - 1)
                else:
                    pe.wait_ge(o_lo, st["o_lo"])
                with pe.Fori(0, KD // 2) as i:
                    for c in range(2):
                        pe.wait_ge(lo_ready, i * 2 + (u0 + c + 1))
                        pe.wait_ge(tile_out, i * 2 + (o0 + c - 1))
                        for k in range(nk):
                            if k == nk - 1 and c == 0 and st["act_lo"]:
                                pe.wait_ge(act_lo_ready, st["act_lo"])
                            mm = product(tiles_ps[(o0 + c) % 2], span, k, (u0 + c) % 2,
                                         act_hi[:, k, :], act_lo[:, k, :], k == 0, k == nk - 1)
                        mm.then_inc(tile_full, 1)

            def auxiliary(jobs, pair=None):
                for what, a, of in jobs:
                    if what == "columns":
                        stats_columns(a, ALL, of)
                    elif what == "spread":
                        stats_spread(a, ALL, of)
                    else:
                        if of.bias is None:
                            pe.wait_ge(tile_out, of.o + 1)
                        else:
                            pe.wait_ge(biased, of.biased)
                        pe.wait_ge(aux_out, a - 1)
                        to = pair or aux_ps[a % 2]
                        if what == "rotate":
                            rot = rot_p if of.kind == "rope_p" else rot_m
                            for bank, t0 in ALL.chunks:
                                mm = pe.matmul(to[:, bank, 0:HALF_T], rot, pre[:, t0:t0 + HALF_T],
                                               start=True, stop=True)
                        else:
                            for j in range(1, 5):
                                pe.transpose(to[:, 0, (j - 1) * P:j * P],
                                             pre[:, TILE_START[j]:TILE_START[j] + P], ident)
                            mm = pe.transpose(to[:, 1, 0:P], pre[:, 0:P], ident)
                        mm.then_inc(aux_full, 1)

            def scores(it):
                q0 = TILE_START[it.i]
                if it.after:
                    plain, rope, value = it.after
                    if plain:
                        pe.wait_ge(tile_out, plain.o + 1)
                        pe.wait_ge(aux_out, plain.jobs[0][1] + 1)
                    pe.wait_ge(rope_done, rope.rope)
                    pe.wait_ge(aux_out, value.jobs[0][1] + 1)
                for c, (x, pair, before) in enumerate(it.sets):
                    slot = scores_ps[pair]
                    if before is not None:
                        pe.wait_ge(exp_done, before + 1)
                    if it.kind == "swa":
                        lo = 0 if it.i > 1 else P
                        for kv in range(2):
                            pe.matmul(slot[:, kv, lo:2 * P + META], sq[it.hd][:, q0:q0 + P],
                                      sk_win[:, kv, it.i - 1, lo:2 * P + META], start=True, stop=True)
                            mm = pe.matmul(slot[:, kv, lo:2 * P], ident_bf,
                                           window_bf if lo == 0 else causal_bf, start=False, stop=True,
                                           skip_group_check=True)
                    else:
                        for bank, k0, kn in it.chunks:
                            diagonal = k0 + kn == it.width
                            cols = slot[:, bank, 0:kn]
                            if it.kind == "diff":
                                mm = pe.matmul(cols, dq[it.hd][:, q0:q0 + P], dk[it.hd][c][:, k0:k0 + kn],
                                               start=True, stop=True)
                            else:
                                pe.matmul(cols, mqn[it.hd][:, q0:q0 + P], mkn[it.hd][:, k0:k0 + kn],
                                          start=True, stop=False)
                                mm = pe.matmul(cols, mqr[it.hd // 2][:, q0:q0 + P],
                                               kr[0][it.hd % 2][:, k0:k0 + kn], start=False, stop=True)
                            if diagonal:
                                mm = pe.matmul(slot[:, bank, kn - P:kn], ident_bf, causal_bf,
                                               start=False, stop=True, skip_group_check=True)
                    mm.then_inc(scores_full, 1)

            turn_free = []

            def turn_probabilities(it, part):
                if part == 0:
                    if it.kind == "diff":
                        pe.wait_ge(mix_ready, it.mix)
                    else:
                        pe.wait_ge(exp_done, it.sets[0][0] + 1)
                if turn_free:
                    pe.wait_ge(*turn_free.pop())
                for place_in_bank, (kv, _, col, _) in enumerate(it.turns[part]):
                    if it.kind == "swa":
                        src = e_win[:, it.m % 2, kv, col:col + P]
                    elif it.kind == "diff":
                        src = mix[:, it.m % 2, col:col + P]
                    else:
                        src = e_buf[it.m % 2][:, 0, col:col + P]
                    mm = pe.transpose(turn_ps[:, place_in_bank * P:(place_in_bank + 1) * P], src, ident)
                mm.then_inc(pt_full, 1)
                turn_free.append((pt_out, it.t0 + part + 1))

            def values(it):
                pe.wait_ge(pt_out, it.t_end)
                if it.p == 0 and it.g:
                    pe.wait_ge(o_taken, it.g)
                pt = (pt_swa if it.kind == "swa" else pt_ab)[:, it.m % 2, :]
                for kv in range(2 if it.kind == "swa" else 1):
                    blocks = [b for b in it.blocks if b[0] == kv]
                    for m, (_, pos, _, kt) in enumerate(blocks):
                        if it.kind == "swa":
                            to = value_ps[:, it.p * P + SD * kv:it.p * P + SD * (kv + 1)]
                            v = sv[:, kt, SD * kv:SD * (kv + 1)]
                        else:
                            to = value_ps[:, it.p * P:(it.p + 1) * P]
                            v = (dv if it.kind == "diff" else mv)[:, kt, it.hd * P:(it.hd + 1) * P]
                        mm = pe.matmul(to, pt[:, pos * P:(pos + 1) * P], v, start=m == 0,
                                       stop=m == len(blocks) - 1)
                mm.then_inc(pv_done, 1)

            def turn_output(it):
                if it.kind == "diff":
                    pe.wait_ge(o_ready, it.g - 4)
                else:
                    pe.wait_ge(o_taken, it.g + 1)
                pe.wait_ge(*turn_free.pop())
                for b in range(4):
                    mm = pe.transpose(turn_ps[:, b * P:(b + 1) * P], o_nat[:, b * P:(b + 1) * P], ident)
                mm.then_inc(o_turned, 1)
                turn_free.append((o_lo, it.g + 1))

            def beat(steps):
                if "output" in steps:
                    turn_output(steps["output"])
                if "scores" in steps:
                    scores(steps["scores"])
                turn = steps.get("turn")
                if turn:
                    turn_probabilities(turn, 0)
                if "values" in steps:
                    values(steps["values"])
                if turn and len(turn.turns) > 1:
                    turn_probabilities(turn, 1)

            def projections(st):
                s, beats = st["stats"], iter(st["beats"])
                n = 0
                for at, its_tiles in enumerate(st["units"]):
                    u = st["u0"] + at
                    pe.wait_ge(lo_ready, u + 1)
                    blk = 0
                    for t in its_tiles:
                        if t.beats is None:
                            pe.wait_ge(tile_out, t.o - 1)
                            pair = tiles_ps[t.o % 2]
                        else:
                            pe.wait_ge(tile_out, t.o)
                            if n and st["flat"][n - 1].beats is not None:
                                pe.wait_ge(aux_out, st["flat"][n - 1].jobs[-1][1] + 1)
                            pair = tiles_ps[0]
                        if t.src == "x":
                            src_hi, src_lo, k0 = xg_hi, xg_lo, 0
                        else:
                            src_hi, src_lo, k0 = act_hi, act_lo, 0 if t.src == "cq" else 2
                            pe.wait_ge(low_lo_ready, k0 + 2)
                        for k in range(t.k):
                            if n == 0:
                                pe.wait_ge(xg_lo_ready, KD * st["norm"] + k + 1)
                            mm = product(pair, ALL, blk, u % 2, src_hi[:, k0 + k, :],
                                         src_lo[:, k0 + k, :], k == 0, k == t.k - 1)
                            blk += 1
                            if k == (t.k - 1) // 2:
                                if n == 1:
                                    stats_spread(s["a"] + 1, ALL, s["r"])
                                if n and st["flat"][n - 1].beats is None:
                                    auxiliary(st["flat"][n - 1].jobs)
                            if t.beats and k + 1 in t.beats[0]:
                                beat(next(beats))
                        mm.then_inc(tile_full, 1)
                        if n == 0:
                            stats_columns(s["a"], ALL, s["sq"])
                        if t.beats:
                            if t.beats[1][0]:
                                beat(next(beats))
                            auxiliary(t.jobs, tiles_ps[0])
                            if t.beats[1][1]:
                                beat(next(beats))
                        n += 1
                for steps in beats:
                    beat(steps)

            for st in stages:
                if st["kind"] == "gu":
                    gate_up(st)
                elif st["kind"] == "dn":
                    down(st)
                elif st["kind"] == "proj":
                    projections(st)
                else:
                    s = st["stats"]
                    stats_columns(s["a"], OUT, s["sq"])
                    stats_spread(s["a"] + 1, OUT, s["r"])

        @block.scalar
        def _(act):
            def split_hi(u, k, i=0):
                act.wait_ge(landed[u % 2], i * 16 + landed_count(u))
                if u >= 2:
                    act.wait_ge(tile_full, i * 2 + (unit_last[u - 2] + 1))
                act.activation(w_hi[:, u % 2, 0:k * P], raw[:, u % 2, 0:k * P], ACT.Copy
                               ).then_inc(hi_ready, 1)

            def residual_hi(norm, d, span):
                row = h[:, bass.ds(d, 1), span.first:T].rearrange("p a n -> p (a n)")
                act.activation(xg_hi[:, bass.ds(d, 1), span.first:T].rearrange("p a n -> p (a n)"), row,
                               ACT.Copy, scale=par[:, bass.ds(d + norm * KD, 1)]).then_inc(xg_hi_ready, 1)

            split_hi(0, KD)
            act.wait_ge(params_in, 16)
            for d in range(KD):
                act.wait_ge(h_in[d // 2], 16)
                residual_hi(0, d, ALL)
                act.activation(first_squares[d][:, :], h[:, d, :], ACT.Square).then_inc(squared, 1)
            split_hi(1, KD)
            act.wait_ge(lam_ready, 1)
            act.activation(lam[:, 2:4], lam[:, 0:2], ACT.Exp).then_inc(lam_exp, 1)

            def gate_up(st):
                u0, o0, f0 = st["u0"], st["o0"], st["f0"]
                span = st["span"]

                def feature(f, i, ks):
                    split_hi(u0 + 2, ks[0], i)
                    act.wait_ge(tile_out, i * 2 + (o0 + 1))
                    act.activation(s_buf[:, span.first:T], g_buf[:, span.first:T], ACT.Silu
                                   ).then_inc(silu_ready, 1)
                    split_hi(u0 + 3, ks[1], i)
                    act.wait_ge(gated, i + (f0 + 1))
                    act.nop()
                    act.activation(act_hi[:, bass.ds(f, 1), span.first:T].rearrange("p a n -> p (a n)"),
                                   p_buf[:, span.first:T], ACT.Copy).then_inc(act_hi_ready, 1)

                with act.Fori(0, FH - 1) as f:
                    feature(f, f, (KD, KD))
                feature(FH - 1, FH - 1, (FH, FH))

            def down(st):
                u0, o0, span = st["u0"], st["o0"], st["span"]

                def pair(i, ks):
                    for c in range(2):
                        if ks:
                            split_hi(u0 + c + 2, ks[c], i)
                        if st["last"] and st["norm"] < NORMS - 1:
                            act.wait_ge(tile_out, i * 2 + (o0 + c + 1))
                            act.nop()
                            residual_hi(st["norm"], i * 2 + c, span)

                with act.Fori(0, KD // 2 - 1) as i:
                    pair(i, (st["k"], st["k"]))
                pair(KD // 2 - 1, unit_k[u0 + KD:u0 + KD + 2])

            def exponentials(it):
                for c, (x, pair, _) in enumerate(it.sets):
                    slot = scores_ps[pair]
                    act.wait_ge(max_ready, x + 1)
                    if it.kind == "diff":
                        if it.before[1].kind == "diff":
                            act.wait_ge(mix_ready, it.before[1].mix)
                        else:
                            act.wait_ge(pt_full, it.before[1].t_end)
                    elif it.before[2]:
                        act.wait_ge(pt_full, it.before[2].t_end)
                    if it.kind == "swa":
                        lo = 0 if it.i > 1 else P
                        for kv in range(2):
                            k = 2 * it.p + kv
                            ex = act.activation(e_win[:, it.m % 2, kv, lo:2 * P + META],
                                                slot[:, kv, lo:2 * P + META], ACT.Exp,
                                                bias=neg_max[:, it.g % 2, k:k + 1], scale=it.scale,
                                                accum_out=row_sum[:, it.g % 2, k:k + 1])
                    else:
                        k = 2 * it.p + c
                        e = e_buf[c if it.kind == "diff" else it.m % 2][:, 0, :]
                        if len(it.chunks) == 1:
                            dst, src = e[:, 0:it.width], slot[:, 0, 0:it.width]
                        else:
                            dst = e[:, 0:it.width].rearrange("p (c n) -> p c n", c=2)
                            src = slot[:, :, 0:HALF_T]
                        ex = act.activation(dst, src, ACT.Exp, bias=neg_max[:, it.g % 2, k:k + 1],
                                            scale=it.scale, accum_out=row_sum[:, it.g % 2, k:k + 1])
                    ex.then_inc(exp_done, 1)
                if it.kind == "swa" and it.last:
                    act.wait_ge(sink_sum, it.hd + 1)
                    act.activation(sink_e[:, :], sink_s[:, :], ACT.Exp).then_inc(sink_exp, 1)

            def copy_probabilities(it, part):
                pt = (pt_swa if it.kind == "swa" else pt_ab)[:, it.m % 2, :]
                if part == 0 and it.before[2]:
                    act.wait_ge(pv_done, it.before[2].n + 1)
                act.wait_ge(pt_full, it.t0 + part + 1)
                pos, nb = it.turns[part][0][1], len(it.turns[part])
                act.activation(pt[:, pos * P:(pos + nb) * P], turn_ps[:, 0:nb * P], ACT.Copy
                               ).then_inc(pt_out, 1)

            def output_hi(it):
                act.wait_ge(o_turned, it.g + 1)
                src = turn_ps
                if it.i == 0:
                    k0 = 0 if it.kind == "diff" else 4
                    dst = act_hi[:, k0:k0 + 4, 0:META]
                    src = turn_ps.rearrange("p (f q) -> p f q", q=P)[:, :, 0:META]
                else:
                    dst = act_hi[:, it.hd + (4 if it.kind == "mla" else 0), META:T]
                if it.kind == "diff":
                    act.activation(dst, src, ACT.Copy, scale=gain_sub[:, 0:1]).then_inc(o_hi, 1)
                else:
                    act.activation(dst, src, ACT.Copy).then_inc(o_hi, 1)

            def beat(steps):
                if "output" in steps:
                    output_hi(steps["output"])
                turn = steps.get("turn")
                if turn:
                    copy_probabilities(turn, 0)
                if "scores" in steps:
                    exponentials(steps["scores"])
                if turn and len(turn.turns) > 1:
                    copy_probabilities(turn, 1)

            def projections(st):
                beats = iter(st["beats"])
                for at, its_tiles in enumerate(st["units"]):
                    u = st["u0"] + at
                    for _ in (its_tiles[0].beats or [()])[0]:
                        beat(next(beats))
                    split_hi(u + 2, unit_k[u + 2])
                    for t in its_tiles:
                        if t.kind == "low_rank":
                            act.wait_ge(tile_out, t.o + 1)
                            col = (C_QN, C_QN + 1, C_KVN, C_KVN + 1)[t.index]
                            act.activation(act_hi[:, t.index, :], craw[:, t.index, :], ACT.Copy,
                                           scale=par[:, col:col + 1]).then_inc(low_hi_ready, 1)
                            act.wait_ge(summed, t.sq - 1)
                            act.activation(square[:, :], craw[:, t.index, :], ACT.Square
                                           ).then_inc(squared, 1)
                        if t.beats:
                            for there in t.beats[1]:
                                if there:
                                    beat(next(beats))
                for steps in beats:
                    beat(steps)

            for st in stages:
                if st["kind"] == "gu":
                    gate_up(st)
                elif st["kind"] == "dn":
                    down(st)
                elif st["kind"] == "proj":
                    projections(st)

        @block.vector
        def _(dve):
            steps = [0]

            def step(ins):
                steps[0] += 1
                ins.then_inc(vec_step, 1)
                dve.wait_ge(vec_step, steps[0])

            def split_lo(u, k, i=0):
                dve.wait_ge(hi_ready, i * 2 + (u + 1))
                dve.tensor_tensor(w_lo[:, u % 2, 0:k * P], raw[:, u % 2, 0:k * P],
                                  w_hi[:, u % 2, 0:k * P], ALU.subtract).then_inc(lo_ready, 1)

            def residual_lo(norm, d, span):
                dve.wait_ge(xg_hi_ready, d + (norm * KD + 1))
                cols = slice(span.first, T)
                dve.scalar_tensor_tensor(
                    out=xg_lo[:, bass.ds(d, 1), cols].rearrange("p a n -> p (a n)"),
                    in0=h[:, bass.ds(d, 1), cols].rearrange("p a n -> p (a n)"),
                    scalar=par[:, bass.ds(d + norm * KD, 1)],
                    in1=xg_hi[:, bass.ds(d, 1), cols].rearrange("p a n -> p (a n)"),
                    op0=ALU.mult, op1=ALU.subtract).then_inc(xg_lo_ready, 1)

            def residual_square(sq0, d, span):
                row = h[:, bass.ds(d, 1), span.first:T].rearrange("p a n -> p (a n)")
                dve.wait_ge(summed, d + sq0)
                dve.tensor_tensor(square[:, span.first:T], row, row, ALU.mult).then_inc(squared, 1)

            def stats_mean(a, span, n_features):
                dve.wait_ge(aux_full, a + 1)
                n = len(span.stat_starts)
                dve.tensor_scalar(mean_sq[:, 0:n], aux_ps[a % 2][:, 0, 0:n], 1.0 / n_features, EPS,
                                  ALU.mult, ALU.add).then_inc(aux_out, 1)

            def stats_take(a, span, dst):
                dve.wait_ge(aux_full, a + 1)
                dve.tensor_copy(span.sb(dst[:, :]), span.ps(aux_ps[a % 2])).then_inc(aux_out, 1)
                dve.wait_ge(aux_out, a + 1)

            split_lo(0, KD)
            dve.wait_ge(params_in, 16)
            for d in range(KD):
                dve.wait_ge(h_in[d // 2], 16)
                residual_lo(0, d, ALL)
                if d:
                    dve.wait_ge(squared, d + 1)
                    so_far = first_squares[0] if d == 1 else square_sum
                    if d > 1:
                        dve.wait_ge(summed, d - 1)
                    dve.tensor_tensor(square_sum[:, :], so_far[:, :], first_squares[d][:, :], ALU.add
                                      ).then_inc(summed, 2 if d == KD - 1 else 1)
            split_lo(1, KD)
            dve.wait_ge(consts_in, 48)
            for n in range(2):
                step(dve.tensor_tensor(lam_prod[:, :], rows[:, 128 * n:128 * n + 64],
                                       rows[:, 128 * n + 64:128 * n + 128], ALU.mult))
                ins = dve.tensor_reduce(lam[:, n:n + 1], lam_prod[:, :], AX.X, ALU.add)
                if n == 0:
                    step(ins)
            ins.then_inc(lam_ready, 1)
            dve.wait_ge(lam_exp, 1)
            step(dve.tensor_tensor(lam[:, 4:5], lam[:, 3:4], lam[:, 2:3], ALU.subtract))
            step(dve.tensor_scalar(lam[:, 5:6], lam[:, 4:5], LAMBDA_INIT, None, ALU.subtract))
            step(dve.tensor_scalar(gain_sub[:, :], par[:, C_SUBLN:C_SUBLN + 1], 1.0 - LAMBDA_INIT, None,
                                   ALU.mult))
            step(dve.tensor_scalar(neg_sink[:, :], rows[:, 256:256 + SH], -1.0, None, ALU.mult))

            def gate_up(st):
                u0, o0, f0, span, s = st["u0"], st["o0"], st["f0"], st["span"], st["stats"]
                cols = slice(span.first, T)
                if s:
                    stats_mean(s["a"], span, D)
                    stats_take(s["a"] + 1, span, rbc)

                def feature(f, i, ks):
                    pair = [tiles_ps[(o0 + c) % 2] for c in range(2)]
                    dve.wait_ge(tile_full, i * 2 + (o0 + 1))
                    dve.tensor_tensor(span.sb(g_buf[:, :]), span.ps(pair[0]), span.sb(rbc[:, :]), ALU.mult
                                      ).then_inc(tile_out, 1)
                    split_lo(u0 + 2, ks[0], i)
                    dve.wait_ge(tile_full, i * 2 + (o0 + 2))
                    dve.tensor_tensor(span.sb(u_buf[:, :]), span.ps(pair[1]), span.sb(rbc[:, :]), ALU.mult
                                      ).then_inc(tile_out, 1)
                    dve.wait_ge(silu_ready, i + (f0 + 1))
                    dve.wait_ge(tile_out, i * 2 + (o0 + 2))
                    dve.tensor_tensor(p_buf[:, cols], s_buf[:, cols], u_buf[:, cols], ALU.mult
                                      ).then_inc(gated, 1)
                    split_lo(u0 + 3, ks[1], i)
                    dve.wait_ge(act_hi_ready, i + (f0 + 1))
                    dve.tensor_tensor(act_lo[:, bass.ds(f, 1), cols].rearrange("p a n -> p (a n)"),
                                      p_buf[:, cols],
                                      act_hi[:, bass.ds(f, 1), cols].rearrange("p a n -> p (a n)"),
                                      ALU.subtract).then_inc(act_lo_ready, 1)

                with dve.Fori(0, FH - 1) as f:
                    feature(f, f, (KD, KD))
                feature(FH - 1, FH - 1, (FH, FH))

            def down(st):
                u0, o0, span = st["u0"], st["o0"], st["span"]

                def pair(i, ks):
                    for c in range(2):
                        d = i * 2 + c
                        row = span.sb(h[:, bass.ds(d, 1), :].rearrange("p a n -> p (a n)"))
                        ps = span.ps(tiles_ps[(o0 + c) % 2])
                        dve.wait_ge(tile_full, i * 2 + (o0 + c + 1))
                        if st["weights"] == "dn":
                            ins = dve.scalar_tensor_tensor(out=row, in0=ps, scalar=0.5, in1=row,
                                                           op0=ALU.mult, op1=ALU.add)
                        elif st["bias"]:
                            ins = dve.scalar_tensor_tensor(out=row, in0=ps, scalar=par[:, bass.ds(d + C_BOUT, 1)],
                                                           in1=row, op0=ALU.add, op1=ALU.add)
                        else:
                            ins = dve.tensor_tensor(row, ps, row, ALU.add)
                        ins.then_inc(tile_out, 1)
                        if st["last"]:
                            dve.wait_ge(tile_out, i * 2 + (o0 + c + 1))
                            residual_square(st["sq0"], d, span)
                        if ks:
                            split_lo(u0 + c + 2, ks[c], i)
                        if st["last"] and st["norm"] < NORMS - 1:
                            residual_lo(st["norm"], d, span)

                if st["act_lo"] is None:
                    dve.wait_ge(lo_ready, u0 + 2)
                with dve.Fori(0, KD // 2 - 1) as i:
                    pair(i, (st["k"], st["k"]))
                pair(KD // 2 - 1, unit_k[u0 + KD:u0 + KD + 2])

            def auxiliary(jobs, pair=None):
                for what, a, of in jobs:
                    src = pair or aux_ps[a % 2]
                    if what == "columns":
                        stats_mean(a, ALL, 256)
                    elif what == "spread":
                        stats_take(a, ALL, rbc_q if of == stats_of_ab + 1 else rbc_kv)
                    elif what == "rotate":
                        cos, sin = (cos_p, sin_p) if of.kind == "rope_p" else (cos_m, sin_m)
                        dst = dest[of.dst][of.index]
                        if of.dst in ("dk", "kr", "sk"):
                            dve.wait_ge(zeroed, ZEROED["swa" if of.dst == "sk" else "late"
                                                       if of.dst == "dk" and of.index > 1 else "ab"])
                        dve.wait_ge(tile_out, of.o + 1)
                        step(dve.tensor_tensor(turned[:, :], pre[:, :], cos, ALU.mult))
                        dve.wait_ge(aux_full, a + 1)
                        dve.tensor_tensor(ALL.sb(pre[:, :]), ALL.ps(src), ALL.sb(sin), ALU.mult
                                          ).then_inc(aux_out, 1)
                        dve.wait_ge(aux_out, a + 1)
                        if of.dst in ("dk", "kr"):
                            dve.tensor_tensor(dst[0][0:64, :], pre[0:64, :], turned[0:64, :], ALU.add)
                            dve.tensor_tensor(dst[1][64:P, :], pre[64:P, :], turned[64:P, :], ALU.add
                                              ).then_inc(rope_done, 1)
                        elif of.dst == "sk":
                            step(dve.tensor_tensor(dst[:, :], pre[:, :], turned[:, :], ALU.add))
                            for kv in range(2):
                                half = slice(64 * kv, 64 * (kv + 1))
                                dve.tensor_copy(sk_win[half, kv, :, 2 * P:2 * P + META],
                                                dst[half, 0:META].unsqueeze(1).to_broadcast([64, 4, META]))
                                for i in range(1, 5):
                                    lo = 0 if i > 1 else P
                                    k0 = TILE_START[i] - P + lo
                                    cp = dve.tensor_copy(sk_win[half, kv, i - 1, lo:2 * P],
                                                         dst[half, k0:k0 + 2 * P - lo])
                            cp.then_inc(rope_done, 1)
                        else:
                            dve.tensor_tensor(dst[:, :], pre[:, :], turned[:, :], ALU.add
                                              ).then_inc(rope_done, 1)
                    else:
                        dst = dest[of.dst]
                        dve.wait_ge(zeroed, ZEROED["swa" if of.dst == "sv" else "ab"])
                        cols = slice(of.index * P, (of.index + 1) * P)
                        dve.wait_ge(aux_full, a + 1)
                        dve.tensor_copy(dst[0:META, 0, cols], src[0:META, 1, 0:P])
                        dve.tensor_copy(dst[:, 1:5, cols],
                                        src[:, 0, :].rearrange("p (j n) -> p j n", j=4)
                                        ).then_inc(aux_out, 1)

            def maxima(it):
                for c, (x, pair, _) in enumerate(it.sets):
                    slot = scores_ps[pair]
                    dve.wait_ge(scores_full, x + 1)
                    if it.kind == "swa":
                        lo = 0 if it.i > 1 else P
                        k = slice(2 * it.p, 2 * it.p + 2)
                        step(dve.tensor_reduce(row_max[:, it.g % 2, k], slot[:, :, lo:2 * P + META],
                                               AX.X, ALU.max))
                        dve.scalar_tensor_tensor(out=neg_max[:, it.g % 2, k], in0=row_max[:, it.g % 2, k],
                                                 scalar=-it.scale,
                                                 in1=neg_sink[:, 2 * it.hd:2 * it.hd + 2],
                                                 op0=ALU.mult, op1=ALU.min).then_inc(max_ready, 1)
                    else:
                        k = 2 * it.p + c
                        src, axis = ((slot[:, 0, 0:it.width], AX.X) if len(it.chunks) == 1 else
                                     (slot[:, :, 0:HALF_T], AX.XY))
                        step(dve.tensor_reduce(row_max[:, it.g % 2, k:k + 1], src, axis, ALU.max))
                        dve.tensor_scalar(neg_max[:, it.g % 2, k:k + 1], row_max[:, it.g % 2, k:k + 1],
                                          -it.scale, None, ALU.mult).then_inc(max_ready, 1)
                if it.kind == "swa" and it.last:
                    dve.wait_ge(max_ready, it.sets[0][0] + 1)
                    two = rows[:, 256 + 2 * it.hd:258 + 2 * it.hd].unsqueeze(1).to_broadcast([P, 4, 2])
                    dve.tensor_tensor(sink_s[:, :].rearrange("p (i v) -> p i v", v=2),
                                      neg_max[:, it.g % 2, :].rearrange("p (i v) -> p i v", v=2),
                                      two, ALU.add).then_inc(sink_sum, 1)

            def combine(it):
                k = 2 * it.p
                dve.wait_ge(exp_done, it.sets[1][0] + 1)
                step(dve.reciprocal(coef[:, 0:1], row_sum[:, it.g % 2, k + 1:k + 2]))
                step(dve.scalar_tensor_tensor(out=coef[:, 1:2], in0=row_sum[:, it.g % 2, k:k + 1],
                                              scalar=lam[:, 5:6], in1=coef[:, 0:1],
                                              op0=ALU.mult, op1=ALU.mult))
                if it.before[2].kind == "diff":
                    dve.wait_ge(pt_full, it.before[2].t_end)
                w = it.width
                dve.scalar_tensor_tensor(out=mix[:, it.m % 2, 0:w], in0=e_buf[1][:, 0, 0:w],
                                         scalar=coef[:, 1:2], in1=e_buf[0][:, 0, 0:w],
                                         op0=ALU.mult, op1=ALU.add).then_inc(mix_ready, 1)

            def normalise(it):
                sums = row_sum[:, it.g % 2, :]
                if it.kind == "swa":
                    dve.wait_ge(sink_exp, it.hd + 1)
                    step(dve.tensor_tensor(inv_sum[:, 0, :], sums, sink_e[:, :], ALU.add))
                    step(dve.reciprocal(inv_sum[:, 1, :], inv_sum[:, 0, :]))
                    n, d = 8, SD
                else:
                    n, d = 4, P
                    dve.wait_ge(exp_done, it.sets[-1][0] + 1)
                    step(dve.reciprocal(inv_sum[:, 1, 0:4], sums[:, 0:8:2]))
                o = o_nat[:, :].rearrange("p (f d) -> p f d", d=d)
                dve.wait_ge(pv_done, it.n + 1)
                dve.tensor_tensor(o, value_ps.rearrange("p (f d) -> p f d", d=d),
                                  inv_sum[:, 1, 0:n].unsqueeze(2).to_broadcast([P, n, d]), ALU.mult
                                  ).then_inc(o_taken, 1)
                if it.kind != "diff":
                    return
                dve.wait_ge(o_taken, it.g + 1)
                step(dve.tensor_tensor(o_sq[:, :], o_nat[:, :], o_nat[:, :], ALU.mult))
                step(dve.tensor_reduce(o_ms[:, :], o_sq[:, :].rearrange("p (f d) -> p f d", d=P),
                                       AX.X, ALU.add))
                dve.tensor_scalar(o_mse[:, :], o_ms[:, :], 1.0 / DV, DIFF_EPS, ALU.mult, ALU.add
                                  ).then_inc(o_mean, 1)

            def output_norm(it):
                dve.wait_ge(o_rstd_ready, it.g - 4)
                o = o_nat[:, :].rearrange("p (f d) -> p f d", d=P)
                dve.tensor_tensor(o, o, o_rstd[:, :].unsqueeze(2).to_broadcast([P, 4, P]), ALU.mult
                                  ).then_inc(o_ready, 1)

            def output_lo(it):
                dve.wait_ge(o_hi, it.g + 1)
                src = turn_ps
                if it.i == 0:
                    k0 = 0 if it.kind == "diff" else 4
                    hi, lo = (x[:, k0:k0 + 4, 0:META] for x in (act_hi, act_lo))
                    src = turn_ps.rearrange("p (f q) -> p f q", q=P)[:, :, 0:META]
                else:
                    hi, lo = (x[:, it.hd + (4 if it.kind == "mla" else 0), META:T] for x in (act_hi, act_lo))
                if it.kind == "diff":
                    dve.scalar_tensor_tensor(out=lo, in0=src, scalar=gain_sub[:, 0:1], in1=hi,
                                             op0=ALU.mult, op1=ALU.subtract).then_inc(o_lo, 1)
                else:
                    dve.tensor_tensor(lo, src, hi, ALU.subtract).then_inc(o_lo, 1)

            def beat(steps):
                for name, does in (("output", output_lo), ("combine", combine), ("output_norm", output_norm),
                                   ("scores", maxima), ("normalise", normalise)):
                    if name in steps:
                        does(steps[name])

            def projections(st):
                turned_last = 0
                s, beats = st["stats"], iter(st["beats"])
                stats_mean(s["a"], ALL, D)
                stats_take(s["a"] + 1, ALL, rbc)
                for at, its_tiles in enumerate(st["units"]):
                    u = st["u0"] + at
                    for t in its_tiles:
                        for _ in (t.beats or [()])[0]:
                            beat(next(beats))
                        pair = tiles_ps[t.o % 2 if t.beats is None else 0]
                        dve.wait_ge(tile_full, t.o + 1)
                        if t.kind in ("rope_p", "rope_m", "value"):
                            dst = pre
                        else:
                            dst = dest[t.dst][t.index]
                        r = rbcs[t.src]
                        if dst is pre and turned_last:
                            dve.wait_ge(rope_done, turned_last)
                        dve.tensor_tensor(ALL.sb(dst[:, :]), ALL.ps(pair), ALL.sb(r[:, :]), ALU.mult
                                          ).then_inc(tile_out, 1)
                        if t.bias is not None:
                            col = C_BQKV + t.bias
                            dve.wait_ge(tile_out, t.o + 1)
                            dve.tensor_scalar(pre[:, :], pre[:, :], par[:, col:col + 1], None, ALU.add
                                              ).then_inc(biased, 1)
                            dve.wait_ge(biased, t.biased)
                        if t.beats and t.beats[1][0]:
                            beat(next(beats))
                        if t is its_tiles[-1] and t.beats is None:
                            split_lo(u + 2, unit_k[u + 2])
                        if t.kind == "low_rank":
                            col = (C_QN, C_QN + 1, C_KVN, C_KVN + 1)[t.index]
                            dve.wait_ge(low_hi_ready, t.low)
                            dve.scalar_tensor_tensor(out=act_lo[:, t.index, :], in0=craw[:, t.index, :],
                                                     scalar=par[:, col:col + 1], in1=act_hi[:, t.index, :],
                                                     op0=ALU.mult, op1=ALU.subtract).then_inc(low_lo_ready, 1)
                        auxiliary(t.jobs, None if t.beats is None else tiles_ps[0])
                        if t.kind in ("rope_p", "rope_m"):
                            turned_last = t.rope
                        if t.beats and t.beats[1][1]:
                            beat(next(beats))
                for steps in beats:
                    beat(steps)

            dve.wait_ge(tables_in, 16)
            for st in stages:
                if st["kind"] == "gu":
                    gate_up(st)
                elif st["kind"] == "dn":
                    down(st)
                elif st["kind"] == "proj":
                    projections(st)
                else:
                    s = st["stats"]
                    stats_mean(s["a"], OUT, D)
                    stats_take(s["a"] + 1, OUT, rbc)
                    for d in range(KD):
                        col = (NORMS - 1) * KD + d
                        dve.scalar_tensor_tensor(out=final[:, d, META:T], in0=h[:, d, META:T],
                                                 scalar=par[:, col:col + 1], in1=rbc[:, META:T],
                                                 op0=ALU.mult, op1=ALU.mult).then_inc(final_ready, 1)

        @block.gpsimd
        def _(pool):
            cleared, zero_steps = [0], [0]

            def sum_squares(sq0, n, span, taken):
                if taken:
                    pool.wait_ge(aux_full, taken)
                cleared[0] += 1
                pool.memset(square_sum[:, :], 0.0).then_inc(sum_clear, 1)
                pool.wait_ge(sum_clear, cleared[0])
                cols = slice(span.first, T)
                with pool.Fori(0, n) as d:
                    pool.wait_ge(squared, d + (sq0 + 1))
                    pool.tensor_tensor(square_sum[:, cols], square_sum[:, cols], square[:, cols], ALU.add
                                       ).then_inc(summed, 1)
                    pool.wait_ge(summed, d + (sq0 + 1))

            def rstd_of(a, r, n):
                pool.wait_ge(aux_out, a + 1)
                pool.tensor_tensor(rstd[:, 0:n], mean_sq[:, 0:n], minus_half.to_broadcast([P, n]), ALU.pow
                                   ).then_inc(rstd_ready, 1)

            def zeros(*rows):
                for row in rows:
                    zero_steps[0] += 1
                    pool.memset(row, 0.0).then_inc(zeroed, 1)
                    pool.wait_ge(zeroed, zero_steps[0])

            def halves(*pairs):
                return [row for a, b in pairs for row in (a[64:P, :], b[0:64, :])]

            def split_lo(u, k):
                pool.wait_ge(lo_ready, u)
                pool.wait_ge(hi_ready, u + 1)
                pool.tensor_tensor(w_lo[:, u % 2, 0:k * P], raw[:, u % 2, 0:k * P],
                                   w_hi[:, u % 2, 0:k * P], ALU.subtract).then_inc(lo_ready, 1)
                pool.wait_ge(lo_ready, u + 1)

            def beat(steps):
                if "scores" in steps and steps["scores"].kind == "diff" and steps["scores"].n == MLA_ITEMS:
                    pool.wait_ge(scores_full, steps["scores"].sets[0][0])
                    zeros(*halves(*dk[2:4]))
                if "output_norm" in steps:
                    it = steps["output_norm"]
                    pool.wait_ge(o_mean, it.g - 4)
                    pool.tensor_tensor(o_rstd[:, :], o_mse[:, :], minus_half.to_broadcast([P, 4]), ALU.pow
                                       ).then_inc(o_rstd_ready, 1)
                    pool.wait_ge(o_rstd_ready, it.g - 4)

            def projections(st, taken):
                beats = iter(st["beats"])
                for at, its_tiles in enumerate(st["units"]):
                    u = st["u0"] + at
                    for t in its_tiles:
                        if t.kind == "low_rank" and t.index % 2 == 1:
                            sum_squares(t.sq - 2, 2, ALL, taken)
                            a = t.jobs[-1][1]
                            rstd_of(a, stats_of_ab + 1 + t.index // 2, 6)
                            taken = a + 1
                        if t.beats:
                            for _ in t.beats[0]:
                                beat(next(beats))
                            split_lo(u + 2, unit_k[u + 2])
                            for there in t.beats[1]:
                                if there:
                                    beat(next(beats))
                for steps in beats:
                    beat(steps)
                return taken

            pool.wait_ge(consts_in, 48)
            taken = 0
            for st in stages:
                s = st.get("stats")
                if s:
                    rstd_of(s["a"], s["r"], len(s["span"].stat_starts))
                    taken = s["a"] + 1
                if st["kind"] == "proj":
                    pool.wait_ge(act_lo_ready, st["act_lo"])
                    if st["which"] == "ab":
                        zeros(dv[:, 0, :], mv[:, 0, :], *halves(kr[0], *dk[0:2]))
                    else:
                        zeros(sv[:, 0, :], e_win[:, :, :, 2 * P + META:3 * P],
                              sk_win[64:P, 0, :, :], sk_win[0:64, 1, :, :])
                if st["kind"] == "dn" and st["last"]:
                    if not st["act_lo"]:
                        pool.wait_ge(o_lo, st["o_lo"])
                    sum_squares(st["sq0"], KD, st["span"], taken)
                elif st["kind"] == "proj":
                    taken = projections(st, taken)
    return nc


def shape_constants():
    f = np.float32
    rot = np.zeros((2, P, P), f)
    for n, half, width in ((0, 8, 16), (1, 32, 64)):
        for start in (0, 64):
            for j in range(half):
                rot[n, start + half + j, start + j] = -1.0
                rot[n, start + j, start + half + j] = 1.0
    con = np.concatenate([np.eye(P, dtype=f), rot[0], rot[1], np.ones((P, 1), f),
                          np.full((P, 1), -0.5, f)], axis=1)
    tab = np.zeros((P, 4, T), f)
    pos = np.arange(T, dtype=f)
    for n, width in ((0, 16), (1, 64)):
        inv = np.power(f(500000.0), -np.arange(0, width, 2, dtype=f) / f(width)).astype(f)
        ang = pos[:, None] * inv[None, :]
        cos, sin = np.cos(ang).astype(f), np.sin(ang).astype(f)
        for p in range(P):
            d = p % 64
            if d < width:
                tab[p, 2 * n] = cos[:, d % (width // 2)]
                tab[p, 2 * n + 1] = sin[:, d % (width // 2)]
            else:
                tab[p, 2 * n] = 1.0
    q, k = np.arange(P)[:, None], np.arange(P)[None, :]
    masks = np.concatenate([np.eye(P), np.where(k > q, 0.0, MASKED), np.where(k <= q, 0.0, MASKED)],
                           axis=1).astype(mybir.dt.np(BF16))
    return con, tab, masks


def kernel(**inputs):
    from concourse import bacc
    from concourse.bass_utils import run_bass_kernel_spmd

    x = {k: np.asarray(v) for k, v in inputs.items()}

    def units(w):
        kk, m = w.shape
        return np.ascontiguousarray(w.reshape(kk // P, P, m // P, P).transpose(2, 1, 0, 3)
                                    ).reshape(m // P, P, kk)

    def cols(v):
        return v.reshape(-1, P).T

    gu, dn = [], []
    for layer, name in ((0, "ffn1"), (0, "ffn2"), (1, "ffn1"), (1, "ffn2")):
        pair = np.stack([units(x[name + "_w_gate"][layer]), units(x[name + "_w_up"][layer])], axis=1)
        gu.append(pair.reshape(2 * pair.shape[0], P, D))
        down = x[name + "_w_down"][layer]
        dn += [units(down[half * FH * P:(half + 1) * FH * P]) for half in range(2)]
    w = x["ab_w_in"][0]
    cut = np.split(w, [512, 1024, 1536, 1792, 2048], axis=1)
    by_head = [part[:, P * i:P * (i + 1)] for i in range(4) for part in cut[0:3]]
    w_ab = np.concatenate([cut[3], cut[4], cut[5], cut[5]] + by_head, axis=1)
    uq = x["mla_w_uq"][0].reshape(256, MH, 192)
    uq = np.concatenate([uq[:, :, :128].reshape(256, 512), uq[:, :, 128:].reshape(256, 256)], axis=1)
    ukv = x["mla_w_ukv"][0].reshape(256, MH, 256)
    ukv = np.concatenate([ukv[:, :, :128].reshape(256, 512), ukv[:, :, 128:].reshape(256, 512)], axis=1)

    def grouped(w, n):
        t = units(w)
        return np.ascontiguousarray(t.reshape(len(t) // n, n, P, 256).transpose(0, 2, 1, 3)
                                    ).reshape(len(t) // n, P, n * 256)

    def by_pair(v):
        lead = v.shape[:-1]
        q = v[..., :1024].reshape(*lead, 2, 8, 64)
        q = np.swapaxes(q, -3, -2).reshape(*lead, 1024)
        return np.concatenate([v[..., 1024:], q], axis=-1)

    swo = np.swapaxes(x["swa_w_out"][0].reshape(2, 8, 64, D), 0, 1).reshape(D, D)
    norms = [x["ffn1_norm"][0], x["mix_norm"][0], x["ffn2_norm"][0], x["ffn1_norm"][1],
             x["mix_norm"][1], x["ffn2_norm"][1], x["final_norm"]]
    params = np.concatenate([cols(v) for v in norms] +
                            [cols(x["mla_q_norm"][0]), cols(x["mla_kv_norm"][0]), cols(x["diff_subln"][0]),
                             cols(by_pair(x["swa_b_qkv"][0])), cols(x["swa_b_out"][0])], axis=1)
    row = np.concatenate([x["diff_lambda_q1"][0], x["diff_lambda_k1"][0], x["diff_lambda_q2"][0],
                          x["diff_lambda_k2"][0], x["swa_sinks"][0].reshape(2, 8).T.reshape(-1)])
    tokens = np.concatenate([x["meta_tokens"], x["x"][0]], axis=0)
    con, tab, masks = shape_constants()
    arrays = {
        "x_t": tokens.T.reshape(KD, P, T).transpose(1, 0, 2),
        "w_gu": np.concatenate(gu), "w_dn": np.concatenate(dn), "w_ab": units(w_ab),
        "w_uq": grouped(uq, 3), "w_ukv": grouped(ukv, 4), "w_abo": units(x["ab_w_out"][0]),
        "w_swa": units(by_pair(x["swa_w_qkv"][0])), "w_swo": units(swo),
        "params": params, "row": row, "consts": con, "tables": tab, "masks": masks,
    }
    nc = bacc.Bacc("TRN2", target_bir_lowering=False, num_devices=1)
    args = {}
    for name, a in arrays.items():
        arrays[name] = np.ascontiguousarray(a)
        args[name] = nc.dram_tensor(name, a.shape, mybir.dt.from_np(a.dtype), kind="ExternalInput").ap()
    args["out"] = nc.dram_tensor("out", (P, KD, SEQ), F32, kind="ExternalOutput").ap()
    build(nc, **args)
    got = run_bass_kernel_spmd(nc, [arrays], core_ids=[0]).results[0]["out"]
    return np.ascontiguousarray(got.transpose(2, 1, 0).reshape(1, SEQ, D))
```

```python
from contextlib import ExitStack

import numpy as np

import concourse.bass as bass
from concourse import mybir

F32 = mybir.dt.float32
F32R = mybir.dt.float32r
BF16 = mybir.dt.bfloat16
ACT = mybir.ActivationFunctionType
ALU = mybir.AluOpType
AX = mybir.AxisListType

P = 128
D = 1024
KD = D // P
META = 16
SEQ = 512
T = META + SEQ
HALF_T = T // 2
F = 2816
FH = F // P // 2
EPS = 1e-6
DIFF_EPS = 1e-5
LAMBDA_INIT = 0.8 - 0.6 * 1.0
DH, DV = 4, 128
MH = 4
MLA_ITEMS = 5 * MH
SH, SD = 16, 64
KT_MAX = FH
SPREAD_AT = 2
LATE = KD - 2
POOL_FINAL = 2
ZEROED = {"ab": 8, "late": 12, "swa": 16}
TILE_START = [0] + [META + P * i for i in range(4)]
MASKED = -1e30

NORMS = 7
C_QN, C_KVN, C_SUBLN = NORMS * KD, NORMS * KD + 2, NORMS * KD + 4
C_BQKV = C_SUBLN + 1
C_BOUT = C_BQKV + 10
N_PARAMS = C_BOUT + KD
N_ROW = 4 * 64 + SH


class Span:

    def __init__(self, first):
        self.first, self.n = first, T - first
        if first == 0:
            self.width, self.chunks = HALF_T, [(0, 0), (1, HALF_T)]
            self.stat_starts = [c * HALF_T + s for c in range(2) for s in (0, P, HALF_T - P)]
        else:
            self.width, self.chunks = SEQ, [(0, first)]
            self.stat_starts = [first + P * s for s in range(SEQ // P)]

    def ps(self, pair):
        return pair[:, 0:len(self.chunks), 0:self.width]

    def sb(self, row):
        return row[:, self.first:T].rearrange("p (c n) -> p c n", c=len(self.chunks))

    def ps_at(self, pair, token, n):
        bank = (token - self.first) // self.width
        col = (token - self.first) % self.width
        return pair[:, bank, col:col + n]


ALL = Span(0)
OUT = Span(META)


class Tile:

    def __init__(self, kind, dst, index=0, k=KD, src="x", bias=None):
        self.kind, self.dst, self.index = kind, dst, index
        self.k, self.src, self.bias = k, src, bias
        self.jobs = []
        self.beats = None
        self.aux_ahead = False

    def slot(self):
        return self.o % 2 if self.beats is None or self.aux_ahead else 0


class Item:

    def __init__(self, kind, i, hd, g, p):
        self.kind, self.i, self.hd, self.g, self.p = kind, i, hd, g, p
        self.scale = (192 if kind == "mla" else 64) ** -0.5
        if kind == "swa":
            self.blocks = [(kv, 3 * kv + b, b * P, kt) for kv in range(2)
                           for b, kt in ((0, i - 1), (1, i), (2, 0)) if b or i > 1]
            per = len(self.blocks) // 2
        else:
            self.blocks = [(0, j, TILE_START[j], j) for j in range(i + 1)]
            per = 4
        self.turns = [self.blocks[j:j + per] for j in range(0, len(self.blocks), per)]
        self.width = META + P * i if i else P
        self.chunks = ([(0, 0, self.width)] if self.width <= 512 else
                       [(c, c * HALF_T, HALF_T) for c in range(2)])


def ab_units():
    units = [[Tile("low_rank", "craw", i)] for i in range(4)]
    units += [[Tile("rope_m", "kr")]]
    qn = [Tile("plain", "mqn", i, 2, "cq") for i in range(4)]
    qr = [Tile("rope_m", "mqr", i, 2, "cq") for i in range(2)]
    uq = [qn[0], qr[0], qn[1], qn[2], qr[1], qn[3]]
    ukv = [t for i in range(4) for t in (Tile("plain", "mkn", i, 2, "ckv"), Tile("value", "mv", i, 2, "ckv"))]
    units += [uq[0:3], uq[3:6], ukv[0:4], ukv[4:8]]
    for i in range(4):
        units += [[Tile("rope_s", "dq", i)], [Tile("rope_s", "dk", i)], [Tile("value", "dv", i)]]
    for n, unit in enumerate(units[9:]):
        if unit[0].kind == "value":
            unit[0].beats = [(4,) if n < 9 else (), (True, True)]
        else:
            unit[0].beats = [(2, 5) if 0 < n < 9 else (6,) if n == 0 else (4,), (True, False)]
    return units


def swa_units():
    units = [[Tile("rope_p", "sk", bias=0)], [Tile("value", "sv", bias=1)]]
    units += [[Tile("rope_p", "sq", i, bias=2 + i)] for i in range(8)]
    for n, unit in enumerate(units[2:]):
        unit[0].beats = [(), (False, False)] if n == 0 else [(4, 6) if n == 1 else (2, 5), (True, True)]
    units[2][0].aux_ahead = True
    return units


def attention_items(which):
    items = []
    if which == "ab":
        for kind, g0 in (("mla", 0), ("diff", 5)):
            items += [Item(kind, i, hd, g0 + hd, i - 1) for hd in range(4) for i in range(1, 5)]
            items += [Item(kind, 0, hd, g0 + 4, hd) for hd in range(4)]
    else:
        items += [Item("swa", i, j, 10 + j, i - 1) for j in range(8) for i in range(1, 5)]
    return items


def beats_of(items):
    beats = [{} for _ in range(len(items) + 6)]
    for it in items:
        diff = it.kind == "diff"
        turn = it.m + (2 if diff else 1)
        steps = dict(scores=it.m, turn=turn, values=turn + 1)
        if diff:
            steps["combine"] = it.m + 1
        if it.last:
            steps["normalise"] = turn + 1
            if diff:
                steps["output_norm"] = turn + 2
                steps["late_output"] = turn + 3
            else:
                steps["output"] = turn + 2
        for step, beat in steps.items():
            assert step not in beats[beat]
            beats[beat][step] = it
    while not beats[-1]:
        beats.pop()
    return beats


def plan():
    unit_k, unit_last, stages = [], [], []
    at = dict(o=0, a=0, r=0, sq=KD, norm=0, rope=0, bias=0, low=0, swap=0)
    att = dict(n=0, x=0, t=0, mix=0, g=0)

    def units(kind, ks, tiles_each, **more):
        st = dict(kind=kind, u0=len(unit_k), o0=at["o"], **more)
        for k, n in zip(ks, tiles_each):
            at["o"] += n
            unit_k.append(k)
            unit_last.append(at["o"] - 1)
        stages.append(st)
        return st

    def stats(span, sq):
        s = dict(span=span, a=at["a"], r=at["r"], sq=sq)
        at["a"] += 2
        at["r"] += 1
        return s

    def splits_h(st):
        at["norm"] += 1
        st.update(last=True, norm=at["norm"], sq0=at["sq"])
        at["sq"] += KD

    def ffn(n, span):
        at["gated"] = 2 * FH * (n + 1)
        for half in range(2):
            first = half == 0
            units("gu", [KD] * 2 * FH, [1] * 2 * FH, w0=(2 * n + half) * 2 * FH, f0=(2 * n + half) * FH,
                  norm=at["norm"], span=span, stats=stats(span, at["sq"]) if first else None)
            st = units("dn", [FH] * KD, [1] * KD, k=FH, span=span, scale=0.5, weights="dn",
                       w0=(2 * n + half) * KD, act_lo=(2 * n + half + 1) * FH, last=False)
        splits_h(st)

    def projections(which, its_units):
        st = units("proj", [sum(t.k for t in ts) for ts in its_units], [len(ts) for ts in its_units],
                   which=which, units=its_units,
                   pool_from=5 if which == "ab" else 2, norm=at["norm"], act_lo=at["gated"], stats=stats(ALL, at["sq"]))
        flat = [t for ts in its_units for t in ts]
        for n, t in enumerate(flat):
            t.o = st["o0"] + n
            if t.bias is not None:
                at["bias"] += 1
                t.biased = at["bias"]
        for n, t in enumerate(flat):
            before = flat[n - 2] if n > 1 else None
            if before and before.kind == "low_rank" and before.index % 2:
                t.jobs.append(("spread", at["a"], at["r"]))
                at["a"] += 1
                at["r"] += 1
            if t.kind == "low_rank":
                at["sq"] += 1
                at["low"] += 1
                t.sq, t.low = at["sq"], at["low"]
                if t.index % 2:
                    t.jobs.append(("columns", at["a"], at["sq"]))
                    at["a"] += 1
            elif t.kind.startswith("rope"):
                at["rope"] += 1
                t.rope = at["rope"]
                if t.kind != "rope_s":
                    t.jobs.append(("rotate", at["a"], t))
                    at["a"] += 1
                else:
                    at["swap"] += 1
                    t.swap = at["swap"]
            elif t.kind == "value":
                t.jobs.append(("turn", at["a"], t))
                at["a"] += 1
        tiles = {(t.dst, t.index): t for t in flat}
        items = attention_items(which)
        in_pair = [None, None]
        for m, it in enumerate(items):
            it.m, it.n = m, att["n"]
            att["n"] += 1
            pairs = (0, 1) if it.kind == "diff" else (m % 2,)
            it.sets = []
            for pair in pairs:
                it.sets.append((att["x"], pair, in_pair[pair]))
                in_pair[pair] = att["x"]
                att["x"] += 1
            it.t0 = att["t"]
            att["t"] += len(it.turns)
            it.t_end = att["t"]
            if it.kind == "diff":
                att["mix"] += 1
                it.mix = att["mix"]
            it.last = m + 1 == len(items) or items[m + 1].g != it.g
            it.after = None
            if it.kind == "mla" and m == 0:
                it.after = tiles["mv", 3], tiles["mqr", 1], tiles["mv", 3]
            elif it.kind == "diff" and it.i == 1:
                it.after = None, tiles["dk", it.hd], tiles["dv", it.hd]
            elif it.kind == "swa" and it.i == 1:
                it.after = None, tiles["sq", it.hd], tiles["sv", 0]
            it.before = [items[m - k] if m >= k else None for k in range(5)]
        att["g"] = items[-1].g + 1
        st.update(flat=flat, items=items, beats=beats_of(items), groups=att["g"])

    def out_projection(weights, span, bias):
        st = units("dn", [KD] * KD, [1] * KD, k=KD, span=span, scale=1.0, bias=bias,
                   weights=weights, w0=0, act_lo=None, o_lo=att["g"])
        splits_h(st)

    def begin_ahead(blocks, upper=()):
        proj, dn = stages[-2:]
        c = dn["o0"] % 2
        dn.update(early={c: [k for a, b in blocks for k in a], 1 - c: [k for a, b in blocks for k in b]},
                  early_o_lo=proj["groups"] - (5 if proj["which"] == "ab" else 1))
        m0 = len(proj["beats"]) - len(blocks)
        proj["after_beat"] = {m0 + n: [(c, k, False) for k in a] + [(1 - c, k, False) for k in b]
                              for n, (a, b) in enumerate(blocks)}
        proj["after_beat"][m0 + len(blocks) - 2] += [(i, k, True) for i in (c, 1 - c) for k in upper]
        dn["upper"] = upper
        proj["out"] = dn
        proj["last_set"] = proj["items"][-1].sets[-1][0]

    ffn(0, ALL)
    projections("ab", ab_units())
    out_projection("abo", ALL, False)
    begin_ahead([([4], []), ([5], []), ([6], []), ([7], []), ([], [4]), ([], [5]), ([], [6]),
                 ([], [7]), ([], [])], upper=(0, 1, 2, 3))
    ffn(1, ALL)
    ffn(2, ALL)
    projections("swa", swa_units())
    out_projection("swo", OUT, True)
    begin_ahead([([0, 1], []), ([2, 3], []), ([], [0, 1]), ([], [2, 3, 4, 5, 6])])
    ffn(3, OUT)
    stages.append(dict(kind="final", stats=stats(OUT, at["sq"])))
    return stages, unit_k, unit_last


def build(nc, x_t, w_gu, w_dn, w_ab, w_uq, w_ukv, w_abo, w_swa, w_swo, params, row, consts,
          tables, masks, out):
    stages, unit_k, unit_last = plan()
    ab, swa = (st for st in stages if st["kind"] == "proj")
    stats_of_ab = ab["stats"]["r"]
    ctx = ExitStack()
    with ctx:
        cursor = [(nc.sbuf_base + 31) // 32 * 32]

        def place(name, shape, dt, at=None):
            n = int(np.prod(shape[1:])) * (2 if dt == BF16 else 4)
            offset = cursor[0] if at is None else at
            if at is None:
                cursor[0] = (offset + n + 31) // 32 * 32
            return nc.alloc_sbuf_tensor_at(name, shape, dt, offset=offset)

        ROW = T * 4
        h = place("h", [P, KD, T], F32)
        at_xg = cursor[0]
        xg_hi = place("xg_hi", [P, KD, T], F32R)
        xg_lo = place("xg_lo", [P, KD, T], F32R)
        at_act = cursor[0]
        act_hi = place("act_hi", [P, FH, T], F32R)
        act_lo = place("act_lo", [P, FH, T], F32R)
        raw = place("raw", [P, 2, KT_MAX * P], F32)
        w_hi = place("w_hi", [P, 2, KT_MAX * P], F32R)
        w_lo = place("w_lo", [P, 2, KT_MAX * P], F32R)
        at_square = cursor[0]
        square = place("square", [P, T], F32)
        at_square_sum = cursor[0]
        square_sum = place("square_sum", [P, T], F32)
        rbc = place("rbc", [P, T], F32)
        con = place("con", [P, 3 * P + 2], F32)
        mask_bf = place("mask_bf", [P, 3 * P], BF16)
        par = place("par", [P, N_PARAMS], F32)
        sinks = place("sinks", [P, SH], F32)
        at_swapped = cursor[0]
        swapped = place("swapped", [P, T], F32)
        lambdas = place("lambdas", [P, 256], F32, at_swapped)
        lam_prod = place("lam_prod", [P, 64], F32, at_swapped + 1024)
        mean_sq = place("mean_sq", [P, 8], F32)
        rstd = place("rstd", [P, 8], F32)
        lam = place("lam", [P, 8], F32)
        gain_sub = place("gain_sub", [P, 1], F32)
        neg_max = place("neg_max", [P, 2, 8], F32)
        row_max = place("row_max", [P, 2, 8], F32)
        row_sum = place("row_sum", [P, 2, 8], F32)
        inv_sum = place("inv_sum", [P, 2, 8], F32)
        coef = place("coef", [P, 2], F32)
        sink_s = place("sink_s", [P, 8], F32)
        sink_e = place("sink_e", [P, 8], F32)
        neg_sink = place("neg_sink", [P, 16], F32)
        o_ms = place("o_ms", [P, 4], F32)
        o_mse = place("o_mse", [P, 4], F32)
        o_rstd = place("o_rstd", [P, 4], F32)

        ident, rot_p, rot_m = con[:, 0:P], con[:, P:2 * P], con[:, 2 * P:3 * P]
        one_col, minus_half = con[:, 3 * P:3 * P + 1], con[:, 3 * P + 1:3 * P + 2]
        ident_bf, window_bf = mask_bf[:, 0:P], mask_bf[:, P:3 * P]
        causal_bf = mask_bf[:, 2 * P:3 * P]

        tab = place("tab", [P, 4, T], F32)
        pt_ab = place("pt_ab", [P, 2, 5 * P], F32, cursor[0] - 2 * ROW)
        cursor[0] += 2 * 5 * P * 4 - 2 * ROW
        cos_p, sin_p, cos_m, sin_m = (tab[:, i, :] for i in range(4))

        at_att = cursor[0]
        g_buf = place("g_buf", [P, T], F32, at_att)
        u_buf = place("u_buf", [P, T], F32, at_att + ROW)
        s_buf = place("s_buf", [P, T], F32, at_att + 2 * ROW)
        p_buf = place("p_buf", [P, T], F32, at_att + 3 * ROW)
        final = place("final", [P, KD, T], F32, at_att + 4 * ROW)
        att = [place(f"att{i}", [P, T], F32, at_att + i * ROW) for i in range(19)]
        mqn, mqr, mkn = att[9:13], att[13:15], att[15:19]
        kr = [(att[3], att[8])]
        first_squares = att[4:12]
        dq = att[0:3] + att[15:16]
        dk = [(att[i], att[i + 1]) for i in (4, 6, 9, 11)]
        dv = place("dv", [P, 5, 512], F32, at_att + 19 * ROW)
        mv = place("mv", [P, 5, 512], F32, at_att + 19 * ROW + 10240)
        sq = place("sq", [P, 8, T], F32, at_att)
        sq = [sq[:, i, :] for i in range(8)]
        sk = [place("sk", [P, T], F32, at_att + 8 * ROW)]
        sv = place("sv", [P, 5, P], F32, at_att + 9 * ROW)
        pt_swa = place("pt_swa", [P, 2, 6 * P], F32, at_att + 9 * ROW + 5 * P * 4)
        e_win = place("e_win", [P, 2, 2, 3 * P], F32, at_att + 9 * ROW + 17 * P * 4)
        sk_win = place("sk_win", [P, 2, 4, 2 * P + META], F32, at_att + 9 * ROW + 29 * P * 4)
        dest = {"dq": dq, "dk": dk, "kr": kr, "mqn": mqn, "mqr": mqr, "mkn": mkn, "dv": dv,
                "mv": mv, "sq": sq, "sk": sk, "sv": sv}
        craw = place("craw", [P, 4, T], F32, at_act + 4 * ROW)
        pre = place("pre", [P, T], F32, at_act + 8 * ROW)
        turned = place("turned", [P, T], F32, at_act + 9 * ROW)
        rbc_q = place("rbc_q", [P, T], F32, at_act + 10 * ROW)
        rbc_kv = place("rbc_kv", [P, T], F32, at_act + (FH + 8) * ROW)
        rbcs = {"x": rbc, "cq": rbc_q, "ckv": rbc_kv}
        dest["craw"] = [craw[:, i, :] for i in range(4)]
        e_buf = place("e_buf", [P, T], F32, at_act + 10 * ROW), \
            place("e_buf1", [P, T], F32, at_act + (FH + 8) * ROW)
        e_diff = (att[13:15], att[16:18])
        mix = place("mix", [P, 2, T], F32, at_act + (FH + 9) * ROW)
        o_sq = place("o_sq", [P, 512], F32, at_square)
        o_nat = place("o_nat", [P, 512], F32, at_square_sum)

        tiles_ps = [ctx.enter_context(nc.psum_tensor(f"tile{i}", [P, 2, 512], F32)) for i in range(2)]
        aux_ps = [ctx.enter_context(nc.psum_tensor(f"aux{i}", [P, 2, 512], F32)) for i in range(2)]

        scores_ps = [tiles_ps[1], aux_ps[0]]
        turn_ps, value_ps = aux_ps[1][:, 0, :], aux_ps[1][:, 1, :]

        def output_ps(it):
            return turn_ps if it.kind == "diff" else value_ps

        all_items = [it for st in stages if st["kind"] == "proj" for it in st["items"]]

        def sem(name):
            return ctx.enter_context(nc.semaphore(name))

        consts_in, tables_in, params_in = sem("consts_in"), sem("tables_in"), sem("params_in")
        h_in = [sem(f"h_in{i}") for i in range(4)]
        landed = [sem("landed0"), sem("landed1")]
        hi_ready = sem("hi_ready")
        lo_ready = sem("lo_ready")
        tile_full = sem("tile_full")
        tile_out = sem("tile_out")
        aux_full = sem("aux_full")
        aux_out = sem("aux_out")
        xg_hi_ready = sem("xg_hi_ready")
        xg_lo_ready = sem("xg_lo_ready")
        squared = sem("squared")
        sum_clear = sem("sum_clear")
        summed = sem("summed")
        rstd_ready = sem("rstd_ready")
        silu_ready = sem("silu_ready")
        gated = sem("gated")
        act_hi_ready = sem("act_hi_ready")
        act_lo_ready = sem("act_lo_ready")
        lam_ready = sem("lam_ready")
        lam_exp = sem("lam_exp")
        low_hi_ready = sem("low_hi_ready")
        low_lo_ready = sem("low_lo_ready")
        biased = sem("biased")
        windows_ready = sem("windows_ready")
        swap_in = sem("swap_in")
        rope_done = sem("rope_done")
        scores_full = sem("scores_full")
        max_ready = sem("max_ready")
        exp_done = sem("exp_done")
        mix_ready = sem("mix_ready")
        pt_full = sem("pt_full")
        pt_out = sem("pt_out")
        pv_done = sem("pv_done")
        sink_sum = sem("sink_sum")
        sink_exp = sem("sink_exp")
        o_squared = sem("o_squared")
        o_mean = sem("o_mean")
        o_rstd_ready = sem("o_rstd_ready")
        o_taken = sem("o_taken")
        o_ready = sem("o_ready")
        o_turned = sem("o_turned")
        o_hi = sem("o_hi")
        o_lo = sem("o_lo")
        final_gained = sem("final_gained")
        final_ready = sem("final_ready")
        final_pool = sem("final_pool")
        zeroed = sem("zeroed")
        stored = sem("stored")
        vec_step = sem("vec_step")

        def landed_count(u):
            return 16 * (u // 2 + 1)

        block = ctx.enter_context(nc.Block())

        @block.sync
        def _(sp):
            sp.dma_start(raw[:, 0, 0:KD * P], w_gu[0, :, :]).then_inc(landed[0], 16)
            sp.dma_start(par[:, :], params).then_inc(params_in, 16)
            for part in range(4):
                ks = slice(part * KD // 4, (part + 1) * KD // 4)
                sp.dma_start(h[:, ks, :], x_t[:, ks, :]).then_inc(h_in[part], 16)
            sp.dma_start(raw[:, 1, 0:KD * P], w_gu[1, :, :]).then_inc(landed[1], 16)
            sp.dma_start(con[:, :], consts).then_inc(consts_in, 16)
            sp.dma_start(mask_bf[:, :], masks).then_inc(consts_in, 16)
            sp.dma_start(lambdas[:, :], row[0:256].partition_broadcast(P)).then_inc(consts_in, 16)
            sp.dma_start(sinks[:, :], row[256:N_ROW].partition_broadcast(P)).then_inc(consts_in, 16)
            sp.dma_start(tab[:, :, :], tables).then_inc(tables_in, 16)
            sources = {"dn": w_dn, "abo": w_abo, "swo": w_swo}

            def load_pairs(src, w0, u0, k, first, last):
                with sp.Fori(first, last) as i:
                    for c in range(2):
                        sp.wait_ge(lo_ready, i * 2 + (u0 + c - 1))
                        sp.dma_start(raw[:, (u0 + c) % 2, 0:k * P],
                                     src[bass.ds(i * 2 + (w0 + c), 1), :, :].rearrange("a p n -> (a p) n")
                                     ).then_inc(landed[(u0 + c) % 2], 16)

            def swap(t):
                sp.wait_ge(tile_out, t.o + 1)
                if t.rope > 1:
                    sp.wait_ge(rope_done, t.rope - 1)
                for start in (0, 64):
                    for to, frm in ((0, 8), (8, 0)):
                        sp.dma_start(swapped[start + to:start + to + 8, :], pre[start + frm:start + frm + 8, :]
                                     ).then_inc(swap_in, 16)

            for st in stages:
                if st["kind"] == "gu":
                    load_pairs(w_gu, st["w0"], st["u0"], KD, 0 if st["u0"] else 1, FH)
                elif st["kind"] == "dn":
                    load_pairs(sources[st["weights"]], st["w0"], st["u0"], st["k"],
                               0 if st["act_lo"] else 2, KD // 2)
                elif st["kind"] == "proj":
                    u0 = st["u0"]
                    if st["which"] == "ab":
                        loads = ([w_ab[n, :, :] for n in range(5)] + [w_uq[n, :, :] for n in range(2)] +
                                 [w_ukv[n, :, :] for n in range(2)] + [w_ab[n, :, :] for n in range(5, 17)])
                    else:
                        loads = [w_swa[n, :, :] for n in range(10)]
                    loads += [sources[st["out"]["weights"]][n, :, :] for n in range(4)]
                    loaded = 0
                    for n, its_tiles in enumerate(st["units"] + [None]):
                        while loaded < min(n + 4, len(loads)):
                            u = u0 + loaded
                            sp.wait_ge(lo_ready, u - 1)
                            sp.dma_start(raw[:, u % 2, 0:unit_k[u] * P], loads[loaded]).then_inc(landed[u % 2], 16)
                            loaded += 1
                        for t in its_tiles or []:
                            if t.kind == "rope_s":
                                swap(t)
            for d in (2, 3, 0, 4, 5, 1, 6, 7):
                if d < POOL_FINAL:
                    sp.wait_ge(final_pool, d + 1)
                else:
                    sp.wait_ge(final_ready, d - POOL_FINAL + 1)
                sp.dma_start(out[:, d, :], final[:, d, META:T]).then_inc(stored, 16)
            sp.wait_ge(stored, 16 * KD)

        @block.tensor
        def _(pe):
            def product(pair, span, blk, slot, x_hi, x_lo, start, stop, chunks=None):
                wh = w_hi[:, slot, blk * P:(blk + 1) * P]
                wl = w_lo[:, slot, blk * P:(blk + 1) * P]
                for n, (w, x) in enumerate(((wh, x_hi), (wh, x_lo), (wl, x_hi))):
                    for bank, t0 in chunks or span.chunks:
                        mm = pe.matmul(pair[:, bank, 0:span.width], w, x[:, t0:t0 + span.width],
                                       start=start and n == 0, stop=stop and n == 2)
                return mm

            def stats_columns(a, span, sq_done):
                pe.wait_ge(summed, sq_done)
                if a >= 2:
                    pe.wait_ge(aux_out, a - 1)
                for j, t0 in enumerate(span.stat_starts):
                    mm = pe.matmul(aux_ps[a % 2][:, 0, j:j + 1], square_sum[:, t0:t0 + P], one_col,
                                   start=True, stop=True)
                mm.then_inc(aux_full, 1)

            def stats_spread(a, span, r):
                pe.wait_ge(rstd_ready, r + 1)
                if a >= 2:
                    pe.wait_ge(aux_out, a - 1)
                for j, t0 in enumerate(span.stat_starts):
                    mm = pe.matmul(span.ps_at(aux_ps[a % 2], t0, P),
                                   rstd[:, j:j + 1].to_broadcast([P, P]), ident, start=True, stop=True)
                mm.then_inc(aux_full, 1)

            def gate_up(st):
                u0, o0, span, norm, s = st["u0"], st["o0"], st["span"], st["norm"], st["stats"]
                first = 0
                if s:
                    for c in range(2):
                        pe.wait_ge(lo_ready, u0 + c + 1)
                        if o0 + c >= 2:
                            pe.wait_ge(tile_out, o0 + c - 1)
                        for k in range(KD):
                            if c == 0:
                                pe.wait_ge(xg_lo_ready, KD * norm + k + 1)
                            mm = product(tiles_ps[(o0 + c) % 2], span, k, (u0 + c) % 2,
                                         xg_hi[:, k, :], xg_lo[:, k, :], k == 0, k == KD - 1)
                            if c == 1 and k == SPREAD_AT:
                                stats_spread(s["a"] + 1, span, s["r"])
                        mm.then_inc(tile_full, 1)
                        if c == 0:
                            if norm == 0:
                                pe.wait_ge(consts_in, 64)
                            stats_columns(s["a"], span, s["sq"])
                    first = 1
                with pe.Fori(first, FH) as f:
                    for c in range(2):
                        pe.wait_ge(lo_ready, f * 2 + (u0 + c + 1))
                        pe.wait_ge(tile_out, f * 2 + (o0 + c - 1))
                        for k in range(KD):
                            mm = product(tiles_ps[(o0 + c) % 2], span, k, (u0 + c) % 2,
                                         xg_hi[:, k, :], xg_lo[:, k, :], k == 0, k == KD - 1)
                        mm.then_inc(tile_full, 1)

            def down(st):
                u0, o0, span, nk = st["u0"], st["o0"], st["span"], st["k"]
                if st["act_lo"]:
                    pe.wait_ge(act_lo_ready, st["act_lo"] - 1)
                else:
                    pe.wait_ge(o_lo, st["o_lo"])
                    for c in range(2):
                        rest = [k for k in range(nk) if k not in st["early"][c]]
                        for k in rest:
                            mm = product(tiles_ps[(o0 + c) % 2], span, k, (u0 + c) % 2,
                                         act_hi[:, k, :], act_lo[:, k, :], False, k == rest[-1],
                                         span.chunks[0:1] if k in st["upper"] else None)
                        mm.then_inc(tile_full, 1)
                with pe.Fori(0 if st["act_lo"] else 1, KD // 2) as i:
                    for c in range(2):
                        pe.wait_ge(lo_ready, i * 2 + (u0 + c + 1))
                        pe.wait_ge(tile_out, i * 2 + (o0 + c - 1))
                        for k in range(nk):
                            if k == nk - 1 and c == 0 and st["act_lo"]:
                                pe.wait_ge(act_lo_ready, st["act_lo"])
                            mm = product(tiles_ps[(o0 + c) % 2], span, k, (u0 + c) % 2,
                                         act_hi[:, k, :], act_lo[:, k, :], k == 0, k == nk - 1)
                        mm.then_inc(tile_full, 1)

            def early_blocks(proj, blocks):
                st = proj["out"]
                for c, k, upper in blocks:
                    if upper and k == st["upper"][0]:
                        pe.wait_ge(o_lo, st["o_lo"] - 1)
                    if not upper and k == st["early"][c][0]:
                        pe.wait_ge(lo_ready, st["u0"] + c + 1)
                        pe.wait_ge(o_lo, st["early_o_lo"])
                        if (st["o0"] + c) % 2 == 0:
                            pe.wait_ge(tile_out, st["o0"])
                            if proj["flat"][-1].jobs:
                                pe.wait_ge(aux_out, proj["flat"][-1].jobs[-1][1] + 1)
                        else:
                            pe.wait_ge(exp_done, proj["last_set"] + 1)
                    product(tiles_ps[(st["o0"] + c) % 2], st["span"], k, (st["u0"] + c) % 2,
                            act_hi[:, k, :], act_lo[:, k, :], not upper and k == st["early"][c][0],
                            upper and k == st["upper"][-1], st["span"].chunks[1:2] if upper else None)

            def auxiliary(jobs, pair=None):
                for what, a, of in jobs:
                    if what == "columns":
                        stats_columns(a, ALL, of)
                    elif what == "spread":
                        stats_spread(a, ALL, of)
                    else:
                        if of.bias is None:
                            pe.wait_ge(tile_out, of.o + 1)
                        else:
                            pe.wait_ge(biased, of.biased)
                        pe.wait_ge(aux_out, a - 1)
                        to = pair or aux_ps[a % 2]
                        if what == "rotate":
                            rot = rot_m if of.kind == "rope_m" else rot_p
                            for bank, t0 in ALL.chunks:
                                mm = pe.matmul(to[:, bank, 0:HALF_T], rot, pre[:, t0:t0 + HALF_T],
                                               start=True, stop=True)
                        else:
                            for j in range(1, 5):
                                pe.transpose(to[:, 0, (j - 1) * P:j * P],
                                             pre[:, TILE_START[j]:TILE_START[j] + P], ident)
                            mm = pe.transpose(to[:, 1, 0:P], pre[:, 0:P], ident)
                        mm.then_inc(aux_full, 1)

            def scores(it):
                q0 = TILE_START[it.i]
                if it.after:
                    plain, rope, value = it.after
                    if plain:
                        pe.wait_ge(tile_out, plain.o + 1)
                        pe.wait_ge(aux_out, plain.jobs[0][1] + 1)
                    pe.wait_ge(rope_done, rope.rope)
                    pe.wait_ge(aux_out, value.jobs[0][1] + 1)
                    if it.kind == "swa":
                        pe.wait_ge(windows_ready, 1)
                for c, (x, pair, before) in enumerate(it.sets):
                    slot = scores_ps[pair]
                    if before is not None:
                        pe.wait_ge(exp_done, before + 1)
                    if it.kind == "swa":
                        lo = 0 if it.i > 1 else P
                        for kv in range(2):
                            pe.matmul(slot[:, kv, lo:2 * P + META], sq[it.hd][:, q0:q0 + P],
                                      sk_win[:, kv, it.i - 1, lo:2 * P + META], start=True, stop=True)
                            mm = pe.matmul(slot[:, kv, lo:2 * P], ident_bf,
                                           window_bf if lo == 0 else causal_bf, start=False, stop=True,
                                           skip_group_check=True)
                    else:
                        for bank, k0, kn in it.chunks:
                            diagonal = k0 + kn == it.width
                            cols = slot[:, bank, 0:kn]
                            if it.kind == "diff":
                                mm = pe.matmul(cols, dq[it.hd][:, q0:q0 + P], dk[it.hd][c][:, k0:k0 + kn],
                                               start=True, stop=True)
                            else:
                                pe.matmul(cols, mqn[it.hd][:, q0:q0 + P], mkn[it.hd][:, k0:k0 + kn],
                                          start=True, stop=False)
                                mm = pe.matmul(cols, mqr[it.hd // 2][:, q0:q0 + P],
                                               kr[0][it.hd % 2][:, k0:k0 + kn], start=False, stop=True)
                            if diagonal:
                                mm = pe.matmul(slot[:, bank, kn - P:kn], ident_bf, causal_bf,
                                               start=False, stop=True, skip_group_check=True)
                    mm.then_inc(scores_full, 1)

            turn_free = []

            def turn_probabilities(it, part):
                if part == 0:
                    if it.kind == "diff":
                        pe.wait_ge(mix_ready, it.mix)
                    else:
                        pe.wait_ge(exp_done, it.sets[0][0] + 1)
                if turn_free:
                    pe.wait_ge(*turn_free.pop())
                for place_in_bank, (kv, _, col, _) in enumerate(it.turns[part]):
                    if it.kind == "swa":
                        src = e_win[:, it.m % 2, kv, col:col + P]
                    elif it.kind == "diff":
                        src = mix[:, it.m % 2, col:col + P]
                    else:
                        src = e_buf[it.m % 2][:, col:col + P]
                    mm = pe.transpose(turn_ps[:, place_in_bank * P:(place_in_bank + 1) * P], src, ident)
                mm.then_inc(pt_full, 1)
                turn_free.append((pt_out, it.t0 + part + 1))

            def values(it):
                pe.wait_ge(pt_out, it.t_end)
                if it.p == 0 and it.g:
                    group_before = all_items[it.n - 1]
                    pe.wait_ge(o_taken if group_before.kind == "diff" else o_lo, it.g)
                pt = (pt_swa if it.kind == "swa" else pt_ab)[:, it.m % 2, :]
                for kv in range(2 if it.kind == "swa" else 1):
                    blocks = [b for b in it.blocks if b[0] == kv]
                    for m, (_, pos, _, kt) in enumerate(blocks):
                        if it.kind == "swa":
                            to = value_ps[:, it.p * P + SD * kv:it.p * P + SD * (kv + 1)]
                            v = sv[:, kt, SD * kv:SD * (kv + 1)]
                        else:
                            to = value_ps[:, it.p * P:(it.p + 1) * P]
                            v = (dv if it.kind == "diff" else mv)[:, kt, it.hd * P:(it.hd + 1) * P]
                        mm = pe.matmul(to, pt[:, pos * P:(pos + 1) * P], v, start=m == 0,
                                       stop=m == len(blocks) - 1)
                mm.then_inc(pv_done, 1)

            def turn_output(it):
                if it.kind == "diff":
                    pe.wait_ge(o_ready, it.g - 4)
                    pe.wait_ge(*turn_free.pop())
                else:
                    pe.wait_ge(o_taken, it.g + 1)
                for b in range(4):
                    mm = pe.transpose(output_ps(it)[:, b * P:(b + 1) * P], o_nat[:, b * P:(b + 1) * P], ident)
                mm.then_inc(o_turned, 1)
                if it.kind == "diff":
                    turn_free.append((o_lo, it.g + 1))

            def beat(steps):
                if "output" in steps:
                    turn_output(steps["output"])
                if "scores" in steps:
                    scores(steps["scores"])
                turn = steps.get("turn")
                if turn:
                    turn_probabilities(turn, 0)
                if "values" in steps:
                    values(steps["values"])
                if turn and len(turn.turns) > 1:
                    turn_probabilities(turn, 1)
                if "late_output" in steps:
                    turn_output(steps["late_output"])

            def projections(st):
                s, beats = st["stats"], iter(st["beats"])
                n = 0
                for at, its_tiles in enumerate(st["units"]):
                    u = st["u0"] + at
                    pe.wait_ge(lo_ready, u + 1)
                    blk = 0
                    for t in its_tiles:
                        before = st["flat"][n - 1] if n else None
                        pe.wait_ge(tile_out, t.o if before and before.slot() == t.slot() else t.o - 1)
                        if before and before.beats is not None and before.jobs and not before.aux_ahead:
                            pe.wait_ge(aux_out, before.jobs[-1][1] + 1)
                        pair = tiles_ps[t.slot()]
                        if t.src == "x":
                            src_hi, src_lo, k0 = xg_hi, xg_lo, 0
                        else:
                            src_hi, src_lo, k0 = act_hi, act_lo, 0 if t.src == "cq" else 2
                            pe.wait_ge(low_lo_ready, k0 + 2)
                        for k in range(t.k):
                            if n == 0:
                                pe.wait_ge(xg_lo_ready, KD * st["norm"] + k + 1)
                            mm = product(pair, ALL, blk, u % 2, src_hi[:, k0 + k, :],
                                         src_lo[:, k0 + k, :], k == 0, k == t.k - 1)
                            blk += 1
                            if n == 1 and k == SPREAD_AT:
                                stats_spread(s["a"] + 1, ALL, s["r"])
                            if n and st["flat"][n - 1].aux_ahead and k == 0:
                                auxiliary(st["flat"][n - 1].jobs, aux_ps[1])
                            late = n and (n == 1 or st["flat"][n - 1].kind == "low_rank")
                            if k == (LATE if late else (t.k - 1) // 2):
                                if n and st["flat"][n - 1].beats is None:
                                    auxiliary(st["flat"][n - 1].jobs)
                            if t.beats and k + 1 in t.beats[0]:
                                beat(next(beats))
                        mm.then_inc(tile_full, 1)
                        if n == 0:
                            stats_columns(s["a"], ALL, s["sq"])
                        if t.beats:
                            if t.beats[1][0]:
                                beat(next(beats))
                            if not t.aux_ahead:
                                auxiliary(t.jobs, tiles_ps[0])
                            if t.beats[1][1]:
                                beat(next(beats))
                        n += 1
                left = list(beats)
                for m, steps in enumerate(left, len(st["beats"]) - len(left)):
                    beat(steps)
                    early_blocks(st, st["after_beat"].get(m, []))

            for st in stages:
                if st["kind"] == "gu":
                    gate_up(st)
                elif st["kind"] == "dn":
                    down(st)
                elif st["kind"] == "proj":
                    projections(st)
                else:
                    s = st["stats"]
                    stats_columns(s["a"], OUT, s["sq"])
                    stats_spread(s["a"] + 1, OUT, s["r"])

        @block.scalar
        def _(act):
            def split_hi(u, k, i=0):
                act.wait_ge(landed[u % 2], i * 16 + landed_count(u))
                if u >= 2:
                    act.wait_ge(tile_full, i * 2 + (unit_last[u - 2] + 1))
                act.activation(w_hi[:, u % 2, 0:k * P], raw[:, u % 2, 0:k * P], ACT.Copy
                               ).then_inc(hi_ready, 1)

            def residual_hi(norm, d, span):
                row = h[:, bass.ds(d, 1), span.first:T].rearrange("p a n -> p (a n)")
                act.activation(xg_hi[:, bass.ds(d, 1), span.first:T].rearrange("p a n -> p (a n)"), row,
                               ACT.Copy, scale=par[:, bass.ds(d + norm * KD, 1)]).then_inc(xg_hi_ready, 1)

            split_hi(0, KD)
            act.wait_ge(params_in, 16)
            for d in range(KD):
                act.wait_ge(h_in[d // 2], 16)
                residual_hi(0, d, ALL)
                act.activation(first_squares[d][:, :], h[:, d, :], ACT.Square).then_inc(squared, 1)
            split_hi(1, KD)
            def gate_up(st):
                u0, o0, f0 = st["u0"], st["o0"], st["f0"]
                span = st["span"]

                def feature(f, i, ks):
                    split_hi(u0 + 2, ks[0], i)
                    act.wait_ge(tile_out, i * 2 + (o0 + 1))
                    act.activation(s_buf[:, span.first:T], g_buf[:, span.first:T], ACT.Silu
                                   ).then_inc(silu_ready, 1)
                    split_hi(u0 + 3, ks[1], i)
                    act.wait_ge(gated, i + (f0 + 1))
                    act.nop()
                    act.activation(act_hi[:, bass.ds(f, 1), span.first:T].rearrange("p a n -> p (a n)"),
                                   p_buf[:, span.first:T], ACT.Copy).then_inc(act_hi_ready, 1)

                with act.Fori(0, FH - 1) as f:
                    feature(f, f, (KD, KD))
                feature(FH - 1, FH - 1, (FH, FH))

            def down(st):
                u0, o0, span = st["u0"], st["o0"], st["span"]

                def pair(i, ks):
                    for c in range(2):
                        if ks:
                            split_hi(u0 + c + 2, ks[c], i)
                        if st["last"] and st["norm"] < NORMS - 1:
                            act.wait_ge(tile_out, i * 2 + (o0 + c + 1))
                            act.nop()
                            residual_hi(st["norm"], i * 2 + c, span)
                        elif st["last"]:
                            act.wait_ge(tile_out, i * 2 + (o0 + c + 1))
                            act.nop()
                            row = h[:, bass.ds(i * 2 + c, 1), META:T].rearrange("p a n -> p (a n)")
                            gained = final[:, bass.ds(i * 2 + c, 1), META:T].rearrange("p a n -> p (a n)")
                            act.activation(gained, row, ACT.Copy,
                                           scale=par[:, bass.ds(i * 2 + ((NORMS - 1) * KD + c), 1)]
                                           ).then_inc(final_gained, 1)

                with act.Fori(0, KD // 2 - 1) as i:
                    pair(i, (st["k"], st["k"]))
                pair(KD // 2 - 1, unit_k[u0 + KD:u0 + KD + 2])

            def exponentials(it):
                for c, (x, pair, _) in enumerate(it.sets):
                    slot = scores_ps[pair]
                    act.wait_ge(max_ready, x + 1)
                    if it.kind == "diff":
                        if it.before[2].kind == "diff":
                            act.wait_ge(mix_ready, it.before[2].mix)
                    elif it.before[2]:
                        act.wait_ge(pt_full, it.before[2].t_end)
                    if it.kind == "swa":
                        lo = 0 if it.i > 1 else P
                        for kv in range(2):
                            k = 2 * it.p + kv
                            ex = act.activation(e_win[:, it.m % 2, kv, lo:2 * P + META],
                                                slot[:, kv, lo:2 * P + META], ACT.Exp,
                                                bias=neg_max[:, it.g % 2, k:k + 1], scale=it.scale,
                                                accum_out=row_sum[:, it.g % 2, k:k + 1])
                    else:
                        k = 2 * it.p + c
                        e = (e_diff[it.m % 2][c] if it.kind == "diff" else e_buf[it.m % 2])[:, :]
                        if len(it.chunks) == 1:
                            dst, src = e[:, 0:it.width], slot[:, 0, 0:it.width]
                        else:
                            dst = e[:, 0:it.width].rearrange("p (c n) -> p c n", c=2)
                            src = slot[:, :, 0:HALF_T]
                        ex = act.activation(dst, src, ACT.Exp, bias=neg_max[:, it.g % 2, k:k + 1],
                                            scale=it.scale, accum_out=row_sum[:, it.g % 2, k:k + 1])
                    ex.then_inc(exp_done, 1)
                if it.kind == "swa" and it.last:
                    act.wait_ge(sink_sum, it.hd + 1)
                    act.activation(sink_e[:, :], sink_s[:, :], ACT.Exp).then_inc(sink_exp, 1)

            def take_values(t):
                dst, (_, a, _) = dest[t.dst], t.jobs[0]
                cols = slice(t.index * P, (t.index + 1) * P)
                src = tiles_ps[0]
                act.wait_ge(aux_full, a + 1)
                act.activation(dst[0:META, 0, cols], src[0:META, 1, 0:P], ACT.Copy)
                act.activation(dst[:, 1:5, cols], src[:, 0, :].rearrange("p (j n) -> p j n", j=4),
                               ACT.Copy).then_inc(aux_out, 1)

            def key_windows(t):
                act.wait_ge(rope_done, t.rope)
                act.wait_ge(zeroed, ZEROED["swa"])
                keys = sk[0]
                for kv in range(2):
                    half = slice(64 * kv, 64 * (kv + 1))
                    act.activation(sk_win[half, kv, :, 2 * P:2 * P + META],
                                   keys[half, 0:META].unsqueeze(1).to_broadcast([64, 4, META]), ACT.Copy)
                    for i in range(1, 5):
                        lo = 0 if i > 1 else P
                        k0 = TILE_START[i] - P + lo
                        cp = act.activation(sk_win[half, kv, i - 1, lo:2 * P],
                                            keys[half, k0:k0 + 2 * P - lo], ACT.Copy)
                cp.then_inc(windows_ready, 1)

            def copy_probabilities(it, part):
                pt = (pt_swa if it.kind == "swa" else pt_ab)[:, it.m % 2, :]
                if part == 0 and it.before[2]:
                    act.wait_ge(pv_done, it.before[2].n + 1)
                act.wait_ge(pt_full, it.t0 + part + 1)
                pos, nb = it.turns[part][0][1], len(it.turns[part])
                act.activation(pt[:, pos * P:(pos + nb) * P], turn_ps[:, 0:nb * P], ACT.Copy
                               ).then_inc(pt_out, 1)

            def output_squares(it):
                act.wait_ge(o_taken, it.g + 1)
                for b in range(4):
                    sq_in = o_nat[:, b * P:(b + 1) * P]
                    ms = act.activation(o_sq[:, b * P:(b + 1) * P], sq_in, ACT.Square,
                                        accum_out=o_ms[:, b:b + 1])
                ms.then_inc(o_squared, 1)
                act.wait_ge(o_squared, it.g - 4)
                act.activation(o_mse[:, :], o_ms[:, :], ACT.Copy, scale=1.0 / DV, bias=DIFF_EPS
                               ).then_inc(o_mean, 1)

            def output_hi(it):
                act.wait_ge(o_turned, it.g + 1)
                src = output_ps(it)
                if it.i == 0:
                    k0 = 0 if it.kind == "diff" else 4
                    dst = act_hi[:, k0:k0 + 4, 0:META]
                    src = src.rearrange("p (f q) -> p f q", q=P)[:, :, 0:META]
                else:
                    dst = act_hi[:, it.hd + (4 if it.kind == "mla" else 0), META:T]
                if it.kind == "diff":
                    act.activation(dst, src, ACT.Copy, scale=gain_sub[:, 0:1]).then_inc(o_hi, 1)
                else:
                    act.activation(dst, src, ACT.Copy).then_inc(o_hi, 1)

            def beat(steps):
                if "output" in steps:
                    output_hi(steps["output"])
                turn = steps.get("turn")
                if turn:
                    copy_probabilities(turn, 0)
                if "scores" in steps:
                    exponentials(steps["scores"])
                if turn and len(turn.turns) > 1:
                    copy_probabilities(turn, 1)
                if "late_output" in steps:
                    output_hi(steps["late_output"])
                if "normalise" in steps and steps["normalise"].kind == "diff":
                    output_squares(steps["normalise"])

            def projections(st):
                beats = iter(st["beats"])
                for at, its_tiles in enumerate(st["units"]):
                    u = st["u0"] + at
                    for _ in (its_tiles[0].beats or [()])[0]:
                        beat(next(beats))
                    after = (its_tiles[0].beats or [(), ()])[1]
                    if after and after[0]:
                        beat(next(beats))
                    if its_tiles[0].beats and its_tiles[0].kind == "value":
                        take_values(its_tiles[0])
                    if st["which"] == "ab" and after and after[1]:
                        beat(next(beats))
                    split_hi(u + 2, unit_k[u + 2])
                    if at == 1 and st["which"] == "swa":
                        key_windows(st["flat"][0])
                    for t in its_tiles:
                        if t.kind == "low_rank":
                            act.wait_ge(tile_out, t.o + 1)
                            col = (C_QN, C_QN + 1, C_KVN, C_KVN + 1)[t.index]
                            act.activation(act_hi[:, t.index, :], craw[:, t.index, :], ACT.Copy,
                                           scale=par[:, col:col + 1]).then_inc(low_hi_ready, 1)
                            act.wait_ge(summed, t.sq - 1)
                            act.activation(square[:, :], craw[:, t.index, :], ACT.Square
                                           ).then_inc(squared, 1)
                    if st["which"] == "swa" and after and after[1]:
                        beat(next(beats))
                for steps in beats:
                    beat(steps)

            for st in stages:
                if st["kind"] == "gu":
                    gate_up(st)
                elif st["kind"] == "dn":
                    if st is stages[1]:
                        act.wait_ge(lam_ready, 1)
                        act.activation(lam[:, 2:4], lam[:, 0:2], ACT.Exp).then_inc(lam_exp, 1)
                    down(st)
                elif st["kind"] == "proj":
                    projections(st)
                else:
                    a = st["stats"]["a"] + 1
                    act.wait_ge(aux_full, a + 1)
                    act.activation(rbc[:, META:T], aux_ps[a % 2][:, 0, 0:SEQ], ACT.Copy
                                   ).then_inc(final_gained, 1)

        @block.vector
        def _(dve):
            steps = [0]

            def step(ins):
                steps[0] += 1
                ins.then_inc(vec_step, 1)
                dve.wait_ge(vec_step, steps[0])

            def split_lo(u, k, i=0):
                dve.wait_ge(hi_ready, i * 2 + (u + 1))
                dve.tensor_tensor(w_lo[:, u % 2, 0:k * P], raw[:, u % 2, 0:k * P],
                                  w_hi[:, u % 2, 0:k * P], ALU.subtract).then_inc(lo_ready, 1)

            def residual_lo(norm, d, span):
                dve.wait_ge(xg_hi_ready, d + (norm * KD + 1))
                cols = slice(span.first, T)
                dve.scalar_tensor_tensor(
                    out=xg_lo[:, bass.ds(d, 1), cols].rearrange("p a n -> p (a n)"),
                    in0=h[:, bass.ds(d, 1), cols].rearrange("p a n -> p (a n)"),
                    scalar=par[:, bass.ds(d + norm * KD, 1)],
                    in1=xg_hi[:, bass.ds(d, 1), cols].rearrange("p a n -> p (a n)"),
                    op0=ALU.mult, op1=ALU.subtract).then_inc(xg_lo_ready, 1)

            def residual_square(sq0, d, span):
                row = h[:, bass.ds(d, 1), span.first:T].rearrange("p a n -> p (a n)")
                dve.wait_ge(summed, d + sq0)
                dve.tensor_tensor(square[:, span.first:T], row, row, ALU.mult).then_inc(squared, 1)

            def stats_mean(a, span, n_features):
                dve.wait_ge(aux_full, a + 1)
                n = len(span.stat_starts)
                dve.tensor_scalar(mean_sq[:, 0:n], aux_ps[a % 2][:, 0, 0:n], 1.0 / n_features, EPS,
                                  ALU.mult, ALU.add).then_inc(aux_out, 1)

            def stats_take(a, span, dst):
                dve.wait_ge(aux_full, a + 1)
                dve.tensor_copy(span.sb(dst[:, :]), span.ps(aux_ps[a % 2])).then_inc(aux_out, 1)
                dve.wait_ge(aux_out, a + 1)

            split_lo(0, KD)
            dve.wait_ge(params_in, 16)
            for d in range(KD):
                dve.wait_ge(h_in[d // 2], 16)
                residual_lo(0, d, ALL)
                if d:
                    dve.wait_ge(squared, d + 1)
                    so_far = first_squares[0] if d == 1 else square_sum
                    if d > 1:
                        dve.wait_ge(summed, d - 1)
                    dve.tensor_tensor(square_sum[:, :], so_far[:, :], first_squares[d][:, :], ALU.add
                                      ).then_inc(summed, 2 if d == KD - 1 else 1)
            split_lo(1, KD)
            def lambda_and_sinks():
                dve.wait_ge(consts_in, 64)
                for n in range(2):
                    step(dve.tensor_tensor(lam_prod[:, :], lambdas[:, 128 * n:128 * n + 64],
                                           lambdas[:, 128 * n + 64:128 * n + 128], ALU.mult))
                    ins = dve.tensor_reduce(lam[:, n:n + 1], lam_prod[:, :], AX.X, ALU.add)
                    if n == 0:
                        step(ins)
                ins.then_inc(lam_ready, 1)
                dve.wait_ge(lam_exp, 1)
                step(dve.tensor_tensor(lam[:, 4:5], lam[:, 3:4], lam[:, 2:3], ALU.subtract))
                step(dve.tensor_scalar(lam[:, 5:6], lam[:, 4:5], LAMBDA_INIT, None, ALU.subtract))
                step(dve.tensor_scalar(gain_sub[:, :], par[:, C_SUBLN:C_SUBLN + 1], 1.0 - LAMBDA_INIT, None,
                                       ALU.mult))
                step(dve.memset(swapped[:, :], 0.0))
                step(dve.tensor_scalar(neg_sink[:, :], sinks[:, :], -1.0, None, ALU.mult))

            def gate_up(st):
                u0, o0, f0, span, s = st["u0"], st["o0"], st["f0"], st["span"], st["stats"]
                cols = slice(span.first, T)
                if s:
                    stats_mean(s["a"], span, D)
                    stats_take(s["a"] + 1, span, rbc)

                def feature(f, i, ks):
                    pair = [tiles_ps[(o0 + c) % 2] for c in range(2)]
                    dve.wait_ge(tile_full, i * 2 + (o0 + 1))
                    dve.tensor_tensor(span.sb(g_buf[:, :]), span.ps(pair[0]), span.sb(rbc[:, :]), ALU.mult
                                      ).then_inc(tile_out, 1)
                    split_lo(u0 + 2, ks[0], i)
                    dve.wait_ge(tile_full, i * 2 + (o0 + 2))
                    dve.tensor_tensor(span.sb(u_buf[:, :]), span.ps(pair[1]), span.sb(rbc[:, :]), ALU.mult
                                      ).then_inc(tile_out, 1)
                    dve.wait_ge(silu_ready, i + (f0 + 1))
                    dve.wait_ge(tile_out, i * 2 + (o0 + 2))
                    dve.tensor_tensor(p_buf[:, cols], s_buf[:, cols], u_buf[:, cols], ALU.mult
                                      ).then_inc(gated, 1)
                    split_lo(u0 + 3, ks[1], i)
                    dve.wait_ge(act_hi_ready, i + (f0 + 1))
                    dve.tensor_tensor(act_lo[:, bass.ds(f, 1), cols].rearrange("p a n -> p (a n)"),
                                      p_buf[:, cols],
                                      act_hi[:, bass.ds(f, 1), cols].rearrange("p a n -> p (a n)"),
                                      ALU.subtract).then_inc(act_lo_ready, 1)

                with dve.Fori(0, FH - 1) as f:
                    feature(f, f, (KD, KD))
                feature(FH - 1, FH - 1, (FH, FH))

            def down(st):
                u0, o0, span = st["u0"], st["o0"], st["span"]

                def pair(i, ks):
                    for c in range(2):
                        d = i * 2 + c
                        row = span.sb(h[:, bass.ds(d, 1), :].rearrange("p a n -> p (a n)"))
                        ps = span.ps(tiles_ps[(o0 + c) % 2])
                        dve.wait_ge(tile_full, i * 2 + (o0 + c + 1))
                        if st["weights"] == "dn":
                            ins = dve.scalar_tensor_tensor(out=row, in0=ps, scalar=0.5, in1=row,
                                                           op0=ALU.mult, op1=ALU.add)
                        elif st["bias"]:
                            ins = dve.scalar_tensor_tensor(out=row, in0=ps, scalar=par[:, bass.ds(d + C_BOUT, 1)],
                                                           in1=row, op0=ALU.add, op1=ALU.add)
                        else:
                            ins = dve.tensor_tensor(row, ps, row, ALU.add)
                        ins.then_inc(tile_out, 1)
                        if st["last"]:
                            dve.wait_ge(tile_out, i * 2 + (o0 + c + 1))
                            residual_square(st["sq0"], d, span)
                        if ks:
                            split_lo(u0 + c + 2, ks[c], i)
                        if st["last"] and st["norm"] < NORMS - 1:
                            residual_lo(st["norm"], d, span)

                if st["act_lo"] is None:
                    dve.wait_ge(lo_ready, u0 + 2)
                with dve.Fori(0, KD // 2 - 1) as i:
                    pair(i, (st["k"], st["k"]))
                pair(KD // 2 - 1, unit_k[u0 + KD:u0 + KD + 2])

            def place_turned(t, part):
                dst = dest[t.dst][t.index]
                if t.dst in ("dk", "kr"):
                    dve.wait_ge(zeroed, ZEROED["late" if t.dst == "dk" and t.index > 1 else "ab"])
                if t.dst in ("dk", "kr"):
                    dve.tensor_tensor(dst[0][0:64, :], part[0:64, :], turned[0:64, :], ALU.add)
                    dve.tensor_tensor(dst[1][64:P, :], part[64:P, :], turned[64:P, :], ALU.add
                                      ).then_inc(rope_done, 1)
                else:
                    dve.tensor_tensor(dst[:, :], part[:, :], turned[:, :], ALU.add
                                      ).then_inc(rope_done, 1)

            def rotate_partial(t):
                dve.wait_ge(tile_out, t.o + 1)
                dve.tensor_tensor(turned[:, :], pre[:, :], cos_p, ALU.mult)
                dve.wait_ge(swap_in, 64 * t.swap)
                step(dve.tensor_tensor(swapped[:, :], swapped[:, :], sin_p, ALU.mult))
                place_turned(t, swapped)

            def auxiliary(jobs, pair=None):
                for what, a, of in jobs:
                    src = pair or aux_ps[a % 2]
                    if what == "columns":
                        stats_mean(a, ALL, 256)
                    elif what == "spread":
                        stats_take(a, ALL, rbc_q if of == stats_of_ab + 1 else rbc_kv)
                    elif what == "rotate":
                        dve.wait_ge(tile_out, of.o + 1)
                        cos, sin = (cos_m, sin_m) if of.kind == "rope_m" else (cos_p, sin_p)
                        step(dve.tensor_tensor(turned[:, :], pre[:, :], cos, ALU.mult))
                        dve.wait_ge(aux_full, a + 1)
                        dve.tensor_tensor(ALL.sb(pre[:, :]), ALL.ps(src), ALL.sb(sin), ALU.mult
                                          ).then_inc(aux_out, 1)
                        dve.wait_ge(aux_out, a + 1)
                        place_turned(of, pre)
                    else:
                        dst = dest[of.dst]
                        dve.wait_ge(zeroed, ZEROED["swa" if of.dst == "sv" else "ab"])
                        cols = slice(of.index * P, (of.index + 1) * P)
                        dve.wait_ge(aux_full, a + 1)
                        dve.tensor_copy(dst[0:META, 0, cols], src[0:META, 1, 0:P])
                        dve.tensor_copy(dst[:, 1:5, cols],
                                        src[:, 0, :].rearrange("p (j n) -> p j n", j=4)
                                        ).then_inc(aux_out, 1)

            def maxima(it):
                for c, (x, pair, _) in enumerate(it.sets):
                    slot = scores_ps[pair]
                    dve.wait_ge(scores_full, x + 1)
                    if it.kind == "swa":
                        lo = 0 if it.i > 1 else P
                        k = slice(2 * it.p, 2 * it.p + 2)
                        step(dve.tensor_reduce(row_max[:, it.g % 2, k], slot[:, :, lo:2 * P + META],
                                               AX.X, ALU.max))
                        dve.scalar_tensor_tensor(out=neg_max[:, it.g % 2, k], in0=row_max[:, it.g % 2, k],
                                                 scalar=-it.scale,
                                                 in1=neg_sink[:, 2 * it.hd:2 * it.hd + 2],
                                                 op0=ALU.mult, op1=ALU.min).then_inc(max_ready, 1)
                    else:
                        k = 2 * it.p + c
                        src, axis = ((slot[:, 0, 0:it.width], AX.X) if len(it.chunks) == 1 else
                                     (slot[:, :, 0:HALF_T], AX.XY))
                        step(dve.tensor_reduce(row_max[:, it.g % 2, k:k + 1], src, axis, ALU.max))
                        dve.tensor_scalar(neg_max[:, it.g % 2, k:k + 1], row_max[:, it.g % 2, k:k + 1],
                                          -it.scale, None, ALU.mult).then_inc(max_ready, 1)
                if it.kind == "swa" and it.last:
                    dve.wait_ge(max_ready, it.sets[0][0] + 1)
                    two = sinks[:, 2 * it.hd:2 * it.hd + 2].unsqueeze(1).to_broadcast([P, 4, 2])
                    dve.tensor_tensor(sink_s[:, :].rearrange("p (i v) -> p i v", v=2),
                                      neg_max[:, it.g % 2, :].rearrange("p (i v) -> p i v", v=2),
                                      two, ALU.add).then_inc(sink_sum, 1)

            def combine(it):
                k = 2 * it.p
                dve.wait_ge(exp_done, it.sets[1][0] + 1)
                step(dve.reciprocal(coef[:, 0:1], row_sum[:, it.g % 2, k + 1:k + 2]))
                step(dve.scalar_tensor_tensor(out=coef[:, 1:2], in0=row_sum[:, it.g % 2, k:k + 1],
                                              scalar=lam[:, 5:6], in1=coef[:, 0:1],
                                              op0=ALU.mult, op1=ALU.mult))
                if it.before[2].kind == "diff":
                    dve.wait_ge(pt_full, it.before[2].t_end)
                w = it.width
                dve.scalar_tensor_tensor(out=mix[:, it.m % 2, 0:w], in0=e_diff[it.m % 2][1][:, 0:w],
                                         scalar=coef[:, 1:2], in1=e_diff[it.m % 2][0][:, 0:w],
                                         op0=ALU.mult, op1=ALU.add).then_inc(mix_ready, 1)

            def normalise(it):
                sums = row_sum[:, it.g % 2, :]
                if it.kind == "swa":
                    dve.wait_ge(sink_exp, it.hd + 1)
                    step(dve.tensor_tensor(inv_sum[:, 0, :], sums, sink_e[:, :], ALU.add))
                    step(dve.reciprocal(inv_sum[:, 1, :], inv_sum[:, 0, :]))
                    n, d = 8, SD
                else:
                    n, d = 4, P
                    dve.wait_ge(exp_done, it.sets[-1][0] + 1)
                    step(dve.reciprocal(inv_sum[:, 1, 0:4], sums[:, 0:8:2]))
                o = o_nat[:, :].rearrange("p (f d) -> p f d", d=d)
                dve.wait_ge(pv_done, it.n + 1)
                dve.tensor_tensor(o, value_ps.rearrange("p (f d) -> p f d", d=d),
                                  inv_sum[:, 1, 0:n].unsqueeze(2).to_broadcast([P, n, d]), ALU.mult
                                  ).then_inc(o_taken, 1)

            def output_norm(it):
                dve.wait_ge(o_rstd_ready, it.g - 4)
                o = o_nat[:, :].rearrange("p (f d) -> p f d", d=P)
                dve.tensor_tensor(o, o, o_rstd[:, :].unsqueeze(2).to_broadcast([P, 4, P]), ALU.mult
                                  ).then_inc(o_ready, 1)

            def output_lo(it):
                dve.wait_ge(o_hi, it.g + 1)
                src = output_ps(it)
                if it.i == 0:
                    k0 = 0 if it.kind == "diff" else 4
                    hi, lo = (x[:, k0:k0 + 4, 0:META] for x in (act_hi, act_lo))
                    src = src.rearrange("p (f q) -> p f q", q=P)[:, :, 0:META]
                else:
                    hi, lo = (x[:, it.hd + (4 if it.kind == "mla" else 0), META:T] for x in (act_hi, act_lo))
                if it.kind == "diff":
                    dve.scalar_tensor_tensor(out=lo, in0=src, scalar=gain_sub[:, 0:1], in1=hi,
                                             op0=ALU.mult, op1=ALU.subtract).then_inc(o_lo, 1)
                else:
                    dve.tensor_tensor(lo, src, hi, ALU.subtract).then_inc(o_lo, 1)

            def beat(steps):
                for name, does in (("output", output_lo), ("scores", maxima), ("combine", combine),
                                   ("output_norm", output_norm), ("late_output", output_lo),
                                   ("normalise", normalise)):
                    if name in steps:
                        does(steps[name])

            def projections(st):
                turned_last, to_rotate = 0, None
                s, beats = st["stats"], iter(st["beats"])
                stats_mean(s["a"], ALL, D)
                stats_take(s["a"] + 1, ALL, rbc)
                for at, its_tiles in enumerate(st["units"]):
                    u = st["u0"] + at
                    for t in its_tiles:
                        for in_block in range(len((t.beats or [()])[0]) or 1):
                            if (t.beats or [()])[0]:
                                beat(next(beats))
                            if in_block == 0 and to_rotate:
                                rotate_partial(to_rotate)
                                to_rotate = None
                        pair = tiles_ps[t.slot()]
                        dve.wait_ge(tile_full, t.o + 1)
                        if t.kind.startswith("rope") or t.kind == "value":
                            dst = pre
                        else:
                            dst = dest[t.dst][t.index]
                        r = rbcs[t.src]
                        if dst is pre and turned_last:
                            dve.wait_ge(rope_done, turned_last)
                        dve.tensor_tensor(ALL.sb(dst[:, :]), ALL.ps(pair), ALL.sb(r[:, :]), ALU.mult
                                          ).then_inc(tile_out, 1)
                        if t.bias is not None:
                            col = C_BQKV + t.bias
                            dve.wait_ge(tile_out, t.o + 1)
                            dve.tensor_scalar(pre[:, :], pre[:, :], par[:, col:col + 1], None, ALU.add
                                              ).then_inc(biased, 1)
                            dve.wait_ge(biased, t.biased)
                        if t.beats and t.beats[1][0]:
                            beat(next(beats))
                        if t is its_tiles[-1] and at < st["pool_from"]:
                            split_lo(u + 2, unit_k[u + 2])
                        if t.kind == "low_rank":
                            col = (C_QN, C_QN + 1, C_KVN, C_KVN + 1)[t.index]
                            dve.wait_ge(low_hi_ready, t.low)
                            dve.scalar_tensor_tensor(out=act_lo[:, t.index, :], in0=craw[:, t.index, :],
                                                     scalar=par[:, col:col + 1], in1=act_hi[:, t.index, :],
                                                     op0=ALU.mult, op1=ALU.subtract).then_inc(low_lo_ready, 1)
                        if not (t.beats and t.kind == "value"):
                            auxiliary(t.jobs, None if t.beats is None else aux_ps[1] if t.aux_ahead else tiles_ps[0])
                        if t.kind == "rope_s":
                            to_rotate = t
                        if t.kind.startswith("rope"):
                            turned_last = t.rope
                        if t.beats and t.beats[1][1]:
                            beat(next(beats))
                for steps in beats:
                    beat(steps)

            dve.wait_ge(tables_in, 16)
            for st in stages:
                if st["kind"] == "gu":
                    gate_up(st)
                elif st["kind"] == "dn":
                    if st is stages[1]:
                        lambda_and_sinks()
                    down(st)
                elif st["kind"] == "proj":
                    projections(st)
                else:
                    s = st["stats"]
                    stats_mean(s["a"], OUT, D)
                    dve.wait_ge(final_gained, KD + 1)
                    for d in range(POOL_FINAL, KD):
                        dve.tensor_tensor(final[:, d, META:T], final[:, d, META:T], rbc[:, META:T], ALU.mult
                                          ).then_inc(final_ready, 1)

        @block.gpsimd
        def _(pool):
            cleared, zero_steps = [0], [0]

            def sum_squares(sq0, n, span, taken):
                if taken:
                    pool.wait_ge(aux_full, taken)
                cleared[0] += 1
                pool.memset(square_sum[:, :], 0.0).then_inc(sum_clear, 1)
                pool.wait_ge(sum_clear, cleared[0])
                cols = slice(span.first, T)
                with pool.Fori(0, n) as d:
                    pool.wait_ge(squared, d + (sq0 + 1))
                    pool.tensor_tensor(square_sum[:, cols], square_sum[:, cols], square[:, cols], ALU.add
                                       ).then_inc(summed, 1)
                    pool.wait_ge(summed, d + (sq0 + 1))

            def rstd_of(a, r, n):
                pool.wait_ge(aux_out, a + 1)
                pool.tensor_tensor(rstd[:, 0:n], mean_sq[:, 0:n], minus_half.to_broadcast([P, n]), ALU.pow
                                   ).then_inc(rstd_ready, 1)

            def zeros(*rows):
                for row in rows:
                    zero_steps[0] += 1
                    pool.memset(row, 0.0).then_inc(zeroed, 1)
                    pool.wait_ge(zeroed, zero_steps[0])

            def halves(*pairs):
                return [row for a, b in pairs for row in (a[64:P, :], b[0:64, :])]

            def split_lo(u, k):
                pool.wait_ge(lo_ready, u)
                pool.wait_ge(hi_ready, u + 1)
                pool.tensor_tensor(w_lo[:, u % 2, 0:k * P], raw[:, u % 2, 0:k * P],
                                   w_hi[:, u % 2, 0:k * P], ALU.subtract).then_inc(lo_ready, 1)
                pool.wait_ge(lo_ready, u + 1)

            def beat(steps):
                if "scores" in steps and steps["scores"].kind == "diff" and steps["scores"].n == MLA_ITEMS:
                    pool.wait_ge(scores_full, steps["scores"].sets[0][0])
                    zeros(*halves(*dk[2:4]))
                if "normalise" in steps and steps["normalise"].kind == "diff":
                    it = steps["normalise"]
                    pool.wait_ge(o_mean, it.g - 4)
                    pool.tensor_tensor(o_rstd[:, :], o_mse[:, :], minus_half.to_broadcast([P, 4]), ALU.pow
                                       ).then_inc(o_rstd_ready, 1)
                    pool.wait_ge(o_rstd_ready, it.g - 4)

            def projections(st, taken):
                beats = iter(st["beats"])
                for at, its_tiles in enumerate(st["units"]):
                    u = st["u0"] + at
                    for t in its_tiles:
                        if t.kind == "low_rank" and t.index % 2 == 1:
                            sum_squares(t.sq - 2, 2, ALL, taken)
                            a = t.jobs[-1][1]
                            rstd_of(a, stats_of_ab + 1 + t.index // 2, 6)
                            taken = a + 1
                        if t.beats:
                            for _ in t.beats[0]:
                                beat(next(beats))
                            if t.beats[1][0]:
                                beat(next(beats))
                            if st["which"] == "swa":
                                split_lo(u + 2, unit_k[u + 2])
                            if t.beats[1][1]:
                                beat(next(beats))
                            if st["which"] == "ab":
                                split_lo(u + 2, unit_k[u + 2])
                        elif t is its_tiles[-1] and at >= st["pool_from"]:
                            split_lo(u + 2, unit_k[u + 2])
                for steps in beats:
                    beat(steps)
                return taken

            pool.wait_ge(consts_in, 64)
            taken = 0
            for st in stages:
                s = st.get("stats")
                if s:
                    rstd_of(s["a"], s["r"], len(s["span"].stat_starts))
                    taken = s["a"] + 1
                if st["kind"] == "proj":
                    pool.wait_ge(act_lo_ready, st["act_lo"])
                    if st["which"] == "ab":
                        zeros(dv[:, 0, :], mv[:, 0, :], *halves(kr[0], *dk[0:2]))
                    else:
                        zeros(sv[:, 0, :], e_win[:, :, :, 2 * P + META:3 * P],
                              sk_win[64:P, 0, :, :], sk_win[0:64, 1, :, :])
                if st["kind"] == "dn" and st["last"]:
                    if not st["act_lo"]:
                        pool.wait_ge(o_lo, st["o_lo"])
                    sum_squares(st["sq0"], KD, st["span"], taken)
                elif st["kind"] == "proj":
                    taken = projections(st, taken)
                elif st["kind"] == "final":
                    pool.wait_ge(final_gained, KD + 1)
                    for d in range(POOL_FINAL):
                        pool.tensor_tensor(final[:, d, META:T], final[:, d, META:T], rbc[:, META:T], ALU.mult
                                           ).then_inc(final_pool, 1)
                        pool.wait_ge(final_pool, d + 1)
    return nc


def shape_constants():
    f = np.float32
    rot = np.zeros((2, P, P), f)
    for n, half in ((0, 8), (1, 32)):
        for start in (0, 64):
            for j in range(half):
                rot[n, start + half + j, start + j] = 1.0
                rot[n, start + j, start + half + j] = 1.0
    con = np.concatenate([np.eye(P, dtype=f), rot[0], rot[1], np.ones((P, 1), f),
                          np.full((P, 1), -0.5, f)], axis=1)
    tab = np.zeros((P, 4, T), f)
    pos = np.arange(T, dtype=f)
    for n, width in ((0, 16), (1, 64)):
        inv = np.power(f(500000.0), -np.arange(0, width, 2, dtype=f) / f(width)).astype(f)
        ang = pos[:, None] * inv[None, :]
        cos, sin = np.cos(ang).astype(f), np.sin(ang).astype(f)
        for p in range(P):
            d = p % 64
            if d < width:
                tab[p, 2 * n] = cos[:, d % (width // 2)]
                sign = -1 if d < width // 2 else 1
                tab[p, 2 * n + 1] = sign * sin[:, d % (width // 2)]
            else:
                tab[p, 2 * n] = 1.0
    q, k = np.arange(P)[:, None], np.arange(P)[None, :]
    masks = np.concatenate([np.eye(P), np.where(k > q, 0.0, MASKED), np.where(k <= q, 0.0, MASKED)],
                           axis=1).astype(mybir.dt.np(BF16))
    return con, tab, masks


def kernel(**inputs):
    from concourse import bacc
    from concourse.bass_utils import run_bass_kernel_spmd

    x = {k: np.asarray(v) for k, v in inputs.items()}

    def units(w):
        kk, m = w.shape
        return np.ascontiguousarray(w.reshape(kk // P, P, m // P, P).transpose(2, 1, 0, 3)
                                    ).reshape(m // P, P, kk)

    def cols(v):
        return v.reshape(-1, P).T

    gu, dn = [], []
    for layer, name in ((0, "ffn1"), (0, "ffn2"), (1, "ffn1"), (1, "ffn2")):
        pair = np.stack([units(x[name + "_w_gate"][layer]), units(x[name + "_w_up"][layer])], axis=1)
        gu.append(pair.reshape(2 * pair.shape[0], P, D))
        down = x[name + "_w_down"][layer]
        dn += [units(down[half * FH * P:(half + 1) * FH * P]) for half in range(2)]
    w = x["ab_w_in"][0]
    cut = np.split(w, [512, 1024, 1536, 1792, 2048], axis=1)
    by_head = [part[:, P * i:P * (i + 1)] for i in range(4) for part in cut[0:3]]
    w_ab = np.concatenate([cut[3], cut[4], cut[5], cut[5]] + by_head, axis=1)
    uq = x["mla_w_uq"][0].reshape(256, MH, 192)
    uq = np.concatenate([part for i in (0, 2) for part in
                         (uq[:, i, :128], uq[:, i, 128:], uq[:, i + 1, 128:], uq[:, i + 1, :128])], axis=1)
    ukv = x["mla_w_ukv"][0]

    def grouped(w, n):
        t = units(w)
        return np.ascontiguousarray(t.reshape(len(t) // n, n, P, 256).transpose(0, 2, 1, 3)
                                    ).reshape(len(t) // n, P, n * 256)

    def by_pair(v):
        lead = v.shape[:-1]
        q = v[..., :1024].reshape(*lead, 2, 8, 64)
        q = np.swapaxes(q, -3, -2).reshape(*lead, 1024)
        return np.concatenate([v[..., 1024:], q], axis=-1)

    swo = np.swapaxes(x["swa_w_out"][0].reshape(2, 8, 64, D), 0, 1).reshape(D, D)
    norms = [x["ffn1_norm"][0], x["mix_norm"][0], x["ffn2_norm"][0], x["ffn1_norm"][1],
             x["mix_norm"][1], x["ffn2_norm"][1], x["final_norm"]]
    params = np.concatenate([cols(v) for v in norms] +
                            [cols(x["mla_q_norm"][0]), cols(x["mla_kv_norm"][0]), cols(x["diff_subln"][0]),
                             cols(by_pair(x["swa_b_qkv"][0])), cols(x["swa_b_out"][0])], axis=1)
    row = np.concatenate([x["diff_lambda_q1"][0], x["diff_lambda_k1"][0], x["diff_lambda_q2"][0],
                          x["diff_lambda_k2"][0], x["swa_sinks"][0].reshape(2, 8).T.reshape(-1)])
    tokens = np.concatenate([x["meta_tokens"], x["x"][0]], axis=0)
    con, tab, masks = shape_constants()
    arrays = {
        "x_t": tokens.T.reshape(KD, P, T).transpose(1, 0, 2),
        "w_gu": np.concatenate(gu), "w_dn": np.concatenate(dn), "w_ab": units(w_ab),
        "w_uq": grouped(uq, 3), "w_ukv": grouped(ukv, 4), "w_abo": units(x["ab_w_out"][0]),
        "w_swa": units(by_pair(x["swa_w_qkv"][0])), "w_swo": units(swo),
        "params": params, "row": row, "consts": con, "tables": tab, "masks": masks,
    }
    nc = bacc.Bacc("TRN2", target_bir_lowering=False, num_devices=1)
    args = {}
    for name, a in arrays.items():
        arrays[name] = np.ascontiguousarray(a)
        args[name] = nc.dram_tensor(name, a.shape, mybir.dt.from_np(a.dtype), kind="ExternalInput").ap()
    args["out"] = nc.dram_tensor("out", (P, KD, SEQ), F32, kind="ExternalOutput").ap()
    build(nc, **args)
    got = run_bass_kernel_spmd(nc, [arrays], core_ids=[0]).results[0]["out"]
    return np.ascontiguousarray(got.transpose(2, 1, 0).reshape(1, SEQ, D))
```
